# Optimizing a Trainium2 kernel written in Bass

```python
import jax, jax.numpy as jnp
from jax import lax
import numpy as np

D_MODEL = 1024
BATCH = 1
SEQ = 1024
DEPTH = 1

HEAD_DIM = 64
N_HEADS = D_MODEL // HEAD_DIM
N_HEADS_NSA = N_HEADS // 2
N_KV_NSA = 2
N_HEADS_SWA = N_HEADS - N_HEADS_NSA
N_KV_SWA = 2
MIX_WIDTH = N_HEADS * HEAD_DIM
CMP_BLOCK = 32
CMP_STRIDE = 16
CMP_HIDDEN = 4 * HEAD_DIM
SEL_BLOCK = 64
SEL_TOPN = 8
NSA_WINDOW = 512
SWA_WINDOW = 128
Q_BLOCK = 128
D_FF = 4 * D_MODEL
NORM_EPS = 1e-6
N_NSA_BRANCHES = 3

kernel_name = "hymba_nsa_swa_sink_alibi_sandwich_block"

def rms_norm(x, g):
    xf = x.astype(jnp.float32)
    y = xf * lax.rsqrt(jnp.mean(xf * xf, axis=-1, keepdims=True) + NORM_EPS)
    return (y * g.astype(jnp.float32)).astype(x.dtype)

def alibi_slopes():
    s = 2.0 ** (-8.0 * (np.arange(N_HEADS) + 1) / N_HEADS)
    s = jnp.asarray(s, dtype=jnp.float32)
    nsa = s[0::2].reshape(N_KV_NSA, N_HEADS_NSA // N_KV_NSA)
    swa = s[1::2].reshape(N_KV_SWA, N_HEADS_SWA // N_KV_SWA)
    return nsa, swa

def masked_softmax(s, mask, sink=None):
    s = jnp.where(mask, s, -jnp.inf)
    m = jnp.max(s, axis=-1, keepdims=True)
    if sink is not None:
        m = jnp.maximum(m, sink)
    m = jnp.where(jnp.isfinite(m), m, 0.0)
    e = jnp.exp(s - m)
    denom = jnp.sum(e, axis=-1, keepdims=True)
    if sink is not None:
        denom = denom + jnp.exp(sink - m)
    return e / jnp.where(denom > 0, denom, 1.0)

def compress_blocks(kv, pe, w1, w2):
    B, G, T, D = kv.shape
    n_cmp = (T - CMP_BLOCK) // CMP_STRIDE + 1
    idx = np.arange(n_cmp)[:, None] * CMP_STRIDE + np.arange(CMP_BLOCK)[None, :]
    blocks = kv[:, :, idx, :] + pe
    flat = blocks.reshape(B, G, n_cmp, CMP_BLOCK * D)
    return jax.nn.gelu(flat @ w1) @ w2

def banded_attention(q, k, v, slopes, window, sinks=None):
    B, G, R, T, D = q.shape
    scale = D ** -0.5
    n_blk = T // Q_BLOCK
    L = window + Q_BLOCK
    kp = jnp.pad(k, ((0, 0), (0, 0), (window, 0), (0, 0)))
    vp = jnp.pad(v, ((0, 0), (0, 0), (window, 0), (0, 0)))
    sink = None if sinks is None else sinks.astype(jnp.float32)[None, :, :, None, None]

    def body(c):
        start = c * Q_BLOCK
        q_b = lax.dynamic_slice_in_dim(q, start, Q_BLOCK, axis=3)
        ks = lax.dynamic_slice_in_dim(kp, start, L, axis=2)
        vs = lax.dynamic_slice_in_dim(vp, start, L, axis=2)
        pos_q = start + jnp.arange(Q_BLOCK)
        pos_k = start - window + jnp.arange(L)
        dist = pos_q[:, None] - pos_k[None, :]
        mask = (pos_k >= 0)[None, :] & (dist >= 0) & (dist < window)
        s = jnp.einsum('bgrqd,bgkd->bgrqk', q_b, ks).astype(jnp.float32) * scale
        s = s - slopes[None, :, :, None, None] * dist.astype(jnp.float32)
        p = masked_softmax(s, mask, sink)
        return jnp.einsum('bgrqk,bgkd->bgrqd', p.astype(vs.dtype), vs)

    out = lax.map(body, jnp.arange(n_blk))
    return out.transpose(1, 2, 3, 0, 4, 5).reshape(B, G, R, T, D)

def selected_attention(q, k, v, tok, slopes):
    B, G, R, T, D = q.shape
    scale = D ** -0.5
    n_blk = T // Q_BLOCK
    qc = q.reshape(B, G, R, n_blk, Q_BLOCK, D).transpose(3, 0, 1, 2, 4, 5)
    tc = tok.reshape(B, G, n_blk, Q_BLOCK, -1).transpose(2, 0, 1, 3, 4)
    pc = jnp.arange(T).reshape(n_blk, Q_BLOCK)
    gather = jax.vmap(jax.vmap(lambda kk, ii: kk[ii]))

    def body(args):
        q_b, tok_b, pos_b = args
        ks = gather(k, tok_b)
        vs = gather(v, tok_b)
        dist = pos_b[None, None, :, None] - tok_b
        s = jnp.einsum('bgrqd,bgqkd->bgrqk', q_b, ks).astype(jnp.float32) * scale
        s = s - slopes[None, :, :, None, None] * dist[:, :, None].astype(jnp.float32)
        p = masked_softmax(s, (dist >= 0)[:, :, None])
        return jnp.einsum('bgrqk,bgqkd->bgrqd', p.astype(vs.dtype), vs)

    out = lax.map(body, (qc, tc, pc))
    return out.transpose(1, 2, 3, 0, 4, 5).reshape(B, G, R, T, D)

def nsa_attention(q, k_cmp, v_cmp, k_slc, v_slc, k_win, v_win, gates, slopes,
                  pe_k, w1_k, w2_k, pe_v, w1_v, w2_v):
    B, G, R, T, D = q.shape
    scale = D ** -0.5
    pos = jnp.arange(T)
    kc = compress_blocks(k_cmp, pe_k, w1_k, w2_k)
    vc = compress_blocks(v_cmp, pe_v, w1_v, w2_v)
    n_cmp = kc.shape[2]
    cmp_start = jnp.arange(n_cmp) * CMP_STRIDE
    cmp_end = cmp_start + CMP_BLOCK - 1
    dist_c = pos[:, None] - cmp_end[None, :]
    s = jnp.einsum('bgrtd,bgnd->bgrtn', q, kc).astype(jnp.float32) * scale
    s = s - slopes[None, :, :, None, None] * dist_c.astype(jnp.float32)
    p_cmp = masked_softmax(s, dist_c >= 0)
    o_cmp = jnp.einsum('bgrtn,bgnd->bgrtd', p_cmp.astype(vc.dtype), vc)
    n_sel = T // SEL_BLOCK
    sel_start = jnp.arange(n_sel) * SEL_BLOCK
    overlap = ((cmp_start[:, None] < sel_start[None, :] + SEL_BLOCK) &
               (cmp_start[:, None] + CMP_BLOCK > sel_start[None, :])).astype(jnp.float32)
    imp = jnp.einsum('bgrtn,nj->bgtj', p_cmp, overlap)
    blk_t = pos // SEL_BLOCK
    j = jnp.arange(n_sel)
    valid = j[None, :] <= blk_t[:, None]
    forced = (j[None, :] == 0) | (j[None, :] == blk_t[:, None]) | (j[None, :] == blk_t[:, None] - 1)
    score = jnp.where(valid, imp, -jnp.inf)
    score = jnp.where(forced & valid, jnp.inf, score)
    top_n = min(SEL_TOPN, n_sel)
    _, sel_idx = lax.top_k(score, top_n)
    tok = (sel_idx[..., None] * SEL_BLOCK + jnp.arange(SEL_BLOCK)).reshape(B, G, T, top_n * SEL_BLOCK)
    o_slc = selected_attention(q, k_slc, v_slc, tok, slopes)
    o_win = banded_attention(q, k_win, v_win, slopes, NSA_WINDOW)
    g = gates.astype(q.dtype)
    return g[..., 0:1] * o_cmp + g[..., 1:2] * o_slc + g[..., 2:3] * o_win

def setup_inputs(seed: int = 0) -> dict:
    key = jax.random.key(seed)
    ks = jax.random.split(key, 16)
    n_cols = (N_HEADS_NSA * HEAD_DIM + 6 * N_KV_NSA * HEAD_DIM + N_HEADS_NSA * N_NSA_BRANCHES
              + N_HEADS_SWA * HEAD_DIM + 2 * N_KV_SWA * HEAD_DIM)
    f = jnp.float32
    nrm = lambda k, shape, s: jax.random.normal(k, shape, f) * s
    gain = lambda k: 1.0 + 0.05 * jax.random.normal(k, (DEPTH, D_MODEL), f)
    flat = CMP_BLOCK * HEAD_DIM
    return {
        "x": jax.random.normal(ks[0], (BATCH, SEQ, D_MODEL), f),
        "norm_mix_pre": gain(ks[1]),
        "w_in": nrm(ks[2], (DEPTH, D_MODEL, n_cols), D_MODEL ** -0.5),
        "cmp_pe_k": nrm(ks[3], (DEPTH, CMP_BLOCK, HEAD_DIM), 0.02),
        "cmp_w1_k": nrm(ks[4], (DEPTH, flat, CMP_HIDDEN), flat ** -0.5),
        "cmp_w2_k": nrm(ks[5], (DEPTH, CMP_HIDDEN, HEAD_DIM), CMP_HIDDEN ** -0.5),
        "cmp_pe_v": nrm(ks[6], (DEPTH, CMP_BLOCK, HEAD_DIM), 0.02),
        "cmp_w1_v": nrm(ks[7], (DEPTH, flat, CMP_HIDDEN), flat ** -0.5),
        "cmp_w2_v": nrm(ks[8], (DEPTH, CMP_HIDDEN, HEAD_DIM), CMP_HIDDEN ** -0.5),
        "sinks": nrm(ks[9], (DEPTH, N_KV_SWA, N_HEADS_SWA // N_KV_SWA), 0.5),
        "w_out": nrm(ks[10], (DEPTH, MIX_WIDTH, D_MODEL), MIX_WIDTH ** -0.5),
        "norm_mix_post": gain(ks[11]),
        "norm_mlp_pre": gain(ks[12]),
        "w_up": nrm(ks[13], (DEPTH, D_MODEL, D_FF), D_MODEL ** -0.5),
        "w_down": nrm(ks[14], (DEPTH, D_FF, D_MODEL), D_FF ** -0.5),
        "norm_mlp_post": gain(ks[15]),
    }

def reference(x, norm_mix_pre, w_in, cmp_pe_k, cmp_w1_k, cmp_w2_k, cmp_pe_v, cmp_w1_v, cmp_w2_v,
              sinks, w_out, norm_mix_post, norm_mlp_pre, w_up, w_down, norm_mlp_post):
    B, T, _ = x.shape
    D = HEAD_DIM
    Rn = N_HEADS_NSA // N_KV_NSA
    Rs = N_HEADS_SWA // N_KV_SWA
    slopes_nsa, slopes_swa = alibi_slopes()
    sizes = [N_HEADS_NSA * D] + [N_KV_NSA * D] * 6 + [N_HEADS_NSA * N_NSA_BRANCHES,
             N_HEADS_SWA * D, N_KV_SWA * D, N_KV_SWA * D]
    split_at = list(np.cumsum(sizes)[:-1])

    def to_q(t, G, R):
        return t.reshape(B, T, G, R, D).transpose(0, 2, 3, 1, 4)

    def to_kv(t, G):
        return t.reshape(B, T, G, D).transpose(0, 2, 1, 3)

    h = x
    for i in range(DEPTH):
        a = rms_norm(h, norm_mix_pre[i])
        proj = a @ w_in[i]
        (q_n, kc_n, vc_n, ks_n, vs_n, kw_n, vw_n, g_n, q_s, k_s, v_s) = jnp.split(proj, split_at, axis=-1)
        gates = jax.nn.sigmoid(g_n.astype(jnp.float32)).reshape(B, T, N_KV_NSA, Rn, N_NSA_BRANCHES)
        gates = gates.transpose(0, 2, 3, 1, 4)
        o_nsa = nsa_attention(to_q(q_n, N_KV_NSA, Rn), to_kv(kc_n, N_KV_NSA), to_kv(vc_n, N_KV_NSA),
                              to_kv(ks_n, N_KV_NSA), to_kv(vs_n, N_KV_NSA),
                              to_kv(kw_n, N_KV_NSA), to_kv(vw_n, N_KV_NSA), gates, slopes_nsa,
                              cmp_pe_k[i], cmp_w1_k[i], cmp_w2_k[i], cmp_pe_v[i], cmp_w1_v[i], cmp_w2_v[i])
        o_swa = banded_attention(to_q(q_s, N_KV_SWA, Rs), to_kv(k_s, N_KV_SWA), to_kv(v_s, N_KV_SWA),
                                 slopes_swa, SWA_WINDOW, sinks[i])
        o_nsa = o_nsa.transpose(0, 3, 1, 2, 4).reshape(B, T, N_HEADS_NSA * D)
        o_swa = o_swa.transpose(0, 3, 1, 2, 4).reshape(B, T, N_HEADS_SWA * D)
        mix = jnp.concatenate([o_nsa, o_swa], axis=-1) @ w_out[i]
        h = h + rms_norm(mix, norm_mix_post[i])
        m = rms_norm(h, norm_mlp_pre[i])
        u = jnp.square(jax.nn.relu(m @ w_up[i]))
        h = h + rms_norm(u @ w_down[i], norm_mlp_post[i])
    return h


_drawn_inputs = setup_inputs


def setup_inputs(seed=0):
    import zlib

    import numpy as np

    out = dict(_drawn_inputs(seed))
    spreads = {}
    factors = {'cmp_pe_k': 47.694, 'cmp_pe_v': 6.3}
    for name, (base, spread) in spreads.items():
        noise = np.random.default_rng([zlib.crc32(name.encode()), seed]).standard_normal(out[name].shape)
        drawn = base * np.exp(spread * noise) if base else spread * noise
        out[name] = __import__('jax').numpy.asarray(drawn.astype(out[name].dtype))
    for name, factor in factors.items():
        out[name] = (out[name] * factor).astype(out[name].dtype)
    return out
```

```python
from contextlib import ExitStack

import numpy as np

import concourse.bass as bass
from concourse import mybir

F32 = mybir.dt.float32
F32R = mybir.dt.float32r
ALU = mybir.AluOpType
ACT = mybir.ActivationFunctionType
AX = mybir.AxisListType

P = 128
D_MODEL = 1024
SEQ = 1024
HALF = 512
KD = D_MODEL // P
NT = SEQ // P
HD = 64
GROUPS = 2
HPG = 4
N_CMP = 63
CMP_PAD = 64
N_SEL = 16
SEL_TOPN = 8
D_FF = 4096
QUARTERS = 4
FQ = D_FF // P // QUARTERS
EPS = 1e-6
NEG = -1e30
FORCED = 1e30
TAKEN = 2e30
NO_KEY = 1e25

KS_SWA, VT_SWA, KC, VC_, VT_SLC, VT_WIN, GATES, K_SLC, K_WIN = range(9)
N_KV_CHUNKS = 9
N_Q_CHUNKS = 8
N_IN = N_KV_CHUNKS + N_Q_CHUNKS
SLC, WIN, SWA = range(3)
U_OUT = 2 * N_IN
U_MLP = U_OUT + 2 * KD
N_MLP = QUARTERS * 2 * FQ
N_UNITS = U_MLP + N_MLP

C_IDENT, C_ONES = 0, P
C_TD = 2 * P
C_TW = C_TD + SEQ
C_TS = C_TW + 640
C_TC = C_TS + 256
C_FORCE = C_TC + NT * CMP_PAD
C_QS = C_FORCE + 4 * N_SEL
C_END = C_QS + N_Q_CHUNKS


def slopes():
    s = (2.0 ** (-8.0 * (np.arange(16) + 1) / 16)).astype(np.float32)
    return np.concatenate([s[0::2], s[1::2]])


def constants():
    p = np.arange(P)[:, None]
    c = np.zeros((P, C_END), np.float32)
    c[:, C_IDENT:C_IDENT + P] = np.eye(P)
    c[:, C_ONES:C_ONES + P] = 1.0

    def table(at, width, before, window):
        dist = p - (np.arange(width)[None, :] - before)
        c[:, at:at + width] = np.where((dist >= 0) & (dist < window), -dist, NEG)

    table(C_TD, SEQ, SEQ - P, SEQ)
    table(C_TW, 640, 512, 512)
    table(C_TS, 256, 128, 128)
    for i in range(NT):
        n = np.arange(CMP_PAD)[None, :]
        dist = P * i + p - (16 * n + 31)
        c[:, C_TC + i * CMP_PAD:C_TC + (i + 1) * CMP_PAD] = np.where((dist >= 0) & (n < N_CMP), -dist, NEG)
    for i in range(4, NT):
        own = 2 * i + p // 64
        j = np.arange(N_SEL)[None, :]
        forced = (j == 0) | (j == own) | (j == own - 1)
        c[:, C_FORCE + (i - 4) * N_SEL:C_FORCE + (i - 3) * N_SEL] = np.where(j > own, NEG, np.where(forced, FORCED, 0.0))
    s = slopes()
    for q in range(N_Q_CHUNKS):
        c[:HD, C_QS + q] = 0.125 / s[2 * q]
        c[HD:, C_QS + q] = 0.125 / s[2 * q + 1]
    return c


def hybrid_layer(nc, xT, w_in, w_out, w_mlp, gains, w1, w2, pe_in, sinks, consts, h_dram, out):
    SL = [float(s) for s in slopes()]
    ctx = ExitStack()
    with ctx:
        small_at = 1152
        ring_at = small_at + 4096
        qa_at = ring_at + 24576
        kv_at = qa_at + 65536
        rest_at = kv_at + 73728

        def sb(name, shape, dt, at):
            return nc.alloc_sbuf_tensor_at(name, shape, dt, offset=at)

        ident = sb("ident", [P, P], F32, small_at)
        ones = sb("ones", [P, P], F32, small_at + 512)
        gain = sb("gain", [P, 4, KD], F32, small_at + 1024)
        gate = sb("gate", [P, NT, 24], F32, small_at + 1152)
        kc_hi = sb("kc_hi", [P, GROUPS, CMP_PAD], F32R, small_at + 1920)
        kc_lo = sb("kc_lo", [P, GROUPS, CMP_PAD], F32R, small_at + 2432)
        vc = sb("vc", [CMP_PAD, GROUPS, HD], F32, small_at + 2944)
        qscale = sb("qscale", [P, N_Q_CHUNKS], F32, small_at + 3456)
        sink = sb("sink", [P, 8], F32, small_at + 3488)
        nsink = sb("nsink", [P, 8], F32, small_at + 3520)
        eps = sb("eps", [P, 1], F32, small_at + 3552)
        nmax = sb("nmax", [P, 3, HPG], F32, small_at + 3584)
        den = sb("den", [P, 3, HPG], F32, small_at + 3648)
        esink = sb("esink", [P, 3, HPG], F32, small_at + 3712)
        rgate = sb("rgate", [P, 3, HPG], F32, small_at + 3776)

        w_raw = [sb(f"w_raw{i}", [P, KD, P], F32, ring_at + 4096 * i) for i in range(2)]
        w_hi = [sb(f"w_hi{i}", [P, KD, P], F32R, ring_at + 8192 + 4096 * i) for i in range(2)]
        w_lo = [sb(f"w_lo{i}", [P, KD, P], F32R, ring_at + 16384 + 4096 * i) for i in range(2)]
        qa = sb("qa", [P, 16, SEQ], F32R, qa_at)
        k_hi = sb("k_hi", [P, 3, GROUPS, SEQ], F32R, kv_at)
        k_lo = sb("k_lo", [P, 3, GROUPS, SEQ], F32R, kv_at + 24576)
        v_hi = sb("v_hi", [P, 3, NT, P], F32R, kv_at + 49152)
        v_lo = sb("v_lo", [P, 3, NT, P], F32R, kv_at + 61440)
        x_hi = sb("x_hi", [P, KD, HALF], F32R, rest_at)
        x_lo = sb("x_lo", [P, KD, HALF], F32R, rest_at + 16384)
        x_raw = sb("x_raw", [P, 2, HALF], F32, rest_at + 32768)
        z = sb("z", [P, HALF], F32, rest_at + 36864)
        z_hi = sb("z_hi", [P, HALF], F32R, rest_at + 38912)
        sq = [sb(f"sq{i}", [P, HALF], F32, rest_at + 36864 + 2048 * i) for i in range(2)]
        zv = sb("zv", [P, 4, HALF], F32, rest_at + 40960)
        zkv = sb("zkv", [P, 2, 8, GROUPS, 64], F32, rest_at + 49152)
        rstd = sb("rstd", [P, HALF], F32, rest_at + 57344)
        w1_sb = [sb(f"w1_sb{i}", [P, 16, 256], F32, rest_at + 16384 * i) for i in range(2)]
        blk = [sb(f"blk{i}", [P, 16, 2 * N_CMP], F32, rest_at + 32768 + 8192 * i) for i in range(2)]
        hid = [sb(f"hid{i}", [P, 2, 2 * N_CMP], F32, ring_at + 8192 + 1024 * i) for i in range(2)]
        w2_sb = sb("w2_sb", [P, 2, 2, P], F32, ring_at + 10240)
        pe_sb = sb("pe_sb", [P, 2, 16], F32, ring_at + 12288)
        wmask = sb("wmask", [P, GROUPS, SEQ], F32, ring_at)
        pt_hi = sb("pt_hi", [P, 2, HALF], F32R, ring_at + 8192)
        pt_lo = sb("pt_lo", [P, 2, HALF], F32R, ring_at + 12288)
        t_d = sb("t_d", [P, SEQ], F32, ring_at + 16384)
        t_w = sb("t_w", [P, 640], F32, ring_at + 20480)
        t_s = sb("t_s", [P, 256], F32, ring_at + 23040)
        prob = sb("prob", [P, 3, HPG, SEQ], F32, rest_at)
        t_c = sb("t_c", [P, NT, CMP_PAD], F32, rest_at + 49152)
        force = sb("force", [P, 4, N_SEL], F32, rest_at + 51200)
        pct = sb("pct", [CMP_PAD, HALF], F32, rest_at + 51456)
        pall = sb("pall", [P, CMP_PAD], F32, rest_at + 53504)
        imp = sb("imp", [P, N_SEL], F32, rest_at + 53760)
        score = sb("score", [P, N_SEL], F32, rest_at + 53824)
        top8 = sb("top8", [P, 8], F32, rest_at + 53888)
        picked = sb("picked", [P, N_SEL], F32, rest_at + 53952)
        selmask = sb("selmask", [P, GROUPS, N_SEL], F32, rest_at + 54016)
        y = sb("y", [P, KD, SEQ], F32, kv_at)
        m_hi = sb("m_hi", [P, KD, SEQ], F32R, rest_at)
        m_lo = sb("m_lo", [P, KD, SEQ], F32R, kv_at + 32768)
        nx = sb("nx", [P, 2, HALF], F32, rest_at + 32768)
        nh = sb("nh", [P, 2, HALF], F32, rest_at + 36864)
        nsq = sb("nsq", [P, 2, HALF], F32, rest_at + 40960)
        nacc = sb("nacc", [P, 2, HALF], F32, rest_at + 45056)
        hacc = sb("hacc", [P, SEQ], F32, rest_at + 49152)
        hsq = sb("hsq", [P, 2, HALF], F32, rest_at + 53248)
        u_hi = sb("u_hi", [P, FQ, SEQ], F32R, qa_at)
        u_lo = sb("u_lo", [P, FQ, SEQ], F32R, qa_at + 32768)
        yacc = sb("yacc", [P, KD, SEQ], F32, kv_at)
        uz = sb("uz", [P, 2, SEQ], F32, rest_at + 32768)
        fsq = sb("fsq", [P, 2, SEQ], F32, rest_at + 32768)
        facc = sb("facc", [P, SEQ], F32, rest_at + 53248)
        fh = sb("fh", [P, KD, SEQ], F32, rest_at)
        fo = sb("fo", [P, KD, SEQ], F32, qa_at)

        mp = [ctx.enter_context(nc.psum_tensor(f"mp{i}", [P, SEQ], F32)) for i in range(2)]
        pt = [ctx.enter_context(nc.psum_tensor(f"pt{i}", [P, HALF], F32)) for i in range(2)]
        ob = [ctx.enter_context(nc.psum_tensor(f"ob{i}", [P, HALF], F32)) for i in range(2)]
        tp = [pt[0][:], pt[1][:], ob[0][:], mp[1][:, HALF:SEQ]]
        stat = ob[1]

        def sem(name):
            return ctx.enter_context(nc.semaphore(name))

        s_const = sem("consts_loaded")
        s_x = [sem("x_loaded0"), sem("x_loaded1")]
        s_xh, s_xl = sem("x_hi_ready"), sem("x_lo_ready")
        s_sq, s_xq = sem("squares_ready"), sem("squares_added")
        s_ss, s_sd, s_rstd = sem("sum_ready"), sem("std_ready"), sem("rstd_ready")
        s_w = [sem("w_loaded0"), sem("w_loaded1")]
        s_wh, s_wl = sem("w_hi_ready"), sem("w_lo_ready")
        s_mm, s_ev = sem("product_ready"), sem("product_taken")
        s_zh, s_za, s_zl = sem("z_hi_ready"), sem("z_copied"), sem("z_lo_written")
        s_sig, s_vt, s_vh, s_vl = sem("gates_ready"), sem("v_turned"), sem("v_hi_ready"), sem("v_lo_ready")
        s_cw, s_blk, s_hp, s_hid = sem("cmp_weights_loaded"), sem("blocks_ready"), sem("hidden_sum"), sem("hidden_ready")
        s_kcp, s_kch, s_kcl = sem("kv_cmp_sum"), sem("kc_hi_ready"), sem("kc_lo_ready")
        s_tab, s_zero = sem("tables_loaded"), sem("zeroed")
        s_S, s_sc, s_exp = sem("scores_ready"), sem("scores_taken"), sem("exp_ready")
        s_ns, s_post, s_p = sem("sink_shift_ready"), sem("scale_ready"), sem("probs_ready")
        s_dc, s_mask, s_wm = sem("dve_chain"), sem("selection_ready"), sem("mask_ready")
        s_tr, s_hi, s_lo, s_pv = sem("probs_turned"), sem("turned_hi"), sem("turned_lo"), sem("pv_done")
        s_oh, s_oev = sem("mixed_hi"), sem("mixed_lo")
        s_y, s_nsq, s_nq = sem("y_ready"), sem("y_squares"), sem("y_squares_added")
        s_nss, s_nsd, s_nr = sem("mix_sum"), sem("mix_std"), sem("mix_rstd")
        s_nx = [sem("nx_loaded0"), sem("nx_loaded1")]
        s_t, s_h = sem("normed"), sem("h_ready")
        s_mh, s_ml, s_hs, s_ha = sem("m_hi_ready"), sem("m_lo_ready"), sem("h_squares"), sem("h_squares_added")
        s_hst = [sem("h_stored0"), sem("h_stored1")]
        s_hss, s_hsd, s_hr = sem("h_sum"), sem("h_std"), sem("h_rstd")
        s_u, s_uh, s_ul = sem("u_ready"), sem("u_hi_ready"), sem("u_lo_ready")
        s_fh, s_fs, s_fa = sem("h_loaded"), sem("y2_squares"), sem("y2_squares_added")
        s_fss, s_fsd, s_fr, s_ft, s_fo, s_fp, s_out = (sem(n) for n in (
            "y2_sum", "y2_std", "y2_rstd", "y2_normed", "out_ready", "out_ready_pool", "out_stored"))

        BLOCKS = [(kind, i, g) for i in range(NT) for g in range(GROUPS) for kind in ("cmp", "win", "sel", "swa")]

        def keys(kind, i):
            before = {"win": 4, "sel": NT, "swa": 1}[kind]
            first = max(0, i - before)
            return first * P, (i + 1 - first) * P

        ITEMS, STEPS = [], []
        ITEM_END, STEP_END, EXP_END, SCALED_END = [], [], [], []
        exps = scaled = 0
        for b, (kind, i, g) in enumerate(BLOCKS):
            ITEMS += [(b, h) for h in ([None] if kind == "cmp" else range(HPG))]
            STEPS += [(b, t) for t in range(1 if kind == "cmp" else keys(kind, i)[1] // P)]
            exps += HPG + (kind == "swa")
            scaled += kind != "cmp"
            ITEM_END.append(len(ITEMS))
            STEP_END.append(len(STEPS))
            EXP_END.append(exps)
            SCALED_END.append(scaled)
        NB = len(BLOCKS)

        def merged(s):
            a = [("S", n) for n in range(ITEM_END[s - 1] if s else 0, ITEM_END[s])] if s < NB else []
            c = [("T", t) for t in range(STEP_END[s - 3] if s >= 3 else 0, STEP_END[s - 2])] if s >= 2 else []
            la, lc = max(len(a), 1), max(len(c), 1)
            both = [((n + 0.4) / la, 0, e) for n, e in enumerate(a)] + [((n + 0.5) / lc, 1, e) for n, e in enumerate(c)]
            return [e for _, _, e in sorted(both)]

        SELECTS = [(i, g) for i in range(4, NT) for g in range(GROUPS)]
        CLOSES = {STEP_END[b] - 1: b for b in range(NB) if BLOCKS[b][0] in ("sel", "swa")}
        CLOSE_NO = {t: n for n, t in enumerate(sorted(CLOSES))}

        POOL_ADDS = [0, 3, 6]

        def w_slab(u):
            if u < U_OUT:
                return w_in[u % N_IN]
            return w_out[(u - U_OUT) % KD]

        block = ctx.enter_context(nc.Block())

        @block.sync
        def _(sp):
            for dst, at, n in ((ident, C_IDENT, P), (ones, C_ONES, P), (qscale, C_QS, N_Q_CHUNKS)):
                sp.dma_start(dst[:], consts[:, at:at + n]).then_inc(s_const, 16)
            sp.dma_start(gain[:], gains).then_inc(s_const, 16)
            sp.dma_start(sink[:], sinks).then_inc(s_const, 16)

            def load_w(u):
                if u >= 2:
                    sp.wait_ge(s_wl, u - 1)
                sp.dma_start(w_raw[u % 2][:], w_slab(u)).then_inc(s_w[u % 2], 16)

            def load_x(n):
                if n >= 2:
                    sp.wait_ge(s_xl, n - 1)
                    sp.wait_ge(s_sq, n - 1)
                sp.dma_start(x_raw[:, n % 2, :], xT[n % KD, :, (n // KD) * HALF:(n // KD + 1) * HALF]).then_inc(s_x[n % 2], 16)

            load_x(0)
            load_x(1)
            load_w(0)
            load_w(1)
            for n in range(2, KD):
                load_x(n)
            for u in range(2, N_IN):
                load_w(u)
            load_x(KD)
            load_x(KD + 1)
            load_w(N_IN)
            load_w(N_IN + 1)
            for n in range(KD + 2, 2 * KD):
                load_x(n)
            for u in range(N_IN + 2, U_OUT):
                load_w(u)

            sp.wait_ge(s_mm, U_OUT)
            sp.wait_ge(s_zl, 2 * 11)
            sp.wait_ge(s_za, 2 * 11)
            for kv in range(2):
                sp.dma_start(pe_sb[:, kv, :], pe_in[kv]).then_inc(s_cw, 16)
                sp.dma_start(w2_sb[:, kv], w2[kv]).then_inc(s_cw, 16)
                sp.dma_start(w1_sb[kv][:], w1[kv]).then_inc(s_cw, 16)
            for dst, at, n in ((t_d, C_TD, SEQ), (t_w, C_TW, 640), (t_s, C_TS, 256)):
                sp.dma_start(dst[:], consts[:, at:at + n]).then_inc(s_tab, 16)
            sp.wait_ge(s_blk, 4)
            sp.dma_start(t_c[:], consts[:, C_TC:C_FORCE]).then_inc(s_tab, 16)
            sp.dma_start(force[:], consts[:, C_FORCE:C_QS]).then_inc(s_tab, 16)

            sp.wait_ge(s_oev, 2 * len(CLOSES))
            sp.wait_ge(s_pv, len(STEPS))

            def load_nx(n):
                if n >= 2:
                    sp.wait_ge(s_h, n - 1)
                c, hf = n % KD, n // KD
                sp.dma_start(nx[:, n % 2, :], xT[c, :, hf * HALF:(hf + 1) * HALF]).then_inc(s_nx[n % 2], 16)

            def store_h(n):
                sp.wait_ge(s_h, n + 1)
                c, hf = n % KD, n // KD
                sp.dma_start(h_dram[c, :, hf * HALF:(hf + 1) * HALF], nh[:, n % 2, :]).then_inc(s_hst[n % 2], 16)

            load_nx(0)
            load_nx(1)
            for u in range(U_OUT, U_MLP):
                load_w(u)
                n = u - U_OUT - KD - 3
                if n >= 0:
                    store_h(n)
                    load_nx(n + 2)

            def load_mlp(u, par):
                sp.wait_ge(s_wl, u - 1)
                slab = w_mlp[bass.ds(u - U_MLP, 1)].rearrange("a p k c -> p (a k) c")
                sp.dma_start(w_raw[par][:], slab).then_inc(s_w[par], 16)

            load_mlp(U_MLP, 0)
            load_mlp(U_MLP + 1, 1)
            for n in range(KD - 3, 2 * KD):
                store_h(n)
                if n + 2 < 2 * KD:
                    load_nx(n + 2)
            with sp.Fori(1, N_MLP // 2) as j:
                for par in range(2):
                    load_mlp(2 * j + (U_MLP + par), par)

            for par in range(2):
                sp.wait_ge(s_hst[par], 16 * KD)
            sp.wait_ge(s_mm, N_UNITS - FQ)
            for c in range(KD):
                sp.dma_start(fh[:, c, :], h_dram[c]).then_inc(s_fh, 16)
            for c in range(KD):
                if c in POOL_ADDS:
                    sp.wait_ge(s_fp, POOL_ADDS.index(c) + 1)
                else:
                    sp.wait_ge(s_fo, c - sum(p < c for p in POOL_ADDS) + 1)
                sp.dma_start(out[c], fo[:, c, :]).then_inc(s_out, 16)
            sp.wait_ge(s_out, 16 * KD)

        @block.tensor
        def _(pe):
            def unit(u, par, out_at, hi, lo, before_k=None):
                pe.wait_ge(s_wl, u + 1)
                if not isinstance(u, int) or u >= 2:
                    pe.wait_ge(s_ev, u - 1)
                for n, (dst, a, b) in enumerate(zip(out_at, hi, lo)):
                    for k in range(KD):
                        if before_k:
                            before_k(n, k)
                        pe.matmul(dst, w_hi[par][:, k, :], a(k), start=(k == 0), stop=False)
                        pe.matmul(dst, w_hi[par][:, k, :], b(k), start=False, stop=False)
                        last = pe.matmul(dst, w_lo[par][:, k, :], a(k), start=False, stop=(k == KD - 1))
                last.then_inc(s_mm, 1)

            pe.wait_ge(s_const, 16 * 5)
            for hf in range(2):
                for j in range(N_IN):
                    u = hf * N_IN + j
                    unit(u, u % 2, [mp[u % 2][:, 0:HALF]], [lambda k: x_hi[:, k, :]], [lambda k: x_lo[:, k, :]],
                         (lambda n, k: pe.wait_ge(s_xl, hf * KD + k + 1)) if j == 0 else None)
                    if j == 0:
                        pe.wait_ge(s_xq, KD * (hf + 1))
                        pe.matmul(stat[:], ones[:], rstd[:], start=True, stop=True).then_inc(s_ss, 1)
                    if j == GATES + 2:
                        pe.wait_ge(s_ev, hf * N_IN + GATES + 1)
                        pe.wait_ge(s_sig, hf + 1)
                        if hf:
                            pe.wait_ge(s_vl, 4)
                        for v in range(4):
                            for t in range(4):
                                last = pe.transpose(tp[v][:, t * P:(t + 1) * P], zv[:, v, t * P:(t + 1) * P], ident[:])
                            last.then_inc(s_vt, 1)

            for kv in range(2):
                pe.wait_ge(s_cw, 16 * 6)
                pe.wait_ge(s_blk, 2 * kv + 2)
                for hh in range(2):
                    for pp in range(16):
                        last = pe.matmul(pt[kv][:, hh * P:hh * P + 2 * N_CMP], w1_sb[kv][:, pp, hh * P:(hh + 1) * P],
                                         blk[kv][:, pp, :], start=(pp == 0), stop=(pp == 15))
                last.then_inc(s_hp, 1)
            pe.wait_ge(s_hid, 1)
            for hh in range(2):
                last = pe.matmul(ob[0][:, 0:2 * N_CMP], w2_sb[:, 0, hh, :], hid[0][:, hh, :], start=(hh == 0), stop=(hh == 1))
            last.then_inc(s_kcp, 1)
            pe.wait_ge(s_hid, 2)
            for g in range(GROUPS):
                for hh in range(2):
                    last = pe.matmul(ob[1][0:N_CMP, g * HD:(g + 1) * HD], hid[1][:, hh, g * N_CMP:(g + 1) * N_CMP],
                                     w2_sb[:, 1, hh, 0:HD], start=(hh == 0), stop=(hh == 1))
            last.then_inc(s_kcp, 1)

            pe.wait_ge(s_kcl, 1)
            pe.wait_ge(s_kcp, 2)

            def scores(n):
                b, h = ITEMS[n]
                kind, i, g = BLOCKS[b]
                if n >= 2:
                    pe.wait_ge(s_sc, n - 1)
                dst = mp[n % 2]
                toks = slice(i * P, (i + 1) * P)
                if kind == "cmp":
                    for r in range(HPG):
                        q = qa[:, g * HPG + r, toks]
                        at = dst[:, r * CMP_PAD:(r + 1) * CMP_PAD]
                        pe.matmul(at, q, kc_hi[:, g, :], start=True, stop=False)
                        last = pe.matmul(at, q, kc_lo[:, g, :], start=False, stop=True)
                else:
                    typ = {"win": WIN, "sel": SLC, "swa": SWA}[kind]
                    q = qa[:, (8 if kind == "swa" else 0) + g * HPG + h, toks]
                    first, width = keys(kind, i)
                    for at in range(0, width, HALF):
                        w = min(HALF, width - at)
                        ks = slice(first + at, first + at + w)
                        pe.matmul(dst[:, at:at + w], q, k_hi[:, typ, g, ks], start=True, stop=False)
                        last = pe.matmul(dst[:, at:at + w], q, k_lo[:, typ, g, ks], start=False, stop=True)
                last.then_inc(s_S, 1)

            def turn(t):
                b, kt = STEPS[t]
                kind, i, g = BLOCKS[b]
                if kind == "cmp":
                    pe.wait_ge(s_post, b + 1)
                else:
                    pe.wait_ge(s_p, SCALED_END[b])
                if t >= 2:
                    pe.wait_ge(s_lo, t - 1)
                for r in range(HPG):
                    if kind == "cmp":
                        last = pe.transpose(pt[t % 2][0:CMP_PAD, r * P:(r + 1) * P],
                                            prob[:, b % 3, 0, r * CMP_PAD:(r + 1) * CMP_PAD], ident[:])
                    else:
                        last = pe.transpose(pt[t % 2][:, r * P:(r + 1) * P], prob[:, b % 3, r, kt * P:(kt + 1) * P], ident[:])
                last.then_inc(s_tr, 1)

            def weigh(t):
                b, kt = STEPS[t]
                kind, i, g = BLOCKS[b]
                dst = ob[kind == "swa"][0:HD, :]
                opens = kind == "cmp" or (kind == "swa" and kt == 0)
                if opens:
                    n = sum(c < t for c in CLOSES)
                    if n >= 2:
                        pe.wait_ge(s_oev, 2 * (n - 1))
                pe.wait_ge(s_lo, t + 1)
                if kind == "cmp":
                    last = pe.matmul(dst, vc[:, g, :], pct[:], start=True, stop=False)
                else:
                    typ = {"win": WIN, "sel": SLC, "swa": SWA}[kind]
                    first, width = keys(kind, i)
                    tile = first // P + kt
                    vh, vl = (v[:, typ, tile, g * HD:(g + 1) * HD] for v in (v_hi, v_lo))
                    end = t in CLOSES
                    pe.matmul(dst, vh, pt_hi[:, t % 2, :], start=opens, stop=False)
                    pe.matmul(dst, vl, pt_hi[:, t % 2, :], start=False, stop=False)
                    last = pe.matmul(dst, vh, pt_lo[:, t % 2, :], start=False, stop=end)
                last.then_inc(s_pv, 1)

            for s in range(NB + 2):
                for what, n in merged(s):
                    if what == "S":
                        scores(n)
                    else:
                        turn(n)
                        if n >= 1:
                            weigh(n - 1)
            weigh(len(STEPS) - 1)

            pe.wait_ge(s_oev, 2 * len(CLOSES))
            for hf in range(2):
                toks = slice(hf * HALF, (hf + 1) * HALF)
                for c in range(KD):
                    u = U_OUT + hf * KD + c
                    unit(u, u % 2, [mp[u % 2][:, 0:HALF]], [lambda k: qa[:, 2 * k, toks]], [lambda k: qa[:, 2 * k + 1, toks]])
                    if hf == 1 and c == 0:
                        pe.wait_ge(s_nq, KD)
                        pe.matmul(stat[:], ones[:], nacc[:, 0, :], start=True, stop=True).then_inc(s_nss, 1)
            pe.wait_ge(s_nq, 2 * KD)
            pe.matmul(stat[:], ones[:], nacc[:, 1, :], start=True, stop=True).then_inc(s_nss, 1)

            halves = [slice(0, HALF), slice(HALF, SEQ)]

            def up(u, par, before_k=None):
                unit(u, par, [mp[par][:, t] for t in halves], [(lambda k, t=t: m_hi[:, k, t]) for t in halves],
                     [(lambda k, t=t: m_lo[:, k, t]) for t in halves], before_k)

            def down(u, par, q):
                def before(n, k):
                    if n == 0 and par == 0 and k in (0, KD - 1):
                        pe.wait_ge(s_ul, q * FQ + (FQ - 1 if k == 0 else FQ))
                unit(u, par, [mp[par][:, t] for t in halves], [(lambda k, t=t: u_hi[:, k, t]) for t in halves],
                     [(lambda k, t=t: u_lo[:, k, t]) for t in halves], before)

            up(U_MLP, 0, lambda n, k: pe.wait_ge(s_ml, n * KD + k + 1))
            pe.wait_ge(s_ha, 2 * KD)
            for hf in range(2):
                pe.matmul(pt[hf][:], ones[:], hacc[:, hf * HALF:(hf + 1) * HALF], start=True, stop=True).then_inc(s_hss, 1)
            up(U_MLP + 1, 1)
            with pe.Fori(1, FQ // 2) as j:
                for par in range(2):
                    up(2 * j + (U_MLP + par), par)
            with pe.Fori(0, FQ // 2) as j:
                for par in range(2):
                    down(2 * j + (U_MLP + FQ + par), par, 0)
            with pe.Fori(1, QUARTERS) as q:
                with pe.Fori(0, FQ // 2) as j:
                    for par in range(2):
                        up(q * (2 * FQ) + 2 * j + (U_MLP + par), par)
                with pe.Fori(0, FQ // 2) as j:
                    for par in range(2):
                        down(q * (2 * FQ) + 2 * j + (U_MLP + FQ + par), par, q)
            pe.wait_ge(s_fa, KD)
            for hf in range(2):
                pe.matmul(pt[hf][:], ones[:], facc[:, hf * HALF:(hf + 1) * HALF], start=True, stop=True).then_inc(s_fss, 1)

        @block.scalar
        def _(act):
            copy = lambda dst, src, **kw: act.activation(dst, src, ACT.Copy, **kw)

            def split_w(u, par=None):
                if par is None:
                    par = u % 2
                act.wait_ge(s_w[par], 8 * u + (16 - 8 * par))
                if not isinstance(u, int) or u >= 2:
                    act.wait_ge(s_mm, u - 1)
                copy(w_hi[par][:], w_raw[par][:]).then_inc(s_wh, 1)

            act.wait_ge(s_const, 16 * 5)
            act.wait_ge(s_zero, 1)
            zn = 0
            for hf in range(2):
                for k in range(KD):
                    n = hf * KD + k
                    act.wait_ge(s_x[n % 2], 16 * (n // 2 + 1))
                    if hf:
                        act.wait_ge(s_mm, N_IN)
                    copy(x_hi[:, k, :], x_raw[:, n % 2, :], scale=gain[:, 0, k:k + 1]).then_inc(s_xh, 1)
                    if n >= 2:
                        act.wait_ge(s_xq, n - 1)
                    if k < 2 and hf:
                        act.wait_ge(s_zl, 11)
                        act.wait_ge(s_za, 11)
                    act.activation(sq[n % 2][:], x_raw[:, n % 2, :], ACT.Square).then_inc(s_sq, 1)
                    if n < 2:
                        split_w(n)
                act.wait_ge(s_ss, hf + 1)
                act.wait_ge(s_xq, KD * (hf + 1))
                act.activation(rstd[:], stat[:], ACT.Sqrt, bias=eps[:, 0:1], scale=1.0 / D_MODEL).then_inc(s_sd, 1)
                for j in range(N_IN):
                    u = hf * N_IN + j
                    if u + 1 < U_OUT and u >= 1:
                        split_w(u + 1)
                    if j == GATES:
                        act.wait_ge(s_ev, u + 1)
                        act.activation(zv[:, 3, :], zv[:, 3, :], ACT.Sigmoid).then_inc(s_sig, 1)
                    if j == GATES + 3:
                        for v in range(3):
                            act.wait_ge(s_vt, 4 * hf + v + 1)
                            copy(v_hi[:, [SWA, SLC, WIN][v], 4 * hf:4 * hf + 4, :], tp[v]).then_inc(s_vh, 1)
                    is_k = j in (KS_SWA, K_SLC, K_WIN)
                    if is_k or j >= N_KV_CHUNKS:
                        toks = slice(hf * HALF, (hf + 1) * HALF)
                        act.wait_ge(s_ev, u + 1)
                        if zn:
                            act.wait_ge(s_zl, zn)
                        copy(z_hi[:], z[:]).then_inc(s_zh, 1)
                        for g in range(2):
                            src = z[g * HD:(g + 1) * HD, :]
                            if is_k:
                                typ = {KS_SWA: SWA, K_SLC: SLC, K_WIN: WIN}[j]
                                copy(k_hi[0:HD, typ, g, toks], src)
                                last = copy(k_hi[HD:P, typ, g, toks], src)
                            else:
                                last = copy(qa[0:HD, 2 * (j - N_KV_CHUNKS) + g, toks], src)
                        last.then_inc(s_za, 1)
                        zn += 1

            for kv in range(2):
                act.wait_ge(s_hp, kv + 1)
                src = pt[kv][:, 0:2 * P].rearrange("p (h n) -> p h n", h=2)[:, :, 0:2 * N_CMP]
                act.activation(hid[kv][:], src, ACT.Gelu_apprx_tanh).then_inc(s_hid, 1)
            act.wait_ge(s_kcp, 1)
            copy(kc_hi[:, :, 0:N_CMP], ob[0][:, 0:2 * N_CMP].rearrange("p (g n) -> p g n", g=2)).then_inc(s_kch, 1)

            def exp_item(n):
                b, h = ITEMS[n]
                kind, i, g = BLOCKS[b]
                base = g * HPG + (8 if kind == "swa" else 0)
                act.wait_ge(s_sc, n + 1)
                for r in (range(HPG) if h is None else [h]):
                    if h is None:
                        p = prob[:, b % 3, 0, r * CMP_PAD:(r + 1) * CMP_PAD]
                    else:
                        p = prob[:, b % 3, r, 0:keys(kind, i)[1]]
                    act.activation(p, p, ACT.Exp, bias=nmax[:, b % 3, r:r + 1], scale=-1.0,
                                   accum_out=den[:, b % 3, r:r + 1]).then_inc(s_exp, 1)
                if kind == "swa" and h == HPG - 1:
                    act.wait_ge(s_ns, i * GROUPS + g + 1)
                    act.activation(esink[:, b % 3, :], esink[:, b % 3, :], ACT.Exp).then_inc(s_exp, 1)

            def turned_hi(t):
                b, kt = STEPS[t]
                act.wait_ge(s_tr, t + 1)
                if t >= 2:
                    act.wait_ge(s_pv, t - 1)
                if BLOCKS[b][0] == "cmp":
                    if b >= 4:
                        act.wait_ge(s_pv, STEP_END[b - 4])
                    copy(pct[:, 0:256], pt[t % 2][0:CMP_PAD, 0:256]).then_inc(s_hi, 1)
                else:
                    copy(pt_hi[:, t % 2, :], pt[t % 2][:]).then_inc(s_hi, 1)

            def mixed_hi(t):
                kind, i, g = BLOCKS[STEPS[t][0]]
                act.wait_ge(s_pv, t + 1)
                h0 = (8 if kind == "swa" else 0) + g * HPG
                src = ob[kind == "swa"][0:HD, :].rearrange("p (c e q) -> p e c q", c=2, e=2)
                for e in range(2):
                    copy(qa[e * HD:(e + 1) * HD, h0:h0 + HPG:2, i * P:(i + 1) * P], src[:, e]).then_inc(s_oh, 1)

            for s in range(NB + 2):
                for what, n in merged(s):
                    if what == "S":
                        exp_item(n)
                    else:
                        if n - 2 in CLOSES:
                            mixed_hi(n - 2)
                        turned_hi(n)
            for t in range(len(STEPS) - 2, len(STEPS)):
                if t in CLOSES:
                    mixed_hi(t)

            def norm_act(n):
                c, hf = n % KD, n // KD
                act.wait_ge(s_h, n + 1)
                copy(m_hi[:, c, hf * HALF:(hf + 1) * HALF], nh[:, n % 2, :], scale=gain[:, 2, c:c + 1]).then_inc(s_mh, 1)
                if n >= 2:
                    act.wait_ge(s_ha, n - 1)
                act.activation(hsq[:, n % 2, :], nh[:, n % 2, :], ACT.Square).then_inc(s_hs, 1)

            def mix_std(hf):
                act.wait_ge(s_nss, hf + 1)
                act.activation(nacc[:, hf, :], stat[:], ACT.Sqrt, bias=eps[:, 0:1], scale=1.0 / D_MODEL).then_inc(s_nsd, 1)

            act.wait_ge(s_lo, len(STEPS))
            split_w(U_OUT)
            for hf in range(2):
                for c in range(KD):
                    n = hf * KD + c
                    u = U_OUT + n
                    split_w(u + 1)
                    act.wait_ge(s_mm, u + 1)
                    copy(y[:, c, hf * HALF:(hf + 1) * HALF], mp[u % 2][:, 0:HALF]).then_inc(s_y, 1)
                    if n >= 2:
                        act.wait_ge(s_nq, n - 1)
                    act.activation(nsq[:, n % 2, :], mp[u % 2][:, 0:HALF], ACT.Square).then_inc(s_ev, 1)
                    if hf == 1:
                        if c == 0:
                            mix_std(0)
                        if c >= 2:
                            norm_act(c - 2)
            norm_act(KD - 2)
            norm_act(KD - 1)
            mix_std(1)
            for n in range(KD, 2 * KD):
                norm_act(n)

            def h_std():
                for hf in range(2):
                    act.wait_ge(s_hss, hf + 1)
                    act.activation(hacc[:, hf * HALF:(hf + 1) * HALF], pt[hf][:], ACT.Sqrt, bias=eps[:, 0:1],
                                   scale=1.0 / D_MODEL).then_inc(s_hsd, 1)

            def up_act(u, par, f, done):
                split_w(u + 1, 1 - par)
                act.wait_ge(s_u, done)
                copy(u_hi[:, bass.ds(f, 1), :].rearrange("p a t -> p (a t)"), uz[:, par, :]).then_inc(s_uh, 1)

            def quarter(q, last):
                u0 = q * (2 * FQ) + U_MLP
                with act.Fori(0, FQ // 2) as j:
                    for par in range(2):
                        f = 2 * j + par
                        up_act(u0 + f, par, f, q * FQ + f + 1)
                n = FQ // 2 - (1 if last else 0)
                with act.Fori(0, n) as j:
                    for par in range(2):
                        split_w(u0 + 2 * j + (FQ + par + 1), 1 - par)

            h_std()
            quarter(0, False)
            with act.Fori(1, QUARTERS - 1) as q:
                quarter(q, False)
            quarter(QUARTERS - 1, True)
            split_w(N_UNITS - 1)

            act.wait_ge(s_mm, N_UNITS)
            for c in range(KD):
                act.wait_ge(s_ev, N_UNITS - KD + c + 1)
                if c >= 2:
                    act.wait_ge(s_fa, c - 1)
                act.activation(fsq[:, c % 2, :], yacc[:, c, :], ACT.Square).then_inc(s_fs, 1)
            for hf in range(2):
                act.wait_ge(s_fss, hf + 1)
                act.activation(facc[:, hf * HALF:(hf + 1) * HALF], pt[hf][:], ACT.Sqrt, bias=eps[:, 0:1],
                               scale=1.0 / D_MODEL).then_inc(s_fsd, 1)

        @block.vector
        def _(dve):
            TT, STT, TS = dve.tensor_tensor, dve.scalar_tensor_tensor, dve.tensor_scalar
            f32 = lambda ap: ap.bitcast(F32)
            chain = [0]

            def link(ins):
                ins.then_inc(s_dc, 1)
                chain[0] += 1
                dve.wait_ge(s_dc, chain[0])

            def split_w(u, par=None):
                if par is None:
                    par = u % 2
                dve.wait_ge(s_wh, u + 1)
                TT(w_lo[par][:], w_raw[par][:], f32(w_hi[par][:]), ALU.subtract).then_inc(s_wl, 1)

            dve.memset(eps[:], EPS)
            dve.memset(f32(kc_hi[:]), 0.0)
            dve.memset(f32(kc_lo[:]), 0.0)
            dve.memset(vc[:], 0.0).then_inc(s_zero, 1)
            dve.wait_ge(s_const, 16 * 5)
            link(TS(nsink[:], sink[:], -1.0, None, ALU.mult))

            zn = 0
            for hf in range(2):
                for k in range(KD):
                    n = hf * KD + k
                    dve.wait_ge(s_xh, n + 1)
                    STT(x_lo[:, k, :], x_raw[:, n % 2, :], gain[:, 0, k:k + 1], f32(x_hi[:, k, :]), ALU.mult,
                        ALU.subtract).then_inc(s_xl, 1)
                    dve.wait_ge(s_sq, n + 1)
                    if k:
                        dve.wait_ge(s_xq, n)
                        TT(rstd[:], rstd[:], sq[n % 2][:], ALU.add).then_inc(s_xq, 1)
                    else:
                        if hf:
                            dve.wait_ge(s_ev, N_IN)
                        dve.tensor_copy(rstd[:], sq[n % 2][:]).then_inc(s_xq, 1)
                    if n < 2:
                        split_w(n)
                dve.wait_ge(s_sd, hf + 1)
                dve.reciprocal(rstd[:], rstd[:]).then_inc(s_rstd, 1)
                dve.wait_ge(s_rstd, hf + 1)
                for j in range(N_IN):
                    u = hf * N_IN + j
                    if u + 1 < U_OUT and u >= 1:
                        split_w(u + 1)
                    dve.wait_ge(s_mm, u + 1)
                    src = mp[u % 2][:, 0:HALF]
                    toks = slice(hf * HALF, (hf + 1) * HALF)
                    if j in (VT_SWA, VT_SLC, VT_WIN, GATES):
                        v = {VT_SWA: 0, VT_SLC: 1, VT_WIN: 2, GATES: 3}[j]
                        if hf:
                            dve.wait_ge(s_vt, 4)
                        TT(zv[:, v, :], src, rstd[:], ALU.mult).then_inc(s_ev, 1)
                    elif j in (KC, VC_):
                        kv = int(j == VC_)
                        for g in range(GROUPS):
                            rows = slice(g * HD, (g + 1) * HD)
                            a = src[rows, :].rearrange("p (n q e) -> p e q n", q=8, e=2)
                            b = rstd[rows, :].rearrange("p (n q e) -> p e q n", q=8, e=2)
                            for e in range(2):
                                last = TT(zkv[e * HD:(e + 1) * HD, kv, :, g, hf * 32:hf * 32 + 32], a[:, e], b[:, e], ALU.mult)
                        last.then_inc(s_ev, 1)
                    else:
                        if zn:
                            dve.wait_ge(s_za, zn)
                            dve.wait_ge(s_zl, zn)
                        if j < N_KV_CHUNKS:
                            TT(z[:], src, rstd[:], ALU.mult).then_inc(s_ev, 1)
                        else:
                            c = j - N_KV_CHUNKS
                            STT(z[:], src, qscale[:, c:c + 1], rstd[:], ALU.mult, ALU.mult).then_inc(s_ev, 1)
                        dve.wait_ge(s_ev, u + 1)
                        dve.wait_ge(s_zh, zn + 1)
                        for g in range(2):
                            rows = slice(g * HD, (g + 1) * HD)
                            if j < N_KV_CHUNKS:
                                typ = {KS_SWA: SWA, K_SLC: SLC, K_WIN: WIN}[j]
                                TT(k_lo[0:HD, typ, g, toks], z[rows, :], f32(z_hi[rows, :]), ALU.subtract)
                                last = TT(k_lo[HD:P, typ, g, toks], z[rows, :], f32(z_hi[rows, :]), ALU.subtract)
                            else:
                                last = TT(qa[HD:P, 2 * (j - N_KV_CHUNKS) + g, toks], z[rows, :], f32(z_hi[rows, :]), ALU.subtract)
                        last.then_inc(s_zl, 1)
                        zn += 1
                    if j == GATES + 3:
                        for v in range(3):
                            dve.wait_ge(s_vh, 3 * hf + v + 1)
                            at = (slice(None), [SWA, SLC, WIN][v], slice(4 * hf, 4 * hf + 4), slice(None))
                            TT(v_lo[at], tp[v].rearrange("p (t c) -> p t c", t=4), f32(v_hi[at]), ALU.subtract).then_inc(s_vl, 1)
                        dve.wait_ge(s_vt, 4 * hf + 4)
                        dve.tensor_copy(gate[:, 4 * hf:4 * hf + 4, :],
                                        tp[3].rearrange("p (t c) -> p t c", t=4)[:, :, 0:24]).then_inc(s_vl, 1)

            dve.wait_ge(s_cw, 16 * 6)
            dve.wait_ge(s_ev, U_OUT)
            dve.wait_ge(s_vl, 8)
            for kv in range(2):
                for late in range(2):
                    dst = blk[kv][:, 8 * late:8 * late + 8, :].rearrange("p q (g n) -> p q g n", g=GROUPS)
                    src = zkv[:, kv, :, :, late:late + N_CMP]
                    emb = pe_sb[:, kv, 8 * late:8 * late + 8].unsqueeze(2).unsqueeze(3).to_broadcast([P, 8, GROUPS, N_CMP])
                    TT(dst, src, emb, ALU.add).then_inc(s_blk, 1)
            dve.wait_ge(s_kch, 1)
            TT(kc_lo[:, :, 0:N_CMP], ob[0][:, 0:2 * N_CMP].rearrange("p (g n) -> p g n", g=2), f32(kc_hi[:, :, 0:N_CMP]), ALU.subtract)
            dve.wait_ge(s_kcp, 2)
            dve.tensor_copy(vc[0:N_CMP, :, :], ob[1][0:N_CMP, 0:P].rearrange("p (g n) -> p g n", g=2)).then_inc(s_kcl, 1)
            dve.wait_ge(s_tab, 16 * 5)

            def score_item(n):
                b, h = ITEMS[n]
                kind, i, g = BLOCKS[b]
                dve.wait_ge(s_S, n + 1)
                if b >= 3:
                    dve.wait_ge(s_tr, STEP_END[b - 3])
                for r in (range(HPG) if h is None else [h]):
                    if kind == "cmp":
                        src = mp[n % 2][:, r * CMP_PAD:(r + 1) * CMP_PAD]
                        dst = prob[:, b % 3, 0, r * CMP_PAD:(r + 1) * CMP_PAD]
                        table, head, floor = t_c[:, i, :], g * HPG + r, NO_KEY
                    else:
                        first, width = keys(kind, i)
                        src, dst = mp[n % 2][:, 0:width], prob[:, b % 3, r, 0:width]
                        head, floor = g * HPG + r, 3e38
                        if kind == "swa":
                            table, head, floor = t_s[:, 256 - width:256], 8 + head, nsink[:, g * HPG + r:g * HPG + r + 1]
                        elif kind == "win":
                            table = t_w[:, 640 - width:640]
                        elif i < 4:
                            table = t_d[:, SEQ - width:SEQ]
                        else:
                            dve.wait_ge(s_wm, SELECTS.index((i, g)) + 1)
                            table = wmask[:, g, 0:width]
                    last = dve.tensor_tensor_reduce(dst, src, table, -SL[head], floor, ALU.add, ALU.min, nmax[:, b % 3, r:r + 1])
                last.then_inc(s_sc, 1)
                if kind == "swa" and h == HPG - 1:
                    dve.wait_ge(s_sc, n + 1)
                    TT(esink[:, b % 3, :], nmax[:, b % 3, :], sink[:, g * HPG:(g + 1) * HPG], ALU.add).then_inc(s_ns, 1)

            def post(b):
                kind, i, g = BLOCKS[b]
                d, r = den[:, b % 3, :], rgate[:, b % 3, :]
                dve.wait_ge(s_exp, EXP_END[b])
                gates = gate[:, i, g * 12:(g + 1) * 12].rearrange("p (h k) -> p k h", k=3)
                if kind == "cmp":
                    pr = prob[:, b % 3, 0, 0:HPG * CMP_PAD].rearrange("p (h n) -> p h n", h=HPG)
                    wide = lambda ap: ap.unsqueeze(2).to_broadcast([P, HPG, CMP_PAD])
                    link(TS(d, d, 1e-30, None, ALU.max))
                    link(dve.reciprocal(r, d))
                    link(TT(pr, pr, wide(r), ALU.mult))
                    if i >= 4:
                        link(dve.tensor_reduce(pall[:], pr.rearrange("p h n -> p n h"), AX.X, ALU.add))
                        link(dve.tensor_reduce(imp[:], pall[:].rearrange("p (j r) -> p j r", r=4), AX.X, ALU.add))
                        link(TT(imp[:, 1:N_SEL], imp[:, 1:N_SEL], pall[:, 3:CMP_PAD - 1:4], ALU.add))
                        link(TT(score[:], imp[:], force[:, i - 4, :], ALU.add))
                        link(dve.max(top8[:], score[:]))
                        link(dve.match_replace(picked[:], top8[:], score[:], TAKEN))
                        n = SELECTS.index((i, g))
                        if n >= 2:
                            dve.wait_ge(s_wm, n - 1)
                        TS(selmask[:, g, :], picked[:], 1.5e30, NEG, ALU.is_lt, ALU.mult).then_inc(s_mask, 1)
                    TT(pr, pr, wide(gates[:, 0, :]), ALU.mult).then_inc(s_post, 1)
                elif kind == "swa":
                    link(TT(d, d, esink[:, b % 3, :], ALU.add))
                    dve.reciprocal(r, d).then_inc(s_post, 1)
                else:
                    link(dve.reciprocal(r, d))
                    TT(r, r, gates[:, 2 if kind == "win" else 1, :], ALU.mult).then_inc(s_post, 1)

            def turned_lo(t):
                b, kt = STEPS[t]
                dve.wait_ge(s_hi, t + 1)
                if BLOCKS[b][0] == "cmp":
                    dve.tensor_copy(pct[:, 256:HALF], pt[t % 2][0:CMP_PAD, 256:HALF]).then_inc(s_lo, 1)
                else:
                    TT(pt_lo[:, t % 2, :], pt[t % 2][:], f32(pt_hi[:, t % 2, :]), ALU.subtract).then_inc(s_lo, 1)

            def mixed_lo(t):
                kind, i, g = BLOCKS[STEPS[t][0]]
                h0 = (8 if kind == "swa" else 0) + g * HPG
                src = ob[kind == "swa"][0:HD, :].rearrange("p (c e q) -> p e c q", c=2, e=2)
                dve.wait_ge(s_oh, 2 * CLOSE_NO[t] + 2)
                for e in range(2):
                    rows, toks = slice(e * HD, (e + 1) * HD), slice(i * P, (i + 1) * P)
                    TT(qa[rows, h0 + 1:h0 + HPG:2, toks], src[:, e], f32(qa[rows, h0:h0 + HPG:2, toks]), ALU.subtract).then_inc(s_oev, 1)

            for s in range(NB + 2):
                order = merged(s)
                mid = max([k for k, e in enumerate(order) if e[0] == "S"][:2] or [0])
                for k, (what, n) in enumerate(order):
                    if what == "S":
                        score_item(n)
                    else:
                        if n - 2 in CLOSES:
                            mixed_lo(n - 2)
                        turned_lo(n)
                    if k == mid and 1 <= s <= NB:
                        post(s - 1)
            for t in range(len(STEPS) - 2, len(STEPS)):
                if t in CLOSES:
                    mixed_lo(t)

            def mix_rstd(hf):
                dve.wait_ge(s_nsd, hf + 1)
                dve.reciprocal(nacc[:, hf, :], nacc[:, hf, :]).then_inc(s_nr, 1)
                dve.wait_ge(s_nr, hf + 1)

            def norm_dve(n):
                c, hf = n % KD, n // KD
                toks = slice(hf * HALF, (hf + 1) * HALF)
                if n >= 2:
                    dve.wait_ge(s_hst[n % 2], 16 * (n // 2))
                    dve.wait_ge(s_hs, n - 1)
                STT(nh[:, n % 2, :], y[:, c, toks], gain[:, 1, c:c + 1], nacc[:, hf, :], ALU.mult, ALU.mult).then_inc(s_t, 1)
                dve.wait_ge(s_nx[n % 2], 16 * (n // 2 + 1))
                dve.wait_ge(s_t, n + 1)
                TT(nh[:, n % 2, :], nh[:, n % 2, :], nx[:, n % 2, :], ALU.add).then_inc(s_h, 1)
                dve.wait_ge(s_mh, n + 1)
                STT(m_lo[:, c, toks], nh[:, n % 2, :], gain[:, 2, c:c + 1], f32(m_hi[:, c, toks]), ALU.mult,
                    ALU.subtract).then_inc(s_ml, 1)

            split_w(U_OUT)
            for hf in range(2):
                for c in range(KD):
                    n = hf * KD + c
                    u = U_OUT + n
                    split_w(u + 1)
                    dve.wait_ge(s_ev, u + 1)
                    if c:
                        dve.wait_ge(s_nq, n)
                        TT(nacc[:, hf, :], nacc[:, hf, :], nsq[:, n % 2, :], ALU.add).then_inc(s_nq, 1)
                    else:
                        dve.tensor_copy(nacc[:, hf, :], nsq[:, n % 2, :]).then_inc(s_nq, 1)
                    if hf == 1:
                        if c == 0:
                            mix_rstd(0)
                        if c >= 2:
                            norm_dve(c - 2)
            norm_dve(KD - 2)
            norm_dve(KD - 1)
            mix_rstd(1)
            for n in range(KD, 2 * KD):
                norm_dve(n)

            def up_dve(u, par, f, done):
                split_w(u + 1, 1 - par)
                dve.wait_ge(s_mm, u + 1)
                TT(uz[:, par, :], mp[par][:], hacc[:], ALU.mult).then_inc(s_ev, 1)
                dve.wait_ge(s_ev, u + 1)
                STT(uz[:, par, :], uz[:, par, :], 0.0, uz[:, par, :], ALU.max, ALU.mult).then_inc(s_u, 1)
                dve.wait_ge(s_uh, done)
                flat = lambda ap: ap.rearrange("p a t -> p (a t)")
                TT(flat(u_lo[:, bass.ds(f, 1), :]), uz[:, par, :], flat(f32(u_hi[:, bass.ds(f, 1), :])),
                   ALU.subtract).then_inc(s_ul, 1)

            def down_dve(u, par, c, first):
                dve.wait_ge(s_mm, u + 1)
                dst = yacc[:, bass.ds(c, 1), :].rearrange("p a t -> p (a t)")
                if first:
                    dve.tensor_copy(dst, mp[par][:]).then_inc(s_ev, 1)
                else:
                    TT(dst, dst, mp[par][:], ALU.add).then_inc(s_ev, 1)

            def quarter(q, first, last):
                u0 = q * (2 * FQ) + U_MLP
                with dve.Fori(0, FQ // 2) as j:
                    for par in range(2):
                        f = 2 * j + par
                        up_dve(u0 + f, par, f, q * FQ + f + 1)
                n = FQ // 2 - (1 if last else 0)
                with dve.Fori(0, n) as j:
                    for par in range(2):
                        c = 2 * j + par
                        split_w(u0 + c + (FQ + 1), 1 - par)
                        down_dve(u0 + c + FQ, par, c, first)
                if last:
                    split_w(N_UNITS - 1)
                    down_dve(N_UNITS - 2, 0, KD - 2, first)
                    down_dve(N_UNITS - 1, 1, KD - 1, first)

            for hf in range(2):
                dve.wait_ge(s_hsd, hf + 1)
                dve.reciprocal(hacc[:, hf * HALF:(hf + 1) * HALF], hacc[:, hf * HALF:(hf + 1) * HALF]).then_inc(s_hr, 1)
            dve.wait_ge(s_hr, 2)
            for par in range(2):
                dve.wait_ge(s_hst[par], 16 * KD)
            dve.wait_ge(s_hs, 2 * KD)
            quarter(0, True, False)
            with dve.Fori(1, QUARTERS - 1) as q:
                quarter(q, False, False)
            quarter(QUARTERS - 1, False, True)

            for c in range(KD):
                dve.wait_ge(s_fs, c + 1)
                if c:
                    dve.wait_ge(s_fa, c)
                    TT(facc[:], facc[:], fsq[:, c % 2, :], ALU.add).then_inc(s_fa, 1)
                else:
                    dve.tensor_copy(facc[:], fsq[:, 0, :]).then_inc(s_fa, 1)
            for hf in range(2):
                dve.wait_ge(s_fsd, hf + 1)
                dve.reciprocal(facc[:, hf * HALF:(hf + 1) * HALF], facc[:, hf * HALF:(hf + 1) * HALF]).then_inc(s_fr, 1)
            dve.wait_ge(s_fr, 2)
            dve.wait_ge(s_fh, 16 * KD)
            for c in range(KD):
                STT(fo[:, c, :], yacc[:, c, :], gain[:, 3, c:c + 1], facc[:], ALU.mult, ALU.mult).then_inc(s_ft, 1)
                if c not in POOL_ADDS:
                    dve.wait_ge(s_ft, c + 1)
                    TT(fo[:, c, :], fo[:, c, :], fh[:, c, :], ALU.add).then_inc(s_fo, 1)

        @block.gpsimd
        def _(pool):
            for b, (kind, i, g) in enumerate(BLOCKS):
                if kind == "cmp":
                    if i >= 4:
                        n = SELECTS.index((i, g))
                        width = (i + 1) * P
                        pool.wait_ge(s_mask, n + 1)
                        if i > 4:
                            pool.wait_ge(s_sc, ITEM_END[BLOCKS.index(("sel", i - 1, g))])
                        pool.tensor_tensor(wmask[:, g, 0:width].rearrange("p (j t) -> p j t", t=HD),
                                           t_d[:, SEQ - width:SEQ].rearrange("p (j t) -> p j t", t=HD),
                                           selmask[:, g, 0:width // HD].unsqueeze(2).to_broadcast([P, width // HD, HD]),
                                           ALU.add).then_inc(s_wm, 1)
                else:
                    width = keys(kind, i)[1]
                    pool.wait_ge(s_post, b + 1)
                    for r in range(HPG):
                        pr = prob[:, b % 3, r, 0:width]
                        last = pool.tensor_scalar(pr, pr, rgate[:, b % 3, r:r + 1], 0.0, ALU.mult, ALU.add)
                    last.then_inc(s_p, 1)

            pool.wait_ge(s_oev, 2 * len(CLOSES))
            pool.wait_ge(s_hs, 1)
            pool.memset(hacc[:], 0.0).then_inc(s_zero, 1)
            pool.wait_ge(s_zero, 2)
            for n in range(2 * KD):
                toks = slice(n // KD * HALF, (n // KD + 1) * HALF)
                pool.wait_ge(s_hs, n + 1)
                if n:
                    pool.wait_ge(s_ha, n)
                pool.tensor_tensor(hacc[:, toks], hacc[:, toks], hsq[:, n % 2, :], ALU.add).then_inc(s_ha, 1)

            pool.wait_ge(s_fh, 16 * KD)
            for c in POOL_ADDS:
                pool.wait_ge(s_ft, c + 1)
                pool.tensor_tensor(fo[:, c, :], fo[:, c, :], fh[:, c, :], ALU.add).then_inc(s_fp, 1)


def kernel(**inputs):
    import concourse.bacc as bacc
    from concourse.bass_utils import run_bass_kernel_spmd

    def layer(name):
        return np.asarray(inputs[name])[0]

    def slabs(w):
        return w.reshape(w.shape[0] // P, P, w.shape[1] // P, P).transpose(2, 1, 0, 3)

    w = layer("w_in")
    starts = np.cumsum([0, 512, 128, 128, 128, 128, 128, 128, 24, 512, 128])
    q_n, kc, v_c, ks, vs, kw, vw, gt, q_s, k_s, v_s = starts
    cols = lambda at, n=P: w[:, at:at + n]
    pad = np.zeros((D_MODEL, P - 24), w.dtype)
    w_in = np.concatenate([cols(k_s), cols(v_s), cols(kc), cols(v_c), cols(vs), cols(vw),
                           cols(gt, 24), pad, cols(ks), cols(kw), cols(q_n, 512), cols(q_s, 512)], axis=1)
    up, down = slabs(layer("w_up")), layer("w_down")
    mlp = []
    for q in range(QUARTERS):
        mlp.append(up[q * FQ:(q + 1) * FQ])
        mlp.append(slabs(down[q * FQ * P:(q + 1) * FQ * P]))
    gains = np.stack([layer(n).reshape(KD, P).T for n in ("norm_mix_pre", "norm_mix_post", "norm_mlp_pre", "norm_mlp_post")], axis=1)
    w1 = np.stack([layer(n).reshape(16, P, 256).transpose(1, 0, 2) for n in ("cmp_w1_k", "cmp_w1_v")])
    w2 = np.stack([np.concatenate([layer(n)] * 2, axis=1).reshape(2, P, P).transpose(1, 0, 2) for n in ("cmp_w2_k", "cmp_w2_v")])
    pe = np.stack([layer(n).reshape(16, P).T for n in ("cmp_pe_k", "cmp_pe_v")])
    arrays = {
        "xT": np.asarray(inputs["x"])[0].T.reshape(KD, P, SEQ),
        "w_in": slabs(w_in),
        "w_out": slabs(layer("w_out")),
        "w_mlp": np.concatenate(mlp),
        "gains": gains, "w1": w1, "w2": w2, "pe": pe,
        "sinks": np.broadcast_to(layer("sinks").reshape(1, 8), (P, 8)),
        "consts": constants(),
    }
    arrays = {n: np.ascontiguousarray(a) for n, a in arrays.items()}
    nc = bacc.Bacc("TRN2", target_bir_lowering=False, num_devices=1, dynamic_dma_scratch_size=1024)
    aps = [nc.dram_tensor(n, a.shape, F32, kind="ExternalInput").ap() for n, a in arrays.items()]
    h_dram = nc.dram_tensor("h_scratch", (KD, P, SEQ), F32, kind="Internal").ap()
    out = nc.dram_tensor("out", (KD, P, SEQ), F32, kind="ExternalOutput").ap()
    hybrid_layer(nc, *aps, h_dram, out)
    result = run_bass_kernel_spmd(nc, [arrays], core_ids=[0]).results[0]["out"]
    return np.ascontiguousarray(result.reshape(D_MODEL, SEQ).T)[None]
```

```python
from contextlib import ExitStack

import numpy as np

import concourse.bass as bass
from concourse import mybir

F32 = mybir.dt.float32
F32R = mybir.dt.float32r
ALU = mybir.AluOpType
ACT = mybir.ActivationFunctionType
AX = mybir.AxisListType

P = 128
D_MODEL = 1024
SEQ = 1024
HALF = 512
KD = D_MODEL // P
NT = SEQ // P
HD = 64
GROUPS = 2
HPG = 4
N_CMP = 63
CMP_PAD = 64
N_SEL = 16
SEL_TOPN = 8
D_FF = 4096
QUARTERS = 4
FQ = D_FF // P // QUARTERS
EPS = 1e-6
NEG = -1e30
FORCED = 1e30
TAKEN = 2e30
NO_KEY = 1e25

KS_SWA, VT_SWA, KC, VC_, VT_SLC, VT_WIN, GATES, K_SLC, K_WIN = range(9)
N_KV_CHUNKS = 9
N_Q_CHUNKS = 8
N_IN = N_KV_CHUNKS + N_Q_CHUNKS
SLC, WIN, SWA = range(3)
U_OUT = 2 * N_IN
U_MLP = U_OUT + 2 * KD
N_MLP = QUARTERS * 2 * FQ
U_LAST = U_MLP + N_MLP - FQ
N_UNITS = U_LAST + 2 * FQ

C_IDENT, C_ONES = 0, P
C_TD = 2 * P
C_TW = C_TD + SEQ
C_TS = C_TW + 640
C_TC = C_TS + 256
C_FORCE = C_TC + NT * CMP_PAD
C_QS = C_FORCE + 4 * N_SEL
C_END = C_QS + N_Q_CHUNKS


def slopes():
    s = (2.0 ** (-8.0 * (np.arange(16) + 1) / 16)).astype(np.float32)
    return np.concatenate([s[0::2], s[1::2]])


def constants():
    p = np.arange(P)[:, None]
    c = np.zeros((P, C_END), np.float32)
    c[:, C_IDENT:C_IDENT + P] = np.eye(P)
    c[:, C_ONES:C_ONES + P] = 1.0

    def table(at, width, before, window):
        dist = p - (np.arange(width)[None, :] - before)
        c[:, at:at + width] = np.where((dist >= 0) & (dist < window), -dist, NEG)

    table(C_TD, SEQ, SEQ - P, SEQ)
    table(C_TW, 640, 512, 512)
    table(C_TS, 256, 128, 128)
    for i in range(NT):
        n = np.arange(CMP_PAD)[None, :]
        dist = P * i + p - (16 * n + 31)
        c[:, C_TC + i * CMP_PAD:C_TC + (i + 1) * CMP_PAD] = np.where((dist >= 0) & (n < N_CMP), -dist, NEG)
    for i in range(4, NT):
        own = 2 * i + p // 64
        j = np.arange(N_SEL)[None, :]
        forced = (j == 0) | (j == own) | (j == own - 1)
        c[:, C_FORCE + (i - 4) * N_SEL:C_FORCE + (i - 3) * N_SEL] = np.where(j > own, NEG, np.where(forced, FORCED, 0.0))
    s = slopes()
    for q in range(N_Q_CHUNKS):
        c[:HD, C_QS + q] = 0.125 / s[2 * q]
        c[HD:, C_QS + q] = 0.125 / s[2 * q + 1]
    return c


def hybrid_layer(nc, xT, w_in, w_out, w_mlp, gains, w1, w2, pe_in, sinks, consts, h_dram, out):
    SL = [float(s) for s in slopes()]
    ctx = ExitStack()
    with ctx:
        small_at = 1152
        ring_at = small_at + 4096
        qa_at = ring_at + 24576
        kv_at = qa_at + 65536
        rest_at = kv_at + 73728

        def sb(name, shape, dt, at):
            return nc.alloc_sbuf_tensor_at(name, shape, dt, offset=at)

        ident = sb("ident", [P, P], F32, small_at)
        ones = sb("ones", [P, P], F32, small_at + 512)
        gain = sb("gain", [P, 4, KD], F32, small_at + 1024)
        gate = sb("gate", [P, NT, 24], F32, small_at + 1152)
        kc_hi = sb("kc_hi", [P, GROUPS, CMP_PAD], F32R, small_at + 1920)
        kc_lo = sb("kc_lo", [P, GROUPS, CMP_PAD], F32R, small_at + 2432)
        vc = sb("vc", [CMP_PAD, GROUPS, HD], F32, small_at + 2944)
        qscale = sb("qscale", [P, N_Q_CHUNKS], F32, small_at + 3456)
        sink = sb("sink", [P, 8], F32, small_at + 3488)
        nsink = sb("nsink", [P, 8], F32, small_at + 3520)
        eps = sb("eps", [P, 1], F32, small_at + 3552)
        nmax = sb("nmax", [P, 4, HPG], F32, small_at + 3584)
        den = sb("den", [P, 4, HPG], F32, small_at + 3648)
        esink = sb("esink", [P, 4, HPG], F32, small_at + 3712)
        rgate = sb("rgate", [P, 4, HPG], F32, small_at + 3776)
        imp = sb("imp", [P, N_SEL], F32, small_at + 3840)
        score = sb("score", [P, N_SEL], F32, small_at + 3904)
        picked = sb("picked", [P, N_SEL], F32, small_at + 3968)
        top8 = sb("top8", [P, 8], F32, small_at + 4032)
        rs = sb("rs", [P, 8], F32, small_at + 4064)

        w_raw = [sb(f"w_raw{i}", [P, KD, P], F32, ring_at + 4096 * i) for i in range(2)]
        w_hi = [sb(f"w_hi{i}", [P, KD, P], F32R, ring_at + 8192 + 4096 * i) for i in range(2)]
        w_lo = [sb(f"w_lo{i}", [P, KD, P], F32R, ring_at + 16384 + 4096 * i) for i in range(2)]
        qa = sb("qa", [P, 16, SEQ], F32R, qa_at)
        k_hi = sb("k_hi", [P, 3, GROUPS, SEQ], F32R, kv_at)
        k_lo = sb("k_lo", [P, 3, GROUPS, SEQ], F32R, kv_at + 24576)
        v_hi = sb("v_hi", [P, 3, NT, P], F32R, kv_at + 49152)
        v_lo = sb("v_lo", [P, 3, NT, P], F32R, kv_at + 61440)
        x_hi = sb("x_hi", [P, KD, HALF], F32R, rest_at)
        x_lo = sb("x_lo", [P, KD, HALF], F32R, rest_at + 16384)
        x_raw = sb("x_raw", [P, 2, HALF], F32, rest_at + 32768)
        z = sb("z", [P, HALF], F32, rest_at + 36864)
        z_hi = sb("z_hi", [P, HALF], F32R, rest_at + 38912)
        sq = [sb(f"sq{i}", [P, HALF], F32, rest_at + 36864 + 2048 * i) for i in range(2)]
        zv = sb("zv", [P, 4, HALF], F32, rest_at + 40960)
        x_in = [x_raw[:, 0], x_raw[:, 1], zv[:, 2], zv[:, 3]]
        zkv = sb("zkv", [P, 2, 8, GROUPS, 64], F32, rest_at + 49152)
        rstd = sb("rstd", [P, HALF], F32, rest_at + 57344)
        xacc = sb("xacc", [P, HALF], F32, kv_at + 71680)
        w1_at = [sb(f"w1_sb{i}", [P, 8, SEQ], F32, qa_at + 32768 * (1 - i))[:, :, HALF:SEQ] for i in range(2)]
        blk_at = [sb(f"blk{i}", [P, 4, SEQ], F32, kv_at + 24576 * i)[:, :, HALF:HALF + 8 * N_CMP] for i in range(2)]
        w2_sb = sb("w2_sb", [P, 2, 2, P], F32, kv_at + 49152 + 2048)
        hid = [sb(f"hid{i}", [P, 2, 2 * N_CMP], F32, kv_at + 49152 + 6144 + 1024 * i) for i in range(2)]
        pe_sb = sb("pe_sb", [P, 2, 16], F32, kv_at + 49152 + 10240)
        wmask = sb("wmask", [P, GROUPS, SEQ], F32, ring_at)
        pt_hi = [sb(f"pt_hi{i}", [P, HALF], F32R, at) for i, at in enumerate((rest_at + 49152, rest_at + 51456, rest_at + 53888))]
        pt_lo = [sb(f"pt_lo{i}", [P, HALF], F32R, at) for i, at in enumerate((ring_at + 12288, ring_at + 14336, rest_at + 55936))]
        t_d = sb("t_d", [P, SEQ], F32, ring_at + 20480)
        t_w = sb("t_w", [P, 640], F32, ring_at + 16384)
        t_s = sb("t_s", [P, 256], F32, ring_at + 18944)
        prob = sb("prob", [P, 3, HPG, SEQ], F32, rest_at)
        t_c = sb("t_c", [P, NT, CMP_PAD], F32, ring_at + 8192)
        force = sb("force", [P, 4, N_SEL], F32, rest_at + 51200)
        pct = sb("pct", [CMP_PAD, HALF], F32, ring_at + 10240)
        pall = sb("pall", [P, CMP_PAD], F32, rest_at + 53504)
        selmask = sb("selmask", [P, GROUPS, N_SEL], F32, rest_at + 53760)
        probc = sb("probc", [P, 2, HPG * CMP_PAD], F32, rest_at + 57984)
        y = sb("y", [P, KD, SEQ], F32, kv_at)
        m_hi = sb("m_hi", [P, KD, SEQ], F32R, rest_at)
        m_lo = sb("m_lo", [P, KD, SEQ], F32R, kv_at + 32768)
        nx = sb("nx", [P, 4, HALF], F32, rest_at + 32768)
        nsq = sb("nsq", [P, 2, HALF], F32, rest_at + 40960)
        nacc = sb("nacc", [P, 2, HALF], F32, rest_at + 45056)
        hacc = sb("hacc", [P, SEQ], F32, rest_at + 49152)
        hsq = sb("hsq", [P, 3, HALF], F32, rest_at + 53248)
        u_hi = sb("u_hi", [P, FQ, SEQ], F32R, qa_at)
        u_lo = sb("u_lo", [P, FQ, SEQ], F32R, qa_at + 32768)
        yacc = sb("yacc", [P, KD, SEQ], F32, kv_at)
        uz = sb("uz", [P, 2, SEQ], F32, rest_at + 32768)
        fsq = sb("fsq", [P, 2, SEQ], F32, rest_at + 32768)
        facc = sb("facc", [P, SEQ], F32, rest_at + 53248)
        fh = sb("fh", [P, KD, SEQ], F32, rest_at)

        banks = ctx.enter_context(nc.psum_tensor("banks", [P, 2 * SEQ], F32))
        mp = [banks[:, 0:SEQ], banks[:, SEQ:2 * SEQ]]
        pts = ctx.enter_context(nc.psum_tensor("pts", [P, SEQ], F32))
        obs = ctx.enter_context(nc.psum_tensor("obs", [P, SEQ], F32))
        halves = [slice(0, HALF), slice(HALF, SEQ)]
        pt, ob = [pts[:, t] for t in halves], [obs[:, t] for t in halves]
        tp = [pt[0], pt[1], ob[0], mp[1][:, HALF:SEQ]]
        stat = ob[1]

        def sem(name):
            return ctx.enter_context(nc.semaphore(name))

        s_gain, s_const = sem("gains_loaded"), sem("consts_loaded")
        s_x = [sem(f"x_loaded{i}") for i in range(4)]
        s_xh, s_xl = sem("x_hi_ready"), sem("x_lo_ready")
        s_sq, s_xq = sem("squares_ready"), sem("squares_added")
        s_xu = sem("x_used")
        s_sum, s_std, s_diag, s_rstd = sem("sum_ready"), sem("std_ready"), sem("diagonal_ready"), sem("rstd_ready")
        s_w = [sem("w_loaded0"), sem("w_loaded1")]
        s_wh, s_wl = sem("w_hi_ready"), sem("w_lo_ready")
        s_mm, s_ev = sem("product_ready"), sem("product_taken")
        s_zh, s_za, s_zl = sem("z_hi_ready"), sem("z_copied"), sem("z_lo_written")
        s_sig, s_vt, s_vh, s_vl = sem("gates_ready"), sem("v_turned"), sem("v_hi_ready"), sem("v_lo_ready")
        s_cw, s_blk, s_hp, s_hid = sem("cmp_weights_loaded"), sem("blocks_ready"), sem("hidden_sum"), sem("hidden_ready")
        s_kcp, s_kch, s_kcl = sem("kv_cmp_sum"), sem("kc_hi_ready"), sem("kc_lo_ready")
        s_tab, s_zero = sem("tables_loaded"), sem("zeroed")
        s_S, s_sc, s_exp = sem("scores_ready"), sem("scores_taken"), sem("exp_ready")
        s_ns, s_post, s_p = sem("sink_shift_ready"), sem("scale_ready"), sem("probs_ready")
        s_dc, s_wm = sem("dve_chain"), sem("mask_ready")
        s_tr, s_hi, s_lo, s_pv = sem("probs_turned"), sem("turned_hi"), sem("turned_lo"), sem("pv_done")
        s_oh, s_oev = sem("mixed_hi"), sem("mixed_lo")
        s_y, s_nsq, s_nq = sem("y_ready"), sem("y_squares"), sem("y_squares_added")
        s_nx = [sem(f"nx_loaded{i}") for i in range(4)]
        s_t, s_h = sem("normed"), [sem("h_ready_even"), sem("h_ready_odd")]
        s_mh, s_ml, s_hs, s_ha = sem("m_hi_ready"), sem("m_lo_ready"), sem("h_squares"), sem("h_squares_added")
        s_hst, s_hq = sem("h_stored"), sem("h_squares_summed")
        s_u, s_uh, s_ul = sem("u_ready"), sem("u_hi_ready"), sem("u_lo_ready")
        s_fh, s_fs, s_fa = [sem("h_loaded0"), sem("h_loaded1")], sem("y2_squares"), sem("y2_squares_added")
        s_ft, s_fo, s_fp, s_out = (sem(n) for n in ("y2_normed", "out_ready", "out_ready_pool", "out_stored"))

        BLOCKS = [(kind, i, g) for i in range(NT) for g in range(GROUPS) for kind in ("swa", "cmp", "win", "sel")]

        def keys(kind, i):
            before = {"win": 4, "sel": NT, "swa": 1}[kind]
            first = max(0, i - before)
            return first * P, (i + 1 - first) * P

        ITEMS, STEPS = [], []
        ITEM_END, STEP_END, EXP_END, SCALED_END = [], [], [], []
        exps = scaled = 0
        for b, (kind, i, g) in enumerate(BLOCKS):
            ITEMS += [(b, h) for h in ([None] if kind == "cmp" else range(HPG))]
            STEPS += [(b, t) for t in range(1 if kind == "cmp" else keys(kind, i)[1] // P)]
            exps += HPG + (kind == "swa")
            scaled += kind != "cmp"
            ITEM_END.append(len(ITEMS))
            STEP_END.append(len(STEPS))
            EXP_END.append(exps)
            SCALED_END.append(scaled)
        NB = len(BLOCKS)

        SLOT, SLOT_BEFORE = [], []
        for b, (kind, i, g) in enumerate(BLOCKS):
            same = [c for c in range(b) if (BLOCKS[c][0] == "cmp") == (kind == "cmp")]
            n = 2 if kind == "cmp" else 3
            SLOT.append(len(same) % n)
            SLOT_BEFORE.append(same[-n] if len(same) >= n else None)

        LAST = {(kind, g): b for b, (kind, i, g) in enumerate(BLOCKS)}
        SELECTS = [(i, g) for i in range(4, NT) for g in range(GROUPS)]
        CLOSES = {STEP_END[b] - 1: b for b in range(NB) if BLOCKS[b][0] in ("sel", "swa")}
        CLOSE_NO = {t: n for n, t in enumerate(sorted(CLOSES))}

        BANK, BANK_BEFORE = [], []
        at, owner = 0, {}
        for n, (b, h) in enumerate(ITEMS):
            n_banks = 1 if h is None or keys(*BLOCKS[b][:2])[1] <= HALF else 2
            if at + n_banks > 4:
                at = 0
            BANK.append(at)
            before = [owner[c] for c in range(at, at + n_banks) if c in owner]
            BANK_BEFORE.append(max(before) if before else None)
            owner.update({c: n for c in range(at, at + n_banks)})
            at = (at + n_banks) % 4

        def n_posts(b):
            kind, i, g = BLOCKS[b]
            return (4 if i < 4 else 11) if kind == "cmp" else 2

        def plan():
            width = lambda b: CMP_PAD if BLOCKS[b][0] == "cmp" else keys(*BLOCKS[b][:2])[1]
            ITEM_B, STEP_B = [b for b, _ in ITEMS], [b for b, _ in STEPS]
            posts = [(b, k) for b in range(NB) for k in range(n_posts(b))]
            closes = sorted(CLOSES)
            lists = {
                "PE": {"weigh": range(len(STEPS)), "turn": range(len(STEPS)), "scores": range(len(ITEMS)), "project": range(KD)},
                "DVE": {"lo": range(len(STEPS)), "out_lo": closes, "post": posts, "take": range(len(ITEMS)), "w_lo": [U_OUT]},
                "ACT": {"hi": range(len(STEPS)), "out_hi": closes, "exp": range(len(ITEMS)), "w_hi": [U_OUT]},
                "SP": {"load": [U_OUT]},
                "POOL": {"scale": range(NB)},
            }
            done = {}
            engine_of = {w: e for e, ws in lists.items() for w in ws}

            def needs(what, x):
                if what == "scores":
                    return [("take", BANK_BEFORE[x])] if BANK_BEFORE[x] is not None else []
                if what == "take":
                    b, out = ITEM_B[x], [("scores", x)]
                    if SLOT_BEFORE[b] is not None:
                        out.append(("turn", STEP_END[SLOT_BEFORE[b]] - 1))
                    if b >= 4:
                        out.append(("post", (b - 4, n_posts(b - 4) - 1)))
                        out.append(("scale", b - 4))
                    if BLOCKS[b][0] == "sel" and BLOCKS[b][1] >= 4:
                        out.append(("scale", b - 2))
                    return out
                if what == "exp":
                    return [("take", x)]
                if what == "post":
                    b, k = x
                    return [("post", (b, k - 1))] if k else [("exp", ITEM_END[b] - 1)]
                if what == "scale":
                    return [("post", (x, n_posts(x) - 1))]
                if what == "turn":
                    return [("scale", STEP_B[x])] + ([("lo", x - 2)] if x >= 2 else [])
                if what == "hi":
                    return [("turn", x)] + ([("weigh", x - 3)] if x >= 3 else [])
                if what == "lo":
                    return [("hi", x)]
                if what == "weigh":
                    out = [("lo", x)]
                    n = sum(c < x for c in CLOSES)
                    if n >= 2:
                        out.append(("out_lo", closes[n - 2]))
                    return out
                if what == "load":
                    return [("take", ITEM_END[LAST["sel", 0]] - 1)]
                if what == "w_hi":
                    return [("load", x), ("weigh", STEP_END[LAST["cmp", 1]] - 1)]
                if what == "w_lo":
                    return [("w_hi", x), ("take", ITEM_END[LAST["win", 1]] - 1)]
                if what == "project":
                    return [("w_lo", U_OUT), ("take", len(ITEMS) - 1)]
                if what == "out_hi":
                    return [("weigh", x)]
                if what == "out_lo":
                    return [("out_hi", x)]

            def cost(what, x):
                if what == "scores":
                    return 450 if ITEMS[x][1] is None else 0.84 * width(ITEM_B[x]) + 10
                if what == "take":
                    return 560 if ITEMS[x][1] is None else 1.05 * width(ITEM_B[x]) + 70
                if what == "exp":
                    return 1330 if ITEMS[x][1] is None else 0.84 * width(ITEM_B[x]) + 290
                if what == "post":
                    return 150
                if what == "scale":
                    kind, i, g = BLOCKS[x]
                    return (1300 if i >= 4 else 1) if kind == "cmp" else 4 * (0.72 * width(x) + 20)
                return {"project": 640, "load": 4000, "w_hi": 950, "w_lo": 1140, "turn": 430, "weigh": 640, "hi": 480, "lo": 605, "out_hi": 900, "out_lo": 750}[what]

            order = {e: [] for e in lists}
            heads = {e: {w: 0 for w in ws} for e, ws in lists.items()}
            free = dict.fromkeys(lists, 0.0)
            left = sum(len(x) for ws in lists.values() for x in ws.values())
            while left:
                best = None
                for e, ws in lists.items():
                    for rank, (w, xs) in enumerate(ws.items()):
                        n = heads[e][w]
                        if n == len(xs):
                            continue
                        got = [done.get(d) for d in needs(w, xs[n])]
                        if None in got:
                            continue
                        start = free[e]
                        for (other, _), t in zip(needs(w, xs[n]), got):
                            start = max(start, t + (210 if "PE" in (e, engine_of[other]) else 140))
                        key = (start + (200 if w == "weigh" else 0), rank)
                        if best is None or key < best[0]:
                            best = (key, e, w, xs[n], start)
                _, e, w, x, start = best
                free[e] = start + cost(w, x)
                done[(w, x)] = free[e]
                heads[e][w] += 1
                order[e].append((w, x))
                left -= 1
            return order

        ORDER = plan()

        NORMS_WITH = {1: [0], 2: [1, 2], 3: [3], 4: [4, 5], 5: [6], 6: [7]}
        LAST_WITH = {1: [0], 2: [1, 2], 3: [3], 4: [4], 5: [5], 6: [6], 7: [7]}
        POOL_ADDS = [0, 3, 6]

        def w_slab(u):
            if u < U_OUT:
                return w_in[u % N_IN]
            return w_out[(u - U_OUT) % KD]

        block = ctx.enter_context(nc.Block())

        @block.sync
        def _(sp):
            def load_w(u):
                if u >= 2:
                    sp.wait_ge(s_wl, u - 1)
                sp.dma_start(w_raw[u % 2][:], w_slab(u)).then_inc(s_w[u % 2], 16)

            def load_x(n):
                if n >= 4:
                    sp.wait_ge(s_xl, n - 3)
                    sp.wait_ge(s_sq, n - 3)
                sp.dma_start(x_in[n % 4], xT[n % KD, :, (n // KD) * HALF:(n // KD + 1) * HALF]).then_inc(s_x[n % 4], 16)

            load_w(0)
            for n in range(4):
                load_x(n)
            load_w(1)
            for n in range(4, KD):
                load_x(n)
            for kv in range(2):
                sp.dma_start(pe_sb[:, kv, :], pe_in[kv]).then_inc(s_cw, 16)
                sp.dma_start(w2_sb[:, kv], w2[kv]).then_inc(s_cw, 16)
            for u in range(2, GATES + 7):
                load_w(u)
                if u < 10:
                    kv, part = divmod(u - 2, 4)
                    sp.dma_start(w1_at[kv][:, 2 * part:2 * part + 2, :],
                                 w1[kv][:, 4 * part:4 * part + 4, :].rearrange("p (s i) h -> p s (i h)", i=2)).then_inc(s_cw, 16)
            sp.wait_ge(s_vt, 4)
            for n in range(KD, KD + 4):
                load_x(n)
            for u in range(GATES + 7, N_IN + 2):
                load_w(u)
            for n in range(KD + 4, 2 * KD):
                load_x(n)
            for u in range(N_IN + 2, U_OUT):
                load_w(u)

            sp.wait_ge(s_blk, 4)
            sp.dma_start(force[:], consts[:, C_FORCE:C_QS]).then_inc(s_tab, 16)
            sp.wait_ge(s_mm, U_OUT - 1)
            for dst, at, n in ((t_s, C_TS, 256), (t_c, C_TC, NT * CMP_PAD), (t_w, C_TW, 640)):
                sp.dma_start(dst[:], consts[:, at:at + n]).then_inc(s_tab, 16)
            sp.wait_ge(s_mm, U_OUT)
            sp.dma_start(t_d[:], consts[:, C_TD:C_TD + SEQ]).then_inc(s_tab, 16)

            for g in range(GROUPS):
                sp.wait_ge(s_sc, ITEM_END[LAST["sel", g]])
                load_w(U_OUT + g)
            sp.wait_ge(s_tr, len(STEPS))
            for n in range(4):
                sp.dma_start(nx[:, n, :], xT[n, :, 0:HALF]).then_inc(s_nx[n], 16)
            for u in range(U_OUT + 2, U_MLP):
                load_w(u)

            def load_mlp(u, par):
                sp.wait_ge(s_wl, u - 1)
                slab = w_mlp[bass.ds(u - U_MLP, 1)].rearrange("a p k c -> p (a k) c")
                sp.dma_start(w_raw[par][:], slab).then_inc(s_w[par], 16)

            load_mlp(U_MLP, 0)
            load_mlp(U_MLP + 1, 1)
            with sp.Fori(1, N_MLP // 2) as j:
                for par in range(2):
                    load_mlp(2 * j + (U_MLP + par), par)

            for u in range(U_MLP + N_MLP, N_UNITS):
                sp.wait_ge(s_wl, u - 1)
                sp.dma_start(w_raw[u % 2][:], w_mlp[u - U_MLP - FQ]).then_inc(s_w[u % 2], 16)

            for n in range(2 * KD):
                c, hf = n % KD, n // KD
                if hf == 0 or c in POOL_ADDS:
                    sp.wait_ge(s_fp, c + 1 if hf == 0 else KD + POOL_ADDS.index(c) + 1)
                else:
                    sp.wait_ge(s_fo, c - sum(p < c for p in POOL_ADDS) + 1)
                sp.dma_start(out[c, :, halves[hf]], yacc[:, c, halves[hf]]).then_inc(s_out, 16)
            sp.wait_ge(s_out, 16 * 2 * KD)

        @block.tensor
        def _(pe):
            def row_sums(dst, acc):
                for t in range(4):
                    last = pe.matmul(dst[:, t:t + 1], acc[:, t * P:(t + 1) * P], ones[:, 0:1], start=True, stop=True)
                last.then_inc(s_sum, 1)

            def spread(n, dst, diag):
                pe.wait_ge(s_diag, n + 1)
                pe.matmul(dst, ones[:], diag, start=True, stop=True).then_inc(s_rstd, 1)

            def unit(u, par, out_at, hi, lo, before_k=None, used=None):
                pe.wait_ge(s_wl, u + 1)
                if not isinstance(u, int) or u >= 2:
                    pe.wait_ge(s_ev, u - 1)
                for k in range(KD):
                    if before_k:
                        before_k(k)
                    for dst, a, b in zip(out_at, hi, lo):
                        pe.matmul(dst, w_hi[par][:, k, :], a(k), start=(k == 0), stop=False)
                        pe.matmul(dst, w_hi[par][:, k, :], b(k), start=False, stop=False)
                    for dst, a in zip(out_at, hi):
                        last = pe.matmul(dst, w_lo[par][:, k, :], a(k), start=False, stop=(k == KD - 1))
                    if used and k < KD - 1:
                        last.then_inc(used, 1)
                last.then_inc(s_mm, 1)

            def hidden(kv):
                pe.wait_ge(s_cw, 16 * 12)
                pe.wait_ge(s_blk, 2 * kv + 2)
                for hh in range(2):
                    for pp in range(16):
                        w_at, b_at = 256 * (pp % 2) + hh * P, 2 * N_CMP * (pp % 4)
                        last = pe.matmul(pt[kv][:, hh * P:hh * P + 2 * N_CMP], w1_at[kv][:, pp // 2, w_at:w_at + P],
                                         blk_at[kv][:, pp // 4, b_at:b_at + 2 * N_CMP], start=(pp == 0), stop=(pp == 15))
                last.then_inc(s_hp, 1)

            def compressed():
                pe.wait_ge(s_hid, 1)
                for hh in range(2):
                    last = pe.matmul(ob[0][:, 0:2 * N_CMP], w2_sb[:, 0, hh, :], hid[0][:, hh, :], start=(hh == 0), stop=(hh == 1))
                last.then_inc(s_kcp, 1)
                pe.wait_ge(s_hid, 2)
                for g in range(GROUPS):
                    for hh in range(2):
                        last = pe.matmul(ob[1][0:N_CMP, g * HD:(g + 1) * HD], hid[1][:, hh, g * N_CMP:(g + 1) * N_CMP],
                                         w2_sb[:, 1, hh, 0:HD], start=(hh == 0), stop=(hh == 1))
                last.then_inc(s_kcp, 1)

            for hf in range(2):
                for j in range(N_IN):
                    u = hf * N_IN + j

                    def before(k):
                        if j == 0:
                            pe.wait_ge(s_xl, hf * KD + k + 1)
                        if j == 1 and k == 2:
                            pe.wait_ge(s_const, 16 * 4)
                            pe.wait_ge(s_xq, KD * (hf + 1))
                            row_sums(ob[0], xacc)
                        if j == 1 and k == KD - 1:
                            spread(hf, stat, xacc[:])
                    unit(u, u % 2, [mp[u % 2][:, 0:HALF]], [lambda k: x_hi[:, k, :]], [lambda k: x_lo[:, k, :]],
                         before, s_xu if u == N_IN - 1 else None)
                    if hf and j in (5, 6):
                        hidden(j - 5)
                    if hf and j == 7:
                        compressed()
                    if j == GATES + 2:
                        pe.wait_ge(s_ev, hf * N_IN + GATES + 1)
                        pe.wait_ge(s_sig, hf + 1)
                        if hf:
                            pe.wait_ge(s_vl, 4)
                            pe.wait_ge(s_kcl, 1)
                        for v in range(4):
                            for t in range(4):
                                last = pe.transpose(tp[v][:, t * P:(t + 1) * P], zv[:, v, t * P:(t + 1) * P], ident[:])
                            last.then_inc(s_vt, 1)

            pe.wait_ge(s_ev, U_OUT)
            pe.wait_ge(s_za, 22)
            pe.wait_ge(s_zl, 22)
            pe.wait_ge(s_vl, 8)

            def scores(n):
                b, h = ITEMS[n]
                kind, i, g = BLOCKS[b]
                if BANK_BEFORE[n] is not None:
                    pe.wait_ge(s_sc, BANK_BEFORE[n] + 1)
                dst = banks[:, BANK[n] * HALF:BANK[n] * HALF + max(HALF, 0 if h is None else keys(kind, i)[1])]
                toks = slice(i * P, (i + 1) * P)
                if kind == "cmp":
                    for r in range(HPG):
                        q = qa[:, g * HPG + r, toks]
                        at = dst[:, r * CMP_PAD:(r + 1) * CMP_PAD]
                        pe.matmul(at, q, kc_hi[:, g, :], start=True, stop=False)
                        last = pe.matmul(at, q, kc_lo[:, g, :], start=False, stop=True)
                else:
                    typ = {"win": WIN, "sel": SLC, "swa": SWA}[kind]
                    q = qa[:, (8 if kind == "swa" else 0) + g * HPG + h, toks]
                    first, width = keys(kind, i)
                    for at in range(0, width, HALF):
                        w = min(HALF, width - at)
                        ks = slice(first + at, first + at + w)
                        pe.matmul(dst[:, at:at + w], q, k_hi[:, typ, g, ks], start=True, stop=False)
                        last = pe.matmul(dst[:, at:at + w], q, k_lo[:, typ, g, ks], start=False, stop=True)
                last.then_inc(s_S, 1)

            def turn(t):
                b, kt = STEPS[t]
                kind, i, g = BLOCKS[b]
                if kind == "cmp":
                    pe.wait_ge(s_post, b + 1)
                else:
                    pe.wait_ge(s_p, SCALED_END[b])
                if t >= 2:
                    pe.wait_ge(s_lo, t - 1)
                for r in range(HPG):
                    if kind == "cmp":
                        last = pe.transpose(pt[t % 2][0:CMP_PAD, r * P:(r + 1) * P],
                                            probc[:, SLOT[b], r * CMP_PAD:(r + 1) * CMP_PAD], ident[:])
                    else:
                        last = pe.transpose(pt[t % 2][:, r * P:(r + 1) * P], prob[:, SLOT[b], r, kt * P:(kt + 1) * P], ident[:])
                last.then_inc(s_tr, 1)

            def weigh(t):
                b, kt = STEPS[t]
                kind, i, g = BLOCKS[b]
                dst = ob[kind == "swa"][0:HD, :]
                opens = kind == "cmp" or (kind == "swa" and kt == 0)
                if opens:
                    n = sum(c < t for c in CLOSES)
                    if n >= 2:
                        pe.wait_ge(s_oev, 2 * (n - 1))
                pe.wait_ge(s_lo, t + 1)
                if kind == "cmp":
                    last = pe.matmul(dst, vc[:, g, :], pct[:], start=True, stop=False)
                else:
                    typ = {"win": WIN, "sel": SLC, "swa": SWA}[kind]
                    first, width = keys(kind, i)
                    tile = first // P + kt
                    vh, vl = (v[:, typ, tile, g * HD:(g + 1) * HD] for v in (v_hi, v_lo))
                    end = t in CLOSES
                    pe.matmul(dst, vh, pt_hi[t % 3][:], start=opens, stop=False)
                    pe.matmul(dst, vl, pt_hi[t % 3][:], start=False, stop=False)
                    last = pe.matmul(dst, vh, pt_lo[t % 3][:], start=False, stop=end)
                last.then_inc(s_pv, 1)

            def project(k):
                if k == 0:
                    pe.wait_ge(s_wl, U_OUT + 1)
                    pe.wait_ge(s_sc, len(ITEMS))
                    pe.wait_ge(s_oev, 2 * len(CLOSES) // 2)
                dst, toks = mp[0][:, 0:HALF], halves[0]
                pe.matmul(dst, w_hi[0][:, k, :], qa[:, 2 * k, toks], start=(k == 0), stop=False)
                pe.matmul(dst, w_hi[0][:, k, :], qa[:, 2 * k + 1, toks], start=False, stop=False)
                last = pe.matmul(dst, w_lo[0][:, k, :], qa[:, 2 * k, toks], start=False, stop=(k == KD - 1))
                if k == KD - 1:
                    last.then_inc(s_mm, 1)

            for what, n in ORDER["PE"]:
                {"scores": scores, "turn": turn, "weigh": weigh, "project": project}[what](n)

            for hf in range(2):
                toks = slice(hf * HALF, (hf + 1) * HALF)
                if hf:
                    pe.wait_ge(s_oev, 2 * len(CLOSES))
                for c in range(KD):
                    u = U_OUT + hf * KD + c
                    if u == U_OUT:
                        continue

                    def before(k):
                        if hf == 1 and c == 0 and k == 3:
                            pe.wait_ge(s_nq, KD)
                            row_sums(pt[0], nacc[:, 0, :])
                        if hf == 1 and c == 0 and k == KD - 1:
                            spread(2, ob[0], nacc[:, 0, :])
                    unit(u, u % 2, [mp[u % 2][:, 0:HALF]], [lambda k: qa[:, 2 * k, toks]], [lambda k: qa[:, 2 * k + 1, toks]], before)

            def up(u, par, before_k=None):
                unit(u, par, [mp[par][:, t] for t in halves], [(lambda k, t=t: m_hi[:, k, t]) for t in halves],
                     [(lambda k, t=t: m_lo[:, k, t]) for t in halves], before_k)

            def down(u, par, q):
                def before(k):
                    if par == 0 and k in (0, KD - 1):
                        pe.wait_ge(s_ul, q * FQ + (FQ - 1 if k == 0 else FQ))
                unit(u, par, [mp[par][:, t] for t in halves], [(lambda k, t=t: u_hi[:, k, t]) for t in halves],
                     [(lambda k, t=t: u_lo[:, k, t]) for t in halves], before)

            def add_row_sums(c):
                pe.wait_ge(s_hs, KD + c + 1)
                for t in range(4):
                    last = pe.matmul(pt[1][:, 8 + t:9 + t], hsq[:, (KD + c) % 3, t * P:(t + 1) * P], ones[:, 0:1],
                                     start=(c == 0 and t == 0), stop=(c == KD - 1 and t == 3))
                last.then_inc(s_sum if c == KD - 1 else s_hq, 1)

            for hf in range(2):
                for par in range(2):
                    u = U_MLP + par
                    if hf == 0:
                        pe.wait_ge(s_wl, u + 1)
                        pe.wait_ge(s_ev, u - 1)
                    for k in range(KD):
                        if par == 0:
                            pe.wait_ge(s_ml, hf * KD + k + 1)
                        if (hf, par, k) == (0, 0, 2):
                            pe.wait_ge(s_nq, 2 * KD)
                            row_sums(pt[1], nacc[:, 1, :])
                        if (hf, par, k) == (0, 0, KD - 1):
                            spread(3, ob[1], nacc[:, 1, :])
                        if (hf, par, k) == (0, 1, 2):
                            pe.wait_ge(s_ha, KD)
                            row_sums(pt[0][:, 8:12], hacc[:, 0:HALF])
                        if (hf, par, k) == (1, 0, KD - 1):
                            spread(4, pt[0], hacc[:, halves[0]])
                        if (hf, par, k) == (1, 1, 3):
                            spread(5, pt[1], hacc[:, halves[1]])
                        dst, a, b = mp[par][:, halves[hf]], m_hi[:, k, halves[hf]], m_lo[:, k, halves[hf]]
                        pe.matmul(dst, w_hi[par][:, k, :], a, start=(k == 0), stop=False)
                        pe.matmul(dst, w_hi[par][:, k, :], b, start=False, stop=False)
                        last = pe.matmul(dst, w_lo[par][:, k, :], a, start=False, stop=(k == KD - 1))
                        if (hf, par) == (1, 0) and k:
                            add_row_sums(k - 1)
                    if hf == 1:
                        last.then_inc(s_mm, 1)
                    if (hf, par) == (1, 0):
                        add_row_sums(KD - 1)
            with pe.Fori(1, FQ // 2) as j:
                for par in range(2):
                    up(2 * j + (U_MLP + par), par)
            with pe.Fori(0, FQ // 2) as j:
                for par in range(2):
                    down(2 * j + (U_MLP + FQ + par), par, 0)
            def quarter(q, last):
                with pe.Fori(0, FQ // 2) as j:
                    for par in range(2):
                        up(q * (2 * FQ) + 2 * j + (U_MLP + par), par)
                if not last:
                    with pe.Fori(0, FQ // 2) as j:
                        for par in range(2):
                            down(q * (2 * FQ) + 2 * j + (U_MLP + FQ + par), par, q)

            with pe.Fori(1, QUARTERS - 1) as q:
                quarter(q, False)
            quarter(QUARTERS - 1, True)

            def last_sums(src, start, stop):
                for t in range(4):
                    last = pe.matmul(ob[1][:, t:t + 1], src[:, t * P:(t + 1) * P], ones[:, 0:1], start=start and t == 0,
                                     stop=stop and t == 3)
                return last

            for n in range(2 * KD):
                def before(k):
                    if n == 0 and k in (0, KD - 1):
                        pe.wait_ge(s_ul, QUARTERS * FQ - (k == 0))
                    if n == KD and k == 5:
                        pe.wait_ge(s_fa, KD)
                        row_sums(ob[0], facc[:, halves[0]])
                    if n == KD and k == KD - 1:
                        spread(6, pt[0], facc[:, halves[0]])
                    if n == 2 * KD - 1 and k == KD - 1:
                        pe.wait_ge(s_fa, 2 * KD - 1)
                        last_sums(facc[:, halves[1]], True, False)
                u, toks = U_LAST + n, halves[n // KD]
                unit(u, u % 2, [mp[u % 2][:, toks]], [lambda k: u_hi[:, k, toks]], [lambda k: u_lo[:, k, toks]], before)
            pe.wait_ge(s_fs, 2 * KD)
            last_sums(fsq[:, 1, 0:HALF], False, True).then_inc(s_sum, 1)
            spread(7, pt[1], facc[:, halves[1]])

        @block.scalar
        def _(act):
            copy = lambda dst, src, **kw: act.activation(dst, src, ACT.Copy, **kw)

            def split_w(u, par=None):
                if par is None:
                    par = u % 2
                act.wait_ge(s_w[par], 8 * u + (16 - 8 * par))
                if not isinstance(u, int) or u >= 2:
                    act.wait_ge(s_mm, u - 1)
                copy(w_hi[par][:], w_raw[par][:]).then_inc(s_wh, 1)

            def std(n, src):
                act.wait_ge(s_sum, n + 1)
                at = 4 * (n % 2)
                act.activation(rs[:, at:at + 4], src[:, 0:4], ACT.Sqrt, bias=eps[:, 0:1], scale=1.0 / D_MODEL).then_inc(s_std, 1)

            act.dma_start(gain[:], gains).then_inc(s_gain, 16)
            for dst, at, n in ((ident, C_IDENT, P), (ones, C_ONES, P), (qscale, C_QS, N_Q_CHUNKS)):
                act.dma_start(dst[:], consts[:, at:at + n]).then_inc(s_const, 16)
            act.dma_start(sink[:], sinks).then_inc(s_const, 16)
            act.wait_ge(s_gain, 16)
            act.wait_ge(s_zero, 1)
            zn = [0]
            def convert_x(hf):
                for k in range(KD):
                    n = hf * KD + k
                    act.wait_ge(s_x[n % 4], 16 * (n // 4 + 1))
                    if hf:
                        act.wait_ge(*((s_xu, k + 1) if k < KD - 1 else (s_mm, N_IN)))
                    copy(x_hi[:, k, :], x_in[n % 4], scale=gain[:, 0, k:k + 1]).then_inc(s_xh, 1)
                    if n >= 2:
                        act.wait_ge(s_xq, n - 1)
                    if k < 2 and hf:
                        act.wait_ge(s_zl, zn[0])
                        act.wait_ge(s_za, zn[0])
                    act.activation(sq[n % 2][:], x_in[n % 4], ACT.Square).then_inc(s_sq, 1)
                    if n == 3:
                        split_w(1)

            def project(hf, j):
                u = hf * N_IN + j
                if hf and j in (6, 7):
                    kv = j - 6
                    act.wait_ge(s_hp, kv + 1)
                    src = pt[kv][:, 0:2 * P].rearrange("p (h n) -> p h n", h=2)[:, :, 0:2 * N_CMP]
                    act.activation(hid[kv][:], src, ACT.Gelu_apprx_tanh).then_inc(s_hid, 1)
                if hf and j == 8:
                    act.wait_ge(s_kcp, 1)
                    copy(kc_hi[:, :, 0:N_CMP], ob[0][:, 0:2 * N_CMP].rearrange("p (g n) -> p g n", g=2)).then_inc(s_kch, 1)
                if u + 2 < U_OUT:
                    split_w(u + 2)
                if j == GATES:
                    act.wait_ge(s_ev, u + 1)
                    act.activation(zv[:, 3, :], zv[:, 3, :], ACT.Sigmoid).then_inc(s_sig, 1)
                if j == GATES + 3:
                    for v in range(3):
                        act.wait_ge(s_vt, 4 * hf + v + 1)
                        copy(v_hi[:, [SWA, SLC, WIN][v], 4 * hf:4 * hf + 4, :], tp[v]).then_inc(s_vh, 1)
                is_k = j in (KS_SWA, K_SLC, K_WIN)
                if is_k or j >= N_KV_CHUNKS:
                    toks = slice(hf * HALF, (hf + 1) * HALF)
                    act.wait_ge(s_ev, u + 1)
                    if zn[0]:
                        act.wait_ge(s_zl, zn[0])
                    copy(z_hi[:], z[:]).then_inc(s_zh, 1)
                    for g in range(2):
                        src = z[g * HD:(g + 1) * HD, :]
                        if is_k:
                            typ = {KS_SWA: SWA, K_SLC: SLC, K_WIN: WIN}[j]
                            copy(k_hi[0:HD, typ, g, toks], src)
                            last = copy(k_hi[HD:P, typ, g, toks], src)
                        else:
                            last = copy(qa[0:HD, 2 * (j - N_KV_CHUNKS) + g, toks], src)
                    last.then_inc(s_za, 1)
                    zn[0] += 1


            split_w(0)
            convert_x(0)
            std(0, ob[0])
            for j in range(N_IN - 1):
                project(0, j)
            convert_x(1)
            project(0, N_IN - 1)
            std(1, ob[0])
            for j in range(N_IN):
                project(1, j)

            def exp_item(n):
                b, h = ITEMS[n]
                kind, i, g = BLOCKS[b]
                base = g * HPG + (8 if kind == "swa" else 0)
                act.wait_ge(s_sc, n + 1)
                for r in (range(HPG) if h is None else [h]):
                    if h is None:
                        p = probc[:, SLOT[b], r * CMP_PAD:(r + 1) * CMP_PAD]
                    else:
                        p = prob[:, SLOT[b], r, 0:keys(kind, i)[1]]
                    act.activation(p, p, ACT.Exp, bias=nmax[:, b % 4, r:r + 1], scale=-1.0,
                                   accum_out=den[:, b % 4, r:r + 1]).then_inc(s_exp, 1)
                if kind == "swa" and h == HPG - 1:
                    act.wait_ge(s_ns, i * GROUPS + g + 1)
                    act.activation(esink[:, b % 4, :], esink[:, b % 4, :], ACT.Exp).then_inc(s_exp, 1)

            def turned_hi(t):
                b, kt = STEPS[t]
                act.wait_ge(s_tr, t + 1)
                if t >= 3:
                    act.wait_ge(s_pv, t - 2)
                if BLOCKS[b][0] == "cmp":
                    if b >= 4:
                        act.wait_ge(s_pv, STEP_END[b - 4])
                    copy(pct[:, 0:256], pt[t % 2][0:CMP_PAD, 0:256]).then_inc(s_hi, 1)
                else:
                    copy(pt_hi[t % 3][:], pt[t % 2]).then_inc(s_hi, 1)

            def mixed_hi(t):
                kind, i, g = BLOCKS[STEPS[t][0]]
                act.wait_ge(s_pv, t + 1)
                h0 = (8 if kind == "swa" else 0) + g * HPG
                src = ob[kind == "swa"][0:HD, :].rearrange("p (c e q) -> p e c q", c=2, e=2)
                for e in range(2):
                    copy(qa[e * HD:(e + 1) * HD, h0:h0 + HPG:2, i * P:(i + 1) * P], src[:, e]).then_inc(s_oh, 1)

            def first_slab(u):
                act.wait_ge(s_pv, STEP_END[LAST["cmp", 1]])
                act.wait_ge(s_sc, ITEM_END[LAST["cmp", 1]])
                split_w(u)

            for what, n in ORDER["ACT"]:
                {"exp": exp_item, "hi": turned_hi, "out_hi": mixed_hi, "w_hi": first_slab}[what](n)

            def norm_act(n):
                c, hf = n % KD, n // KD
                h = y[:, c, halves[hf]]
                act.wait_ge(*((s_h[0], n // 2 + 1) if n in (0, 2, 4, 6) else (s_h[1], n // 2 + 1 if n < KD else n - 3)))
                copy(m_hi[:, c, halves[hf]], h, scale=gain[:, 2, c:c + 1]).then_inc(s_mh, 1)
                act.dma_start(h_dram[c, :, halves[hf]], h).then_inc(s_hst, 16)
                if n + 4 < 2 * KD:
                    c4, hf4 = (n + 4) % KD, (n + 4) // KD
                    act.dma_start(nx[:, n % 4, :], xT[c4, :, halves[hf4]]).then_inc(s_nx[n % 4], 16)

            def square_h(n):
                c, hf = n % KD, n // KD
                if n >= KD + 3:
                    act.wait_ge(s_hq, n - KD - 2)
                elif n >= 3:
                    act.wait_ge(s_ha, n - 2)
                act.activation(hsq[:, n % 3, :], y[:, c, halves[hf]], ACT.Square).then_inc(s_hs, 1)

            act.wait_ge(s_lo, len(STEPS))
            split_w(U_OUT + 1)
            for n in range(2 * KD):
                c, hf = n % KD, n // KD
                u = U_OUT + n
                act.wait_ge(s_mm, u + 1)
                if n >= 2:
                    act.wait_ge(s_nq, n - 1)
                if c < KD - 1:
                    split_w(u + 2)
                act.activation(nsq[:, n % 2, :], mp[u % 2][:, 0:HALF], ACT.Square).then_inc(s_y, 1)
                copy(y[:, c, halves[hf]], mp[u % 2][:, 0:HALF]).then_inc(s_ev, 1)
                if c == KD - 1:
                    split_w(u + 2)
                if n == KD - 1:
                    std(2, pt[0])
                for m in NORMS_WITH.get(n - 1 - KD, []):
                    norm_act(m)
                    square_h(m)
            std(3, pt[1])
            for n in range(KD, 2 * KD):
                norm_act(n)
                if n >= KD + 3:
                    square_h(n - 3)
                if n == KD + 4:
                    std(4, pt[0][:, 8:12])
            for n in range(2 * KD - 3, 2 * KD):
                square_h(n)

            def up_act(u, par, f, done):
                split_w(u + 2, par)
                act.wait_ge(s_u, done)
                copy(u_hi[:, bass.ds(f, 1), :].rearrange("p a t -> p (a t)"), uz[:, par, :]).then_inc(s_uh, 1)

            def quarter(q, last):
                u0 = q * (2 * FQ) + U_MLP
                with act.Fori(0, FQ // 2) as j:
                    for par in range(2):
                        f = 2 * j + par
                        up_act(u0 + f, par, f, q * FQ + f + 1)
                if not last:
                    with act.Fori(0, FQ // 2) as j:
                        for par in range(2):
                            split_w(u0 + 2 * j + (FQ + par + 2), par)

            std(5, pt[1][:, 8:12])
            quarter(0, False)
            with act.Fori(1, QUARTERS - 1) as q:
                quarter(q, False)
            quarter(QUARTERS - 1, True)

            act.wait_ge(s_hst, 16 * 2 * KD)
            act.wait_ge(s_ul, QUARTERS * FQ)
            for n in range(2 * KD):
                c, u, toks = n % KD, U_LAST + n, halves[n // KD]
                act.wait_ge(s_mm, u + 1)
                act.dma_start(fh[:, c, toks], h_dram[c, :, toks]).then_inc(s_fh[n // KD], 16)
                if u + 2 < N_UNITS:
                    split_w(u + 2)
                act.wait_ge(s_ev, u + 1)
                if n >= 2:
                    act.wait_ge(s_fa, n - 1)
                act.activation(fsq[:, n % 2, 0:HALF], yacc[:, c, toks], ACT.Square).then_inc(s_fs, 1)
                if n == KD - 1:
                    std(6, ob[0])
            std(7, ob[1])

        @block.vector
        def _(dve):
            TT, STT, TS = dve.tensor_tensor, dve.scalar_tensor_tensor, dve.tensor_scalar
            f32 = lambda ap: ap.bitcast(F32)
            chain = [0]

            def link(ins):
                ins.then_inc(s_dc, 1)
                chain[0] += 1
                dve.wait_ge(s_dc, chain[0])

            def diagonal(n, dst):
                at = 4 * (n % 2)
                dve.wait_ge(s_std, n + 1)
                link(dve.reciprocal(rs[:, at:at + 4], rs[:, at:at + 4]))
                TT(dst.rearrange("p (t q) -> p t q", t=4), ident[:].unsqueeze(1).to_broadcast([P, 4, P]),
                   rs[:, at:at + 4].unsqueeze(2).to_broadcast([P, 4, P]), ALU.mult).then_inc(s_diag, 1)

            def split_w(u, par=None):
                if par is None:
                    par = u % 2
                dve.wait_ge(s_wh, u + 1)
                TT(w_lo[par][:], w_raw[par][:], f32(w_hi[par][:]), ALU.subtract).then_inc(s_wl, 1)

            dve.memset(eps[:], EPS)
            dve.memset(f32(kc_hi[:]), 0.0)
            dve.memset(f32(kc_lo[:]), 0.0)
            dve.memset(vc[:], 0.0).then_inc(s_zero, 1)
            dve.wait_ge(s_gain, 16)

            zn = [0]

            def convert_x(hf):
                for k in range(KD):
                    n = hf * KD + k
                    dve.wait_ge(s_xh, n + 1)
                    STT(x_lo[:, k, :], x_in[n % 4], gain[:, 0, k:k + 1], f32(x_hi[:, k, :]), ALU.mult,
                        ALU.subtract).then_inc(s_xl, 1)
                    dve.wait_ge(s_sq, n + 1)
                    if k:
                        dve.wait_ge(s_xq, n)
                        TT(xacc[:], xacc[:], sq[n % 2][:], ALU.add).then_inc(s_xq, 1)
                    else:
                        dve.tensor_copy(xacc[:], sq[n % 2][:]).then_inc(s_xq, 1)
                    if n == 3:
                        split_w(1)

            def blocks(kv):
                dve.wait_ge(s_cw, 16 * 12)
                dve.wait_ge(s_ev, N_IN + (VC_ if kv else KC) + 1)
                for c in range(4):
                    late, q = c // 2, c % 2 * 4
                    dst = blk_at[kv][:, c, :].rearrange("p (q g n) -> p q g n", q=4, g=GROUPS)
                    src = zkv[:, kv, q:q + 4, :, late:late + N_CMP]
                    emb = pe_sb[:, kv, 4 * c:4 * c + 4].unsqueeze(2).unsqueeze(3).to_broadcast([P, 4, GROUPS, N_CMP])
                    last = TT(dst, src, emb, ALU.add)
                    if c % 2:
                        last.then_inc(s_blk, 1)

            def project(hf, j):
                u = hf * N_IN + j
                if hf and j == 8:
                    dve.wait_ge(s_kch, 1)
                    TT(kc_lo[:, :, 0:N_CMP], ob[0][:, 0:2 * N_CMP].rearrange("p (g n) -> p g n", g=2),
                       f32(kc_hi[:, :, 0:N_CMP]), ALU.subtract)
                    dve.wait_ge(s_kcp, 2)
                    dve.tensor_copy(vc[0:N_CMP, :, :], ob[1][0:N_CMP, 0:P].rearrange("p (g n) -> p g n", g=2)).then_inc(s_kcl, 1)
                if u + 2 < U_OUT:
                    split_w(u + 2)
                if hf and j in (KC + 1, VC_ + 1):
                    blocks(j - KC - 1)
                if j == 0:
                    dve.wait_ge(s_rstd, hf + 1)
                    link(dve.tensor_copy(rstd[:], stat))
                dve.wait_ge(s_mm, u + 1)
                src = mp[u % 2][:, 0:HALF]
                toks = slice(hf * HALF, (hf + 1) * HALF)
                if j in (VT_SWA, VT_SLC, VT_WIN, GATES):
                    v = {VT_SWA: 0, VT_SLC: 1, VT_WIN: 2, GATES: 3}[j]
                    if hf:
                        dve.wait_ge(s_vt, 4)
                    TT(zv[:, v, :], src, rstd[:], ALU.mult).then_inc(s_ev, 1)
                elif j in (KC, VC_):
                    kv = int(j == VC_)
                    for g in range(GROUPS):
                        rows = slice(g * HD, (g + 1) * HD)
                        a = src[rows, :].rearrange("p (n q e) -> p e q n", q=8, e=2)
                        b = rstd[rows, :].rearrange("p (n q e) -> p e q n", q=8, e=2)
                        for e in range(2):
                            last = TT(zkv[e * HD:(e + 1) * HD, kv, :, g, hf * 32:hf * 32 + 32], a[:, e], b[:, e], ALU.mult)
                    last.then_inc(s_ev, 1)
                else:
                    if zn[0]:
                        dve.wait_ge(s_za, zn[0])
                        dve.wait_ge(s_zl, zn[0])
                    if j < N_KV_CHUNKS:
                        TT(z[:], src, rstd[:], ALU.mult).then_inc(s_ev, 1)
                    else:
                        c = j - N_KV_CHUNKS
                        STT(z[:], src, qscale[:, c:c + 1], rstd[:], ALU.mult, ALU.mult).then_inc(s_ev, 1)
                    dve.wait_ge(s_ev, u + 1)
                    dve.wait_ge(s_zh, zn[0] + 1)
                    for g in range(2):
                        rows = slice(g * HD, (g + 1) * HD)
                        if j < N_KV_CHUNKS:
                            typ = {KS_SWA: SWA, K_SLC: SLC, K_WIN: WIN}[j]
                            TT(k_lo[0:HD, typ, g, toks], z[rows, :], f32(z_hi[rows, :]), ALU.subtract)
                            last = TT(k_lo[HD:P, typ, g, toks], z[rows, :], f32(z_hi[rows, :]), ALU.subtract)
                        else:
                            last = TT(qa[HD:P, 2 * (j - N_KV_CHUNKS) + g, toks], z[rows, :], f32(z_hi[rows, :]), ALU.subtract)
                    last.then_inc(s_zl, 1)
                    zn[0] += 1
                if j == GATES + 3:
                    for v in range(3):
                        dve.wait_ge(s_vh, 3 * hf + v + 1)
                        at = (slice(None), [SWA, SLC, WIN][v], slice(4 * hf, 4 * hf + 4), slice(None))
                        TT(v_lo[at], tp[v].rearrange("p (t c) -> p t c", t=4), f32(v_hi[at]), ALU.subtract).then_inc(s_vl, 1)
                    dve.wait_ge(s_vt, 4 * hf + 4)
                    dve.tensor_copy(gate[:, 4 * hf:4 * hf + 4, :],
                                    tp[3].rearrange("p (t c) -> p t c", t=4)[:, :, 0:24]).then_inc(s_vl, 1)

            split_w(0)
            convert_x(0)
            dve.wait_ge(s_const, 16 * 4)
            link(TS(nsink[:], sink[:], -1.0, None, ALU.mult))
            diagonal(0, xacc[:])
            for j in range(N_IN - 1):
                project(0, j)
            convert_x(1)
            project(0, N_IN - 1)
            diagonal(1, xacc[:])
            for j in range(N_IN):
                project(1, j)

            dve.wait_ge(s_tab, 16 * 5)

            def score_item(n):
                b, h = ITEMS[n]
                kind, i, g = BLOCKS[b]
                dve.wait_ge(s_S, n + 1)
                if SLOT_BEFORE[b] is not None:
                    dve.wait_ge(s_tr, STEP_END[SLOT_BEFORE[b]])
                for r in (range(HPG) if h is None else [h]):
                    if kind == "cmp":
                        src = banks[:, BANK[n] * HALF + r * CMP_PAD:BANK[n] * HALF + (r + 1) * CMP_PAD]
                        dst = probc[:, SLOT[b], r * CMP_PAD:(r + 1) * CMP_PAD]
                        table, head, floor = t_c[:, i, :], g * HPG + r, NO_KEY
                    else:
                        first, width = keys(kind, i)
                        src, dst = banks[:, BANK[n] * HALF:BANK[n] * HALF + width], prob[:, SLOT[b], r, 0:width]
                        head, floor = g * HPG + r, 3e38
                        if kind == "swa":
                            table, head, floor = t_s[:, 256 - width:256], 8 + head, nsink[:, g * HPG + r:g * HPG + r + 1]
                        elif kind == "win":
                            table = t_w[:, 640 - width:640]
                        elif i < 4:
                            table = t_d[:, SEQ - width:SEQ]
                        else:
                            dve.wait_ge(s_wm, SELECTS.index((i, g)) + 1)
                            table = wmask[:, g, 0:width]
                    last = dve.tensor_tensor_reduce(dst, src, table, -SL[head], floor, ALU.add, ALU.min, nmax[:, b % 4, r:r + 1])
                last.then_inc(s_sc, 1)
                if kind == "swa" and h == HPG - 1:
                    dve.wait_ge(s_sc, n + 1)
                    TT(esink[:, b % 4, :], nmax[:, b % 4, :], sink[:, g * HPG:(g + 1) * HPG], ALU.add).then_inc(s_ns, 1)

            def post(x):
                b, k = x
                kind, i, g = BLOCKS[b]
                d, r = den[:, b % 4, :], rgate[:, b % 4, :]
                gates = gate[:, i, g * 12:(g + 1) * 12].rearrange("p (h k) -> p k h", k=3)
                last = k == n_posts(b) - 1
                if k:
                    dve.wait_ge(s_dc, chain[0])
                else:
                    dve.wait_ge(s_exp, EXP_END[b])
                if kind == "cmp":
                    pr = probc[:, SLOT[b], :].rearrange("p (h n) -> p h n", h=HPG)
                    wide = lambda ap: ap.unsqueeze(2).to_broadcast([P, HPG, CMP_PAD])
                    if k == 0:
                        step = TS(d, d, 1e-30, None, ALU.max)
                    elif k == 1:
                        step = dve.reciprocal(r, d)
                    elif k == 2:
                        step = TT(pr, pr, wide(r), ALU.mult)
                    elif last:
                        step = TT(pr, pr, wide(gates[:, 0, :]), ALU.mult)
                    elif k == 3:
                        step = dve.tensor_reduce(pall[:], pr.rearrange("p h n -> p n h"), AX.X, ALU.add)
                    elif k == 4:
                        step = dve.tensor_reduce(imp[:], pall[:].rearrange("p (j r) -> p j r", r=4), AX.X, ALU.add)
                    elif k == 5:
                        step = TT(imp[:, 1:N_SEL], imp[:, 1:N_SEL], pall[:, 3:CMP_PAD - 1:4], ALU.add)
                    elif k == 6:
                        step = TT(score[:], imp[:], force[:, i - 4, :], ALU.add)
                    elif k == 7:
                        step = dve.max(top8[:], score[:])
                    elif k == 8:
                        step = dve.match_replace(picked[:], top8[:], score[:], TAKEN)
                    else:
                        n = SELECTS.index((i, g))
                        if n >= 2:
                            dve.wait_ge(s_wm, n - 1)
                        step = TS(selmask[:, g, :], picked[:], 1.5e30, NEG, ALU.is_lt, ALU.mult)
                elif k == 0:
                    step = TT(d, d, esink[:, b % 4, :], ALU.add) if kind == "swa" else dve.reciprocal(r, d)
                elif kind == "swa":
                    step = dve.reciprocal(r, d)
                else:
                    step = TT(r, r, gates[:, 2 if kind == "win" else 1, :], ALU.mult)
                if last:
                    step.then_inc(s_post, 1)
                else:
                    step.then_inc(s_dc, 1)
                    chain[0] += 1

            def turned_lo(t):
                b, kt = STEPS[t]
                dve.wait_ge(s_hi, t + 1)
                if BLOCKS[b][0] == "cmp":
                    dve.tensor_copy(pct[:, 256:HALF], pt[t % 2][0:CMP_PAD, 256:HALF]).then_inc(s_lo, 1)
                else:
                    TT(pt_lo[t % 3][:], pt[t % 2], f32(pt_hi[t % 3][:]), ALU.subtract).then_inc(s_lo, 1)

            def mixed_lo(t):
                kind, i, g = BLOCKS[STEPS[t][0]]
                h0 = (8 if kind == "swa" else 0) + g * HPG
                src = ob[kind == "swa"][0:HD, :].rearrange("p (c e q) -> p e c q", c=2, e=2)
                dve.wait_ge(s_oh, 2 * CLOSE_NO[t] + 2)
                for e in range(2):
                    rows, toks = slice(e * HD, (e + 1) * HD), slice(i * P, (i + 1) * P)
                    TT(qa[rows, h0 + 1:h0 + HPG:2, toks], src[:, e], f32(qa[rows, h0:h0 + HPG:2, toks]), ALU.subtract).then_inc(s_oev, 1)

            def first_slab(u):
                dve.wait_ge(s_sc, ITEM_END[LAST["win", 1]])
                split_w(u)

            for what, n in ORDER["DVE"]:
                {"take": score_item, "post": post, "lo": turned_lo, "out_lo": mixed_lo, "w_lo": first_slab}[what](n)

            def norm_dve(n):
                c, hf = n % KD, n // KD
                h = y[:, c, halves[hf]]
                STT(h, h, gain[:, 1, c:c + 1], ob[hf], ALU.mult, ALU.mult).then_inc(s_t, 1)
                if hf == 0 and n % 2 == 0:
                    dve.wait_ge(s_nx[n % 4], 16 * (n // 4 + 1))
                    dve.wait_ge(s_t, n + 1)
                    TT(h, h, nx[:, n % 4, :], ALU.add).then_inc(s_h[0], 1)

            def norm_lo(n):
                c, hf = n % KD, n // KD
                dve.wait_ge(s_mh, n + 1)
                STT(m_lo[:, c, halves[hf]], y[:, c, halves[hf]], gain[:, 2, c:c + 1], f32(m_hi[:, c, halves[hf]]), ALU.mult,
                    ALU.subtract).then_inc(s_ml, 1)

            split_w(U_OUT + 1)
            for n in range(2 * KD):
                if n % KD < KD - 1:
                    split_w(U_OUT + n + 2)
                dve.wait_ge(s_y, n + 1)
                dst = nacc[:, n // KD, :]
                if n % KD:
                    dve.wait_ge(s_nq, n)
                    TT(dst, dst, nsq[:, n % 2, :], ALU.add).then_inc(s_nq, 1)
                else:
                    dve.tensor_copy(dst, nsq[:, n % 2, :]).then_inc(s_nq, 1)
                if n % KD == KD - 1:
                    split_w(U_OUT + n + 2)
                if n == KD - 1:
                    diagonal(2, nacc[:, 0, :])
                if n == KD:
                    dve.wait_ge(s_rstd, 3)
                for m in NORMS_WITH.get(n - KD, []):
                    norm_dve(m)
                for m in NORMS_WITH.get(n - 2 - KD, []):
                    norm_lo(m)
            norm_lo(KD - 1)
            diagonal(3, nacc[:, 1, :])
            dve.wait_ge(s_rstd, 4)
            for n in range(KD, 2 * KD):
                norm_dve(n)
                if n >= KD + 2:
                    norm_lo(n - 2)
                if n == KD + 6:
                    diagonal(4, hacc[:, 0:HALF])
            norm_lo(2 * KD - 2)
            norm_lo(2 * KD - 1)
            diagonal(5, hacc[:, HALF:SEQ])

            def up_dve(u, par, f, done):
                dve.wait_ge(s_mm, u + 1)
                TT(uz[:, par, :], mp[par], hacc[:], ALU.mult).then_inc(s_ev, 1)
                dve.wait_ge(s_ev, u + 1)
                STT(uz[:, par, :], uz[:, par, :], 0.0, uz[:, par, :], ALU.max, ALU.mult).then_inc(s_u, 1)
                split_w(u + 2, par)
                dve.wait_ge(s_uh, done)
                flat = lambda ap: ap.rearrange("p a t -> p (a t)")
                TT(flat(u_lo[:, bass.ds(f, 1), :]), uz[:, par, :], flat(f32(u_hi[:, bass.ds(f, 1), :])),
                   ALU.subtract).then_inc(s_ul, 1)

            def down_dve(u, par, c, first):
                dve.wait_ge(s_mm, u + 1)
                dst = yacc[:, bass.ds(c, 1), :].rearrange("p a t -> p (a t)")
                if first:
                    dve.tensor_copy(dst, mp[par]).then_inc(s_ev, 1)
                else:
                    TT(dst, dst, mp[par], ALU.add).then_inc(s_ev, 1)

            def quarter(q, first, last):
                u0 = q * (2 * FQ) + U_MLP
                with dve.Fori(0, FQ // 2) as j:
                    for par in range(2):
                        f = 2 * j + par
                        up_dve(u0 + f, par, f, q * FQ + f + 1)
                if not last:
                    with dve.Fori(0, FQ // 2) as j:
                        for par in range(2):
                            c = 2 * j + par
                            split_w(u0 + c + (FQ + 2), par)
                            down_dve(u0 + c + FQ, par, c, first)

            for t in range(2):
                dve.wait_ge(s_rstd, 5 + t)
                link(dve.tensor_copy(hacc[:, halves[t]], pt[t]))
            dve.wait_ge(s_hst, 16 * 2 * KD)
            dve.wait_ge(s_h[1], 12)
            quarter(0, True, False)
            with dve.Fori(1, QUARTERS - 1) as q:
                quarter(q, False, False)
            quarter(QUARTERS - 1, False, True)

            def norm_out(n):
                c, hf = n % KD, n // KD
                y2 = yacc[:, c, halves[hf]]
                STT(y2, y2, gain[:, 3, c:c + 1], pt[hf], ALU.mult, ALU.mult).then_inc(s_ft, 1)
                if hf and c not in POOL_ADDS:
                    dve.wait_ge(s_ft, n + 1)
                    TT(y2, y2, fh[:, c, halves[hf]], ALU.add).then_inc(s_fo, 1)

            for n in range(2 * KD):
                c, hf, u = n % KD, n // KD, U_LAST + n
                toks = halves[hf]
                dve.wait_ge(s_mm, u + 1)
                TT(yacc[:, c, toks], yacc[:, c, toks], mp[u % 2][:, toks], ALU.add).then_inc(s_ev, 1)
                if u + 2 < N_UNITS:
                    split_w(u + 2)
                if n < 2 * KD - 1:
                    dve.wait_ge(s_fs, n + 1)
                    dst = facc[:, toks]
                    if c:
                        dve.wait_ge(s_fa, n)
                        TT(dst, dst, fsq[:, n % 2, 0:HALF], ALU.add).then_inc(s_fa, 1)
                    else:
                        dve.tensor_copy(dst, fsq[:, n % 2, 0:HALF]).then_inc(s_fa, 1)
                if n == KD - 1:
                    diagonal(6, facc[:, halves[0]])
                if n == KD:
                    dve.wait_ge(s_rstd, 7)
                for m in LAST_WITH.get(n - KD, []):
                    norm_out(m)
            diagonal(7, facc[:, halves[1]])
            dve.wait_ge(s_rstd, 8)
            dve.wait_ge(s_fh[1], 16 * KD)
            for n in range(KD, 2 * KD):
                norm_out(n)

        @block.gpsimd
        def _(pool):
            for b, (kind, i, g) in enumerate(BLOCKS):
                if kind == "cmp":
                    if i >= 4:
                        n = SELECTS.index((i, g))
                        width = (i + 1) * P
                        pool.wait_ge(s_post, b + 1)
                        if i > 4:
                            pool.wait_ge(s_sc, ITEM_END[BLOCKS.index(("sel", i - 1, g))])
                        pool.tensor_tensor(wmask[:, g, 0:width].rearrange("p (j t) -> p j t", t=HD),
                                           t_d[:, SEQ - width:SEQ].rearrange("p (j t) -> p j t", t=HD),
                                           selmask[:, g, 0:width // HD].unsqueeze(2).to_broadcast([P, width // HD, HD]),
                                           ALU.add).then_inc(s_wm, 1)
                else:
                    width = keys(kind, i)[1]
                    pool.wait_ge(s_post, b + 1)
                    for r in range(HPG):
                        pr = prob[:, SLOT[b], r, 0:width]
                        last = pool.tensor_scalar(pr, pr, rgate[:, b % 4, r:r + 1], 0.0, ALU.mult, ALU.add)
                    last.then_inc(s_p, 1)

            pool.wait_ge(s_oev, 2 * len(CLOSES))
            pool.wait_ge(s_sum, 3)
            pool.memset(hacc[:], 0.0).then_inc(s_zero, 1)
            pool.wait_ge(s_zero, 2)
            def add_square(n):
                toks = halves[n // KD]
                pool.wait_ge(s_hs, n + 1)
                if n:
                    pool.wait_ge(s_ha, n)
                pool.tensor_tensor(hacc[:, toks], hacc[:, toks], hsq[:, n % 3, :], ALU.add).then_inc(s_ha, 1)

            for n in range(2 * KD):
                if n % 2 or n >= KD:
                    h = y[:, n % KD, halves[n // KD]]
                    pool.wait_ge(s_t, n + 1)
                    pool.wait_ge(s_nx[n % 4], 16 * (n // 4 + 1))
                    pool.tensor_tensor(h, h, nx[:, n % 4, :], ALU.add).then_inc(s_h[1], 1)
                if 1 <= n <= KD:
                    add_square(n - 1)

            for n in list(range(KD)) + [KD + c for c in POOL_ADDS]:
                y2 = yacc[:, n % KD, halves[n // KD]]
                pool.wait_ge(s_ft, n + 1)
                pool.wait_ge(s_fh[n // KD], 16 * KD)
                pool.tensor_tensor(y2, y2, fh[:, n % KD, halves[n // KD]], ALU.add).then_inc(s_fp, 1)


def kernel(**inputs):
    import concourse.bacc as bacc
    from concourse.bass_utils import run_bass_kernel_spmd

    def layer(name):
        return np.asarray(inputs[name])[0]

    def slabs(w):
        return w.reshape(w.shape[0] // P, P, w.shape[1] // P, P).transpose(2, 1, 0, 3)

    w = layer("w_in")
    starts = np.cumsum([0, 512, 128, 128, 128, 128, 128, 128, 24, 512, 128])
    q_n, kc, v_c, ks, vs, kw, vw, gt, q_s, k_s, v_s = starts
    cols = lambda at, n=P: w[:, at:at + n]
    pad = np.zeros((D_MODEL, P - 24), w.dtype)
    w_in = np.concatenate([cols(k_s), cols(v_s), cols(kc), cols(v_c), cols(vs), cols(vw),
                           cols(gt, 24), pad, cols(ks), cols(kw), cols(q_n, 512), cols(q_s, 512)], axis=1)
    up, down = slabs(layer("w_up")), layer("w_down")
    mlp = []
    for q in range(QUARTERS):
        mlp.append(up[q * FQ:(q + 1) * FQ])
        mlp.append(slabs(down[q * FQ * P:(q + 1) * FQ * P]))
    gains = np.stack([layer(n).reshape(KD, P).T for n in ("norm_mix_pre", "norm_mix_post", "norm_mlp_pre", "norm_mlp_post")], axis=1)
    w1 = np.stack([layer(n).reshape(16, P, 256).transpose(1, 0, 2) for n in ("cmp_w1_k", "cmp_w1_v")])
    w2 = np.stack([np.concatenate([layer(n)] * 2, axis=1).reshape(2, P, P).transpose(1, 0, 2) for n in ("cmp_w2_k", "cmp_w2_v")])
    pe = np.stack([layer(n).reshape(16, P).T for n in ("cmp_pe_k", "cmp_pe_v")])
    arrays = {
        "xT": np.asarray(inputs["x"])[0].T.reshape(KD, P, SEQ),
        "w_in": slabs(w_in),
        "w_out": slabs(layer("w_out")),
        "w_mlp": np.concatenate(mlp),
        "gains": gains, "w1": w1, "w2": w2, "pe": pe,
        "sinks": np.broadcast_to(layer("sinks").reshape(1, 8), (P, 8)),
        "consts": constants(),
    }
    arrays = {n: np.ascontiguousarray(a) for n, a in arrays.items()}
    nc = bacc.Bacc("TRN2", target_bir_lowering=False, num_devices=1, dynamic_dma_scratch_size=1024)
    aps = [nc.dram_tensor(n, a.shape, F32, kind="ExternalInput").ap() for n, a in arrays.items()]
    h_dram = nc.dram_tensor("h_scratch", (KD, P, SEQ), F32, kind="Internal").ap()
    out = nc.dram_tensor("out", (KD, P, SEQ), F32, kind="ExternalOutput").ap()
    hybrid_layer(nc, *aps, h_dram, out)
    result = run_bass_kernel_spmd(nc, [arrays], core_ids=[0]).results[0]["out"]
    return np.ascontiguousarray(result.reshape(D_MODEL, SEQ).T)[None]
```

```python
from contextlib import ExitStack

import numpy as np

import concourse.bass as bass
from concourse import mybir

F32 = mybir.dt.float32
F32R = mybir.dt.float32r
ALU = mybir.AluOpType
ACT = mybir.ActivationFunctionType
AX = mybir.AxisListType

P = 128
D_MODEL = 1024
SEQ = 1024
HALF = 512
KD = D_MODEL // P
NT = SEQ // P
HD = 64
GROUPS = 2
HPG = 4
N_CMP = 63
CMP_PAD = 64
CMP_W = 120
N_SEL = 16
SEL_TOPN = 8
D_FF = 4096
QUARTERS = 4
FQ = D_FF // P // QUARTERS
EPS = 1e-6
NEG = -1e30
FORCED = 1e30
TAKEN = 2e30
NO_KEY = 1e25

KS_SWA, VT_SWA, KC, VC_, VT_SLC, VT_WIN, GATES, K_SLC, K_WIN = range(9)
N_KV_CHUNKS = 9
N_Q_CHUNKS = 8
N_IN = N_KV_CHUNKS + N_Q_CHUNKS
SLC, WIN, SWA = range(3)
U_OUT = 2 * N_IN
U_MLP = U_OUT + 2 * KD
N_MLP = QUARTERS * 2 * FQ
U_LAST = U_MLP + N_MLP - FQ
N_UNITS = U_LAST + 2 * FQ

C_IDENT, C_ONES = 0, P
C_TD = 2 * P
C_TW = C_TD + SEQ
C_TS = C_TW + 640
C_TC = C_TS + 256
C_FORCE = C_TC + CMP_W
C_QS = C_FORCE + 4 * N_SEL
C_END = C_QS + N_Q_CHUNKS


def slopes():
    s = (2.0 ** (-8.0 * (np.arange(16) + 1) / 16)).astype(np.float32)
    return np.concatenate([s[0::2], s[1::2]])


def constants():
    p = np.arange(P)[:, None]
    c = np.zeros((P, C_END), np.float32)
    c[:, C_IDENT:C_IDENT + P] = np.eye(P)
    c[:, C_ONES:C_ONES + P] = 1.0

    def table(at, width, before, window):
        dist = p - (np.arange(width)[None, :] - before)
        c[:, at:at + width] = np.where((dist >= 0) & (dist < window), -dist, NEG)

    table(C_TD, SEQ, SEQ - P, SEQ)
    table(C_TW, 640, 512, 512)
    table(C_TS, 256, 128, 128)
    dist = P * (NT - 1) + p - (16 * np.arange(CMP_W)[None, :] + 31)
    c[:, C_TC:C_TC + CMP_W] = np.where(dist >= 0, -dist, NEG)
    for i in range(4, NT):
        own = 2 * i + p // 64
        j = np.arange(N_SEL)[None, :]
        forced = (j == 0) | (j == own) | (j == own - 1)
        c[:, C_FORCE + (i - 4) * N_SEL:C_FORCE + (i - 3) * N_SEL] = np.where(j > own, NEG, np.where(forced, FORCED, 0.0))
    s = slopes()
    for q in range(N_Q_CHUNKS):
        c[:HD, C_QS + q] = 0.125 / s[2 * q]
        c[HD:, C_QS + q] = 0.125 / s[2 * q + 1]
    return c


def hybrid_layer(nc, xT, w_in, w_out, w_mlp, gains, w1, w2, pe_in, sinks, consts, h_dram, out):
    SL = [float(s) for s in slopes()]
    ctx = ExitStack()
    with ctx:
        small_at = 1152
        ring_at = small_at + 4096
        qa_at = ring_at + 24576
        kv_at = qa_at + 65536
        rest_at = kv_at + 73728

        def sb(name, shape, dt, at):
            return nc.alloc_sbuf_tensor_at(name, shape, dt, offset=at)

        ident = sb("ident", [P, P], F32, small_at)
        ones = sb("ones", [P, P], F32, small_at + 512)
        gain = sb("gain", [P, 4, KD], F32, small_at + 1024)
        gate = sb("gate", [P, NT, 24], F32, small_at + 1152)
        kc_hi = sb("kc_hi", [P, GROUPS, CMP_PAD], F32R, small_at + 1920)
        kc_lo = sb("kc_lo", [P, GROUPS, CMP_PAD], F32R, small_at + 2432)
        vc = sb("vc", [CMP_PAD, GROUPS, 608], F32, small_at + 512)[:, :, 0:P]
        qscale = sb("qscale", [P, N_Q_CHUNKS], F32, small_at + 3456)
        sink = sb("sink", [P, 8], F32, small_at + 3488)
        nsink = sb("nsink", [P, 8], F32, small_at + 3520)
        eps = sb("eps", [P, 1], F32, small_at + 3552)
        nmax = sb("nmax", [P, 4, HPG], F32, small_at + 3584)
        den = sb("den", [P, 4, HPG], F32, small_at + 3648)
        esink = sb("esink", [P, 4, HPG], F32, small_at + 3712)
        rgate = sb("rgate", [P, 4, HPG], F32, small_at + 3776)
        imp = sb("imp", [P, N_SEL], F32, small_at + 3840)
        score = sb("score", [P, N_SEL], F32, small_at + 3904)
        picked = sb("picked", [P, N_SEL], F32, small_at + 3968)
        top8 = sb("top8", [P, 8], F32, small_at + 4032)
        rs = sb("rs", [P, 8], F32, small_at + 4064)

        w_raw = [sb(f"w_raw{i}", [P, KD, P], F32, ring_at + 4096 * i) for i in range(2)]
        w_hi = [sb(f"w_hi{i}", [P, KD, P], F32R, ring_at + 8192 + 4096 * i) for i in range(2)]
        w_lo = [sb(f"w_lo{i}", [P, KD, P], F32R, ring_at + 16384 + 4096 * i) for i in range(2)]
        qa = sb("qa", [P, 16, SEQ], F32R, qa_at)
        k_hi = sb("k_hi", [P, 3, GROUPS, SEQ], F32R, kv_at)
        k_lo = sb("k_lo", [P, 3, GROUPS, SEQ], F32R, kv_at + 24576)
        v = sb("v", [P, 3, NT, GROUPS, 2, HD], F32R, kv_at + 49152)
        x_hi = sb("x_hi", [P, KD, HALF], F32R, rest_at)
        x_lo = sb("x_lo", [P, KD, HALF], F32R, rest_at + 16384)
        x_raw = sb("x_raw", [P, 2, HALF], F32, rest_at + 32768)
        z = sb("z", [P, HALF], F32, rest_at + 36864)
        z_hi = sb("z_hi", [P, HALF], F32R, rest_at + 38912)
        sq = [sb(f"sq{i}", [P, HALF], F32, kv_at + 49152 + 6144 + 8192 * i) for i in range(2)]
        zv = sb("zv", [P, 4, HALF], F32, rest_at + 40960)
        x_in = [x_raw[:, 0], x_raw[:, 1]] + [zv[:, n] for n in range(4)] + [
            sb(f"x_in{i}", [P, HALF], F32, kv_at + 2048 + 24576 * i)[:] for i in range(2)]
        zkv = sb("zkv", [P, 2, 8, GROUPS, 64], F32, rest_at + 49152)
        rstd = sb("rstd", [P, HALF], F32, rest_at + 57344)
        xacc = sb("xacc", [P, HALF], F32, kv_at + 71680)
        w1_at = [sb(f"w1_sb{i}", [P, 8, SEQ], F32, qa_at + 32768 * (1 - i))[:, :, HALF:SEQ] for i in range(2)]
        blk_at = [sb(f"blk{i}", [P, 4, SEQ], F32, kv_at + 24576 * i)[:, :, HALF:HALF + 8 * N_CMP] for i in range(2)]
        w2_sb = sb("w2_sb", [P, 2, 2, P], F32, kv_at + 49152 + 4096)
        hid = [sb(f"hid{i}", [P, 2, 2 * N_CMP], F32, kv_at + 49152 + 6144 + 1024 * i) for i in range(2)]
        pe_sb = sb("pe_sb", [P, 2, 16], F32, kv_at + 49152 + 12288)
        wmask = sb("wmask", [P, GROUPS, SEQ], F32, ring_at)
        pt_hi = [sb(f"pt_hi{i}", [P, HALF], F32R, at) for i, at in enumerate((rest_at + 49152, rest_at + 51200, rest_at + 53248))]
        pt_lo = [sb(f"pt_lo{i}", [P, HALF], F32R, at) for i, at in enumerate((ring_at + 12288, ring_at + 14336, rest_at + 55296))]
        t_d = sb("t_d", [P, SEQ], F32, ring_at + 20480)
        t_w = sb("t_w", [P, 640], F32, ring_at + 16384)
        t_s = sb("t_s", [P, 256], F32, ring_at + 18944)
        pt_lo_end = [sb(f"pt_lo_end{i}", [P, HALF], F32R, rest_at + 16384 + 2048 * i) for i in range(3)]
        prob = sb("prob", [P, 3, HPG, SEQ], F32, rest_at)
        t_c = sb("t_c", [P, CMP_W], F32, ring_at + 8192)
        force = sb("force", [P, 4, N_SEL], F32, ring_at + 11776)
        pct = sb("pct", [CMP_PAD, HALF], F32, ring_at + 8704)
        pall = sb("pall", [P, CMP_PAD], F32, ring_at + 12032)
        selmask = sb("selmask", [P, GROUPS, N_SEL], F32, rest_at + 59392)
        probc = [sb(f"probc{i}", [P, HPG * CMP_PAD], F32, at) for i, at in enumerate((ring_at + 10752, rest_at + 57344))]
        mixed = sb("mixed", [P, 2, P], F32, rest_at + 58368)
        y = sb("y", [P, KD, SEQ], F32, kv_at)
        m_hi = sb("m_hi", [P, KD, SEQ], F32R, rest_at)
        m_lo = sb("m_lo", [P, KD, SEQ], F32R, kv_at + 32768)
        nx = sb("nx", [P, 4, HALF], F32, rest_at + 32768)
        nsq = sb("nsq", [P, 2, HALF], F32, rest_at + 40960)
        nacc = sb("nacc", [P, 2, HALF], F32, rest_at + 45056)
        hacc = sb("hacc", [P, SEQ], F32, rest_at + 49152)
        hsq = sb("hsq", [P, 3, HALF], F32, rest_at + 53248)
        u_hi = sb("u_hi", [P, FQ, SEQ], F32R, qa_at)
        u_lo = sb("u_lo", [P, FQ, SEQ], F32R, qa_at + 32768)
        yacc = sb("yacc", [P, KD, SEQ], F32, kv_at)
        uz = sb("uz", [P, 2, SEQ], F32, rest_at + 32768)
        fsq = sb("fsq", [P, 2, SEQ], F32, rest_at + 32768)
        facc = sb("facc", [P, SEQ], F32, rest_at + 53248)
        fh = sb("fh", [P, KD, SEQ], F32, rest_at)

        banks = ctx.enter_context(nc.psum_tensor("banks", [P, 2 * SEQ], F32))
        mp = [banks[:, 0:SEQ], banks[:, SEQ:2 * SEQ]]
        pts = ctx.enter_context(nc.psum_tensor("pts", [P, SEQ], F32))
        obs = ctx.enter_context(nc.psum_tensor("obs", [P, SEQ], F32))
        halves = [slice(0, HALF), slice(HALF, SEQ)]
        pt, ob = [pts[:, t] for t in halves], [obs[:, t] for t in halves]
        tp = [pt[0], pt[1], ob[0], mp[1][:, HALF:SEQ]]
        stat = ob[1]

        def sem(name):
            return ctx.enter_context(nc.semaphore(name))

        s_gain, s_const = sem("gains_loaded"), sem("consts_loaded")
        s_x = [sem(f"x_loaded{i}") for i in range(KD)]
        s_xh, s_xl = sem("x_hi_ready"), sem("x_lo_ready")
        s_sq, s_xq = sem("squares_ready"), sem("squares_added")
        s_xu = sem("x_used")
        s_sum, s_std, s_diag, s_rstd = sem("sum_ready"), sem("std_ready"), sem("diagonal_ready"), sem("rstd_ready")
        s_w = [sem("w_loaded0"), sem("w_loaded1")]
        s_wh, s_wl = sem("w_hi_ready"), sem("w_lo_ready")
        s_mm, s_ev = sem("product_ready"), sem("product_taken")
        s_zh, s_za, s_zl = sem("z_hi_ready"), sem("z_copied"), sem("z_lo_written")
        s_sig, s_vt, s_vh, s_vl = sem("gates_ready"), sem("v_turned"), sem("v_hi_ready"), sem("v_lo_ready")
        s_cw, s_blk, s_hp, s_hid = sem("cmp_weights_loaded"), sem("blocks_ready"), sem("hidden_sum"), sem("hidden_ready")
        s_kcp, s_kch, s_kcl = sem("kv_cmp_sum"), sem("kc_hi_ready"), sem("kc_lo_ready")
        s_one = sem("ones_ready")
        s_tab, s_zero = sem("tables_loaded"), sem("zeroed")
        s_S, s_sc, s_exp = sem("scores_ready"), sem("scores_taken"), sem("exp_ready")
        s_ns, s_post, s_p = sem("sink_shift_ready"), sem("scale_ready"), sem("probs_ready")
        s_dc, s_wm = sem("dve_chain"), sem("mask_ready")
        s_tr, s_hi, s_lo, s_pv = sem("probs_turned"), sem("turned_hi"), sem("turned_lo"), sem("pv_done")
        s_oa, s_om = sem("mixed_rows_copied"), sem("mixed_ready")
        s_oh, s_oev = sem("mixed_hi"), sem("mixed_lo")
        s_y, s_nq = sem("y_squares"), sem("y_squares_added")
        s_nx = [sem(f"nx_loaded{i}") for i in range(4)]
        s_t, s_h = sem("normed"), [sem("h_ready_even"), sem("h_ready_odd")]
        s_mh, s_ml, s_hs, s_ha = sem("m_hi_ready"), sem("m_lo_ready"), sem("h_squares"), sem("h_squares_added")
        s_hst, s_hq = sem("h_stored"), sem("h_squares_summed")
        s_u, s_uh, s_ul = sem("u_ready"), sem("u_hi_ready"), sem("u_lo_ready")
        s_fh, s_fs, s_fa = [sem("h_loaded0"), sem("h_loaded1")], sem("y2_squares"), sem("y2_squares_added")
        s_ft, s_fo, s_fp, s_out = (sem(n) for n in ("y2_normed", "out_ready", "out_ready_pool", "out_stored"))

        BLOCKS = [(kind, i, g) for i in range(NT) for g in range(GROUPS) for kind in ('swa', 'cmp', 'win', 'sel')]

        def keys(kind, i):
            before = {"win": 4, "sel": NT, "swa": 1}[kind]
            first = max(0, i - before)
            return first * P, (i + 1 - first) * P

        ITEMS, STEPS = [], []
        ITEM_END, STEP_END, EXP_END, SCALED_END = [], [], [], []
        exps = scaled = 0
        for b, (kind, i, g) in enumerate(BLOCKS):
            ITEMS += [(b, h) for h in ([None] if kind == "cmp" else range(HPG))]
            STEPS += [(b, t) for t in range(1 if kind == "cmp" else keys(kind, i)[1] // P)]
            exps += HPG + (kind == "swa")
            scaled += kind != "cmp"
            ITEM_END.append(len(ITEMS))
            STEP_END.append(len(STEPS))
            EXP_END.append(exps)
            SCALED_END.append(scaled)
        NB = len(BLOCKS)

        SLOT, SLOT_BEFORE = [], []
        for b, (kind, i, g) in enumerate(BLOCKS):
            same = [c for c in range(b) if (BLOCKS[c][0] == "cmp") == (kind == "cmp")]
            n = 2 if kind == "cmp" else 3
            SLOT.append(len(same) % n)
            SLOT_BEFORE.append(same[-n] if len(same) >= n else None)

        LAST = {(kind, g): b for b, (kind, i, g) in enumerate(BLOCKS)}
        SELECTS = [(i, g) for i in range(4, NT) for g in range(GROUPS)]
        CLOSES = {STEP_END[b] - 1: b for b in range(NB) if BLOCKS[b][0] in ("sel", "swa")}
        CLOSE_NO = {t: n for n, t in enumerate(sorted(CLOSES))}

        BANK, BANK_BEFORE = [], []
        at, owner = 0, {}
        for n, (b, h) in enumerate(ITEMS):
            n_banks = 1 if h is None or keys(*BLOCKS[b][:2])[1] <= HALF else 2
            if at + n_banks > 4:
                at = 0
            BANK.append(at)
            before = [owner[c] for c in range(at, at + n_banks) if c in owner]
            BANK_BEFORE.append(max(before) if before else None)
            owner.update({c: n for c in range(at, at + n_banks)})
            at = (at + n_banks) % 4

        def lo_part(t):
            return (pt_lo if t < STEP_END[NB - 2] else pt_lo_end)[t % 3][:]

        def n_posts(b):
            kind, i, g = BLOCKS[b]
            return (4 if i < 4 else 11) if kind == "cmp" else 2

        def plan():
            width = lambda b: CMP_PAD if BLOCKS[b][0] == "cmp" else keys(*BLOCKS[b][:2])[1]
            ITEM_B, STEP_B = [b for b, _ in ITEMS], [b for b, _ in STEPS]
            posts = [(b, k) for b in range(NB) for k in range(n_posts(b))]
            closes = sorted(CLOSES)
            lists = {
                "PE": {"weigh": range(len(STEPS)), "turn": range(len(STEPS)), "scores": range(len(ITEMS)), "project": range(2 * KD)},
                "DVE": {"lo": range(len(STEPS)), "out_mix": closes, "post": posts, "take": range(len(ITEMS)), "w_lo": [0, 1, 2]},
                "ACT": {"hi": range(len(STEPS)), "out_copy": closes, "out_hi": closes, "exp": range(len(ITEMS)), "w_hi": [0, 1, 2]},
                "SP": {"load": [0, 1, 2]},
                "POOL": {"scale": range(NB), "out_lo": closes},
            }
            done = {}
            LATER = {"turn": -500, "scores": -300, "weigh": -150, "hi": -50, "post": -50, "out_lo": 50}
            engine_of = {w: e for e, ws in lists.items() for w in ws}

            def needs(what, x):
                if what == "scores":
                    return [("take", BANK_BEFORE[x])] if BANK_BEFORE[x] is not None else []
                if what == "take":
                    b, out = ITEM_B[x], [("scores", x)]
                    if SLOT_BEFORE[b] is not None:
                        out.append(("turn", STEP_END[SLOT_BEFORE[b]] - 1))
                    if b >= 4:
                        out.append(("post", (b - 4, n_posts(b - 4) - 1)))
                        out.append(("scale", b - 4))
                    if BLOCKS[b][0] == "sel" and BLOCKS[b][1] >= 4:
                        out.append(("scale", b - 2))
                    return out
                if what == "exp":
                    return [("take", x)]
                if what == "post":
                    b, k = x
                    return [("post", (b, k - 1))] if k else [("exp", ITEM_END[b] - 1)]
                if what == "scale":
                    return [("post", (x, n_posts(x) - 1))]
                if what == "turn":
                    return [("scale", STEP_B[x])] + ([("lo", x - 2)] if x >= 2 else [])
                if what == "hi":
                    return [("turn", x)] + ([("weigh", x - 3)] if x >= 3 else [])
                if what == "lo":
                    return [("hi", x)]
                if what == "weigh":
                    out = [("lo", x)]
                    n = sum(c < x for c in CLOSES)
                    if n >= 2:
                        out.append(("out_mix", closes[n - 2]))
                    return out
                if what == "load":
                    return [("w_lo", 0)] if x == 2 else [("take", ITEM_END[LAST["sel", x]] - 1)]
                if what == "w_hi":
                    before = ("project", KD - 1) if x == 2 else ("weigh", STEP_END[LAST["win" if x else "cmp", 1]] - 1)
                    return [("load", x), before]
                if what == "w_lo":
                    return [("w_hi", x), ("take", ITEM_END[LAST["win", 1]] - 1)]
                if what == "project":
                    return [("w_lo", x // KD), ("take", len(ITEMS) - 1)]
                if what == "out_copy":
                    return [("weigh", x)] + ([("out_lo", closes[CLOSE_NO[x] - 1])] if CLOSE_NO[x] else [])
                if what == "out_mix":
                    return [("out_copy", x)]
                if what == "out_hi":
                    return [("out_mix", x)]
                if what == "out_lo":
                    return [("out_hi", x)]

            def cost(what, x):
                if what == "scores":
                    return 450 if ITEMS[x][1] is None else 0.84 * width(ITEM_B[x]) + 10
                if what == "take":
                    return 560 if ITEMS[x][1] is None else 1.05 * width(ITEM_B[x]) + 70
                if what == "exp":
                    return 1330 if ITEMS[x][1] is None else 0.84 * width(ITEM_B[x]) + 290
                if what == "post":
                    b, k = x
                    if BLOCKS[b][0] != "cmp":
                        return 85
                    return 335 if k in (2, n_posts(b) - 1) or k == 3 else 90
                if what == "scale":
                    kind, i, g = BLOCKS[x]
                    if kind == "cmp":
                        return 1.8 * (i + 1) * P + 50 if i >= 4 else 1
                    return 4 * (0.833 * width(x) + 244)
                if what in ("hi", "lo", "weigh") and BLOCKS[STEPS[x][0]][0] == "cmp":
                    return {"hi": 264, "lo": 335, "weigh": 860}[what]
                return {"project": 640, "load": 4000, "w_hi": 950, "w_lo": 1140, "turn": 430, "weigh": 430,
                        "hi": 480, "lo": 605, "out_copy": 530, "out_mix": 680, "out_hi": 310, "out_lo": 620}[what]

            order = {e: [] for e in lists}
            heads = {e: {w: 0 for w in ws} for e, ws in lists.items()}
            free = dict.fromkeys(lists, 0.0)
            left = sum(len(x) for ws in lists.values() for x in ws.values())
            while left:
                best = None
                for e, ws in lists.items():
                    for rank, (w, xs) in enumerate(ws.items()):
                        n = heads[e][w]
                        if n == len(xs):
                            continue
                        got = [done.get(d) for d in needs(w, xs[n])]
                        if None in got:
                            continue
                        start = free[e]
                        for (other, _), t in zip(needs(w, xs[n]), got):
                            start = max(start, t + (210 if "PE" in (e, engine_of[other]) else 140))
                        key = (start + LATER.get(w, 0), rank)
                        if best is None or key < best[0]:
                            best = (key, e, w, xs[n], start)
                _, e, w, x, start = best
                free[e] = start + cost(w, x)
                done[(w, x)] = free[e]
                heads[e][w] += 1
                order[e].append((w, x))
                left -= 1
            return order

        ORDER = plan()

        TAKE_X = [[w for k in range(KD) for w in [("parts", k), ("square", k)] + [("slab", 1)] * (k == 3)],
                  [("parts", 0)] + [w for k in range(1, KD) for w in [("parts", k)] + [("square", k - 1)] * (k < KD - 1)]
                  + [("slab", N_IN + 1), ("square", KD - 2), ("square", KD - 1), ("project", N_IN - 1)]]
        NORMS_WITH = {1: [0], 2: [1, 2], 3: [3], 4: [4, 5], 5: [6], 6: [7]}
        LAST_WITH = {1: [0], 2: [1, 2], 3: [3], 4: [4], 5: [5], 6: [6], 7: [7]}
        POOL_ADDS = [0, 3, 6]

        def w_slab(u):
            if u < U_OUT:
                return w_in[u % N_IN]
            return w_out[(u - U_OUT) % KD]

        block = ctx.enter_context(nc.Block())

        @block.sync
        def _(sp):
            def load_w(u):
                if u >= 2:
                    sp.wait_ge(s_wl, u - 1)
                sp.dma_start(w_raw[u % 2][:], w_slab(u)).then_inc(s_w[u % 2], 16)

            def load_x(n):
                if n >= KD:
                    sp.wait_ge(s_xl, n - KD + 1)
                    sp.wait_ge(s_sq, n - KD + 1)
                sp.dma_start(x_in[n % KD], xT[n % KD, :, (n // KD) * HALF:(n // KD + 1) * HALF]).then_inc(s_x[n % KD], 16)

            load_w(0)
            for n in range(4):
                load_x(n)
            load_w(1)
            for n in range(4, KD):
                load_x(n)
            for dst, at, n in ((ident, C_IDENT, P), (ones, C_ONES, P), (qscale, C_QS, N_Q_CHUNKS)):
                sp.dma_start(dst[:], consts[:, at:at + n]).then_inc(s_const, 16)
            sp.dma_start(sink[:], sinks).then_inc(s_const, 16)
            for kv in range(2):
                sp.dma_start(pe_sb[:, kv, :], pe_in[kv]).then_inc(s_cw, 16)
                sp.dma_start(w2_sb[:, kv], w2[kv]).then_inc(s_cw, 16)
            for u in range(2, GATES + 7):
                load_w(u)
                if u < 10:
                    kv, part = divmod(u - 2, 4)
                    sp.dma_start(w1_at[kv][:, 2 * part:2 * part + 2, :],
                                 w1[kv][:, 4 * part:4 * part + 4, :].rearrange("p (s i) h -> p s (i h)", i=2)).then_inc(s_cw, 16)
            sp.wait_ge(s_vt, 4)
            for n in range(KD, 2 * KD):
                load_x(n)
            for u in range(GATES + 7, N_IN + 2):
                load_w(u)
            for u in range(N_IN + 2, U_OUT):
                load_w(u)

            sp.wait_ge(s_mm, U_OUT - 1)
            for dst, at, n in ((t_s, C_TS, 256), (t_c, C_TC, CMP_W), (t_w, C_TW, 640)):
                sp.dma_start(dst[:], consts[:, at:at + n]).then_inc(s_tab, 16)
            sp.dma_start(force[:], consts[:, C_FORCE:C_QS].rearrange("p (i n) -> p i n", n=N_SEL)).then_inc(s_tab, 16)
            sp.wait_ge(s_mm, U_OUT)
            sp.dma_start(t_d[:], consts[:, C_TD:C_TD + SEQ]).then_inc(s_tab, 16)

            for g in range(GROUPS):
                sp.wait_ge(s_sc, ITEM_END[LAST["sel", g]])
                load_w(U_OUT + g)
            load_w(U_OUT + 2)
            sp.wait_ge(s_tr, len(STEPS))
            for n in range(4):
                sp.dma_start(nx[:, n, :], xT[n, :, 0:HALF]).then_inc(s_nx[n], 16)
            for u in range(U_OUT + 3, U_MLP):
                load_w(u)

            def load_mlp(u, par):
                sp.wait_ge(s_wl, u - 1)
                slab = w_mlp[bass.ds(u - U_MLP, 1)].rearrange("a p k c -> p (a k) c")
                sp.dma_start(w_raw[par][:], slab).then_inc(s_w[par], 16)

            load_mlp(U_MLP, 0)
            load_mlp(U_MLP + 1, 1)
            with sp.Fori(1, N_MLP // 2) as j:
                for par in range(2):
                    load_mlp(2 * j + (U_MLP + par), par)

            for u in range(U_MLP + N_MLP, N_UNITS):
                sp.wait_ge(s_wl, u - 1)
                sp.dma_start(w_raw[u % 2][:], w_mlp[u - U_MLP - FQ]).then_inc(s_w[u % 2], 16)

            for n in range(2 * KD):
                c, hf = n % KD, n // KD
                if hf == 0 or c in POOL_ADDS:
                    sp.wait_ge(s_fp, c + 1 if hf == 0 else KD + POOL_ADDS.index(c) + 1)
                else:
                    sp.wait_ge(s_fo, c - sum(p < c for p in POOL_ADDS) + 1)
                sp.dma_start(out[c, :, halves[hf]], yacc[:, c, halves[hf]]).then_inc(s_out, 16)
            sp.wait_ge(s_out, 16 * 2 * KD)

        @block.tensor
        def _(pe):
            def row_sums(dst, acc):
                for t in range(4):
                    last = pe.matmul(dst[:, t:t + 1], acc[:, t * P:(t + 1) * P], ones[:, 0:1], start=True, stop=True)
                last.then_inc(s_sum, 1)

            def spread(n, dst, diag):
                pe.wait_ge(s_diag, n + 1)
                pe.matmul(dst, ones[:], diag, start=True, stop=True).then_inc(s_rstd, 1)

            def unit(u, par, out_at, hi, lo, before_k=None, used=None):
                pe.wait_ge(s_wl, u + 1)
                if not isinstance(u, int) or u >= 2:
                    pe.wait_ge(s_ev, u - 1)
                for k in range(KD):
                    if before_k:
                        before_k(k)
                    for dst, a, b in zip(out_at, hi, lo):
                        pe.matmul(dst, w_hi[par][:, k, :], a(k), start=(k == 0), stop=False)
                        pe.matmul(dst, w_hi[par][:, k, :], b(k), start=False, stop=False)
                    for dst, a in zip(out_at, hi):
                        last = pe.matmul(dst, w_lo[par][:, k, :], a(k), start=False, stop=(k == KD - 1))
                    if used and k < KD - 1:
                        last.then_inc(used, 1)
                last.then_inc(s_mm, 1)

            def hidden(kv):
                pe.wait_ge(s_cw, 16 * 12)
                pe.wait_ge(s_blk, 2 * kv + 2)
                for hh in range(2):
                    for pp in range(16):
                        w_at, b_at = 256 * (pp % 2) + hh * P, 2 * N_CMP * (pp % 4)
                        last = pe.matmul(pt[kv][:, hh * P:hh * P + 2 * N_CMP], w1_at[kv][:, pp // 2, w_at:w_at + P],
                                         blk_at[kv][:, pp // 4, b_at:b_at + 2 * N_CMP], start=(pp == 0), stop=(pp == 15))
                last.then_inc(s_hp, 1)

            def compressed():
                pe.wait_ge(s_hid, 1)
                for hh in range(2):
                    last = pe.matmul(ob[0][:, 0:2 * N_CMP], w2_sb[:, 0, hh, :], hid[0][:, hh, :], start=(hh == 0), stop=(hh == 1))
                last.then_inc(s_kcp, 1)
                pe.wait_ge(s_hid, 2)
                for g in range(GROUPS):
                    for hh in range(2):
                        last = pe.matmul(ob[1][0:N_CMP, g * HD:(g + 1) * HD], hid[1][:, hh, g * N_CMP:(g + 1) * N_CMP],
                                         w2_sb[:, 1, hh, 0:HD], start=(hh == 0), stop=(hh == 1))
                last.then_inc(s_kcp, 1)

            for hf in range(2):
                for j in range(N_IN):
                    u = hf * N_IN + j

                    def before(k):
                        if j == 0:
                            pe.wait_ge(s_xl, hf * KD + k + 1)
                        if j == 1 and k == KD - 2:
                            pe.wait_ge(s_const, 16 * 4)
                            pe.wait_ge(s_xq, KD * (hf + 1))
                            row_sums(ob[0], xacc)
                        if j == 1 and k == KD - 1:
                            spread(hf, stat, xacc[:])
                    unit(u, u % 2, [mp[u % 2][:, 0:HALF]], [lambda k: x_hi[:, k, :]], [lambda k: x_lo[:, k, :]],
                         before, s_xu if u == N_IN - 1 else None)
                    if hf and j in (5, 6):
                        hidden(j - 5)
                    if hf and j == 7:
                        compressed()
                    if j == GATES + 2:
                        pe.wait_ge(s_ev, hf * N_IN + GATES + 1)
                        pe.wait_ge(s_sig, hf + 1)
                        if hf:
                            pe.wait_ge(s_vl, 4)
                            pe.wait_ge(s_kcl, 1)
                        for n in range(4):
                            for t in range(4):
                                last = pe.transpose(tp[n][:, t * P:(t + 1) * P], zv[:, n, t * P:(t + 1) * P], ident[:])
                            last.then_inc(s_vt, 1)

            pe.wait_ge(s_ev, U_OUT - 1)
            pe.wait_ge(s_za, 21)
            pe.wait_ge(s_zl, 21)
            pe.wait_ge(s_vl, 8)

            def scores(n):
                b, h = ITEMS[n]
                kind, i, g = BLOCKS[b]
                if BANK_BEFORE[n] is not None:
                    pe.wait_ge(s_sc, BANK_BEFORE[n] + 1)
                if n == 2:
                    pe.wait_ge(s_ev, U_OUT)
                if n == ITEM_END[3]:
                    pe.wait_ge(s_za, 22)
                    pe.wait_ge(s_zl, 22)
                dst = banks[:, BANK[n] * HALF:BANK[n] * HALF + max(HALF, 0 if h is None else keys(kind, i)[1])]
                toks = slice(i * P, (i + 1) * P)
                if kind == "cmp":
                    for r in range(HPG):
                        q = qa[:, g * HPG + r, toks]
                        at = dst[:, r * CMP_PAD:(r + 1) * CMP_PAD]
                        pe.matmul(at, q, kc_hi[:, g, :], start=True, stop=False)
                        last = pe.matmul(at, q, kc_lo[:, g, :], start=False, stop=True)
                else:
                    typ = {"win": WIN, "sel": SLC, "swa": SWA}[kind]
                    q = qa[:, (8 if kind == "swa" else 0) + g * HPG + h, toks]
                    first, width = keys(kind, i)
                    for at in range(0, width, HALF):
                        w = min(HALF, width - at)
                        ks = slice(first + at, first + at + w)
                        pe.matmul(dst[:, at:at + w], q, k_hi[:, typ, g, ks], start=True, stop=False)
                        last = pe.matmul(dst[:, at:at + w], q, k_lo[:, typ, g, ks], start=False, stop=True)
                last.then_inc(s_S, 1)

            def turn(t):
                b, kt = STEPS[t]
                kind, i, g = BLOCKS[b]
                if kind == "cmp":
                    pe.wait_ge(s_post, b + 1)
                else:
                    pe.wait_ge(s_p, SCALED_END[b])
                if t >= 2:
                    pe.wait_ge(s_lo, t - 1)
                for r in range(HPG):
                    if kind == "cmp":
                        last = pe.transpose(pt[t % 2][0:CMP_PAD, r * P:(r + 1) * P],
                                            probc[SLOT[b]][:, r * CMP_PAD:(r + 1) * CMP_PAD], ident[:])
                    else:
                        last = pe.transpose(pt[t % 2][:, r * P:(r + 1) * P], prob[:, SLOT[b], r, kt * P:(kt + 1) * P], ident[:])
                last.then_inc(s_tr, 1)

            def weigh(t):
                b, kt = STEPS[t]
                kind, i, g = BLOCKS[b]
                dst = ob[kind == "swa"]
                opens = kind == "cmp" or (kind == "swa" and kt == 0)
                if opens:
                    n = sum(c < t for c in CLOSES)
                    if n >= 2:
                        pe.wait_ge(s_om, n - 1)
                pe.wait_ge(s_lo, t + 1)
                if kind == "cmp":
                    last = pe.matmul(dst, vc[:, g, :], pct[:], start=True, stop=False)
                else:
                    typ = {"win": WIN, "sel": SLC, "swa": SWA}[kind]
                    first, width = keys(kind, i)
                    tile = first // P + kt
                    both = v[:, typ, tile, g].rearrange("p e d -> p (e d)")
                    pe.matmul(dst, both, pt_hi[t % 3][:], start=opens, stop=False)
                    last = pe.matmul(dst, both, lo_part(t), start=False, stop=t in CLOSES)
                last.then_inc(s_pv, 1)

            def project(x):
                par, k = divmod(x, KD)
                if k == 0:
                    pe.wait_ge(s_wl, U_OUT + par + 1)
                    pe.wait_ge(s_sc, len(ITEMS))
                    pe.wait_ge(s_oev, len(CLOSES) // 2)
                dst, toks = mp[par][:, 0:HALF], halves[0]
                pe.matmul(dst, w_hi[par][:, k, :], qa[:, 2 * k, toks], start=(k == 0), stop=False)
                pe.matmul(dst, w_hi[par][:, k, :], qa[:, 2 * k + 1, toks], start=False, stop=False)
                last = pe.matmul(dst, w_lo[par][:, k, :], qa[:, 2 * k, toks], start=False, stop=(k == KD - 1))
                if k == KD - 1:
                    last.then_inc(s_mm, 1)

            for what, n in ORDER["PE"]:
                {"scores": scores, "turn": turn, "weigh": weigh, "project": project}[what](n)

            for hf in range(2):
                toks = slice(hf * HALF, (hf + 1) * HALF)
                if hf:
                    pe.wait_ge(s_oev, len(CLOSES))
                for c in range(KD):
                    u = U_OUT + hf * KD + c
                    if u < U_OUT + 2:
                        continue

                    def before(k):
                        if hf == 1 and c == 0 and k == 3:
                            pe.wait_ge(s_one, 1)
                            pe.wait_ge(s_nq, KD)
                            row_sums(pt[0], nacc[:, 0, :])
                        if hf == 1 and c == 0 and k == KD - 1:
                            spread(2, ob[0], nacc[:, 0, :])
                    unit(u, u % 2, [mp[u % 2][:, 0:HALF]], [lambda k: qa[:, 2 * k, toks]], [lambda k: qa[:, 2 * k + 1, toks]], before)

            def up(u, par, before_k=None):
                unit(u, par, [mp[par][:, t] for t in halves], [(lambda k, t=t: m_hi[:, k, t]) for t in halves],
                     [(lambda k, t=t: m_lo[:, k, t]) for t in halves], before_k)

            def down(u, par, q):
                def before(k):
                    if par == 0 and k in (0, KD - 1):
                        pe.wait_ge(s_ul, q * FQ + (FQ - 1 if k == 0 else FQ))
                unit(u, par, [mp[par][:, t] for t in halves], [(lambda k, t=t: u_hi[:, k, t]) for t in halves],
                     [(lambda k, t=t: u_lo[:, k, t]) for t in halves], before)

            def add_row_sums(c):
                pe.wait_ge(s_hs, KD + c + 1)
                for t in range(4):
                    last = pe.matmul(pt[1][:, 8 + t:9 + t], hsq[:, (KD + c) % 3, t * P:(t + 1) * P], ones[:, 0:1],
                                     start=(c == 0 and t == 0), stop=(c == KD - 1 and t == 3))
                last.then_inc(s_sum if c == KD - 1 else s_hq, 1)

            for hf in range(2):
                for par in range(2):
                    u = U_MLP + par
                    if hf == 0:
                        pe.wait_ge(s_wl, u + 1)
                        pe.wait_ge(s_ev, u - 1)
                    for k in range(KD):
                        if par == 0:
                            pe.wait_ge(s_ml, hf * KD + k + 1)
                        if (hf, par, k) == (0, 0, 2):
                            pe.wait_ge(s_nq, 2 * KD)
                            row_sums(pt[1], nacc[:, 1, :])
                        if (hf, par, k) == (0, 0, KD - 1):
                            spread(3, ob[1], nacc[:, 1, :])
                        if (hf, par, k) == (0, 1, 2):
                            pe.wait_ge(s_ha, KD)
                            row_sums(pt[0][:, 8:12], hacc[:, 0:HALF])
                        if (hf, par, k) == (1, 0, KD - 1):
                            spread(4, pt[0], hacc[:, halves[0]])
                        if (hf, par, k) == (1, 1, 3):
                            spread(5, pt[1], hacc[:, halves[1]])
                        dst, a, b = mp[par][:, halves[hf]], m_hi[:, k, halves[hf]], m_lo[:, k, halves[hf]]
                        pe.matmul(dst, w_hi[par][:, k, :], a, start=(k == 0), stop=False)
                        pe.matmul(dst, w_hi[par][:, k, :], b, start=False, stop=False)
                        last = pe.matmul(dst, w_lo[par][:, k, :], a, start=False, stop=(k == KD - 1))
                        if (hf, par) == (1, 0) and k:
                            add_row_sums(k - 1)
                    if hf == 1:
                        last.then_inc(s_mm, 1)
                    if (hf, par) == (1, 0):
                        add_row_sums(KD - 1)
            with pe.Fori(1, FQ // 2) as j:
                for par in range(2):
                    up(2 * j + (U_MLP + par), par)
            with pe.Fori(0, FQ // 2) as j:
                for par in range(2):
                    down(2 * j + (U_MLP + FQ + par), par, 0)
            def quarter(q, last):
                with pe.Fori(0, FQ // 2) as j:
                    for par in range(2):
                        up(q * (2 * FQ) + 2 * j + (U_MLP + par), par)
                if not last:
                    with pe.Fori(0, FQ // 2) as j:
                        for par in range(2):
                            down(q * (2 * FQ) + 2 * j + (U_MLP + FQ + par), par, q)

            with pe.Fori(1, QUARTERS - 1) as q:
                quarter(q, False)
            quarter(QUARTERS - 1, True)

            def last_sums(src, start, stop):
                for t in range(4):
                    last = pe.matmul(ob[1][:, t:t + 1], src[:, t * P:(t + 1) * P], ones[:, 0:1], start=start and t == 0,
                                     stop=stop and t == 3)
                return last

            for n in range(2 * KD):
                def before(k):
                    if n == 0 and k in (0, KD - 1):
                        pe.wait_ge(s_ul, QUARTERS * FQ - (k == 0))
                    if n == KD and k == 5:
                        pe.wait_ge(s_fa, KD)
                        row_sums(ob[0], facc[:, halves[0]])
                    if n == KD and k == KD - 1:
                        spread(6, pt[0], facc[:, halves[0]])
                    if n == 2 * KD - 1 and k == KD - 1:
                        pe.wait_ge(s_fa, 2 * KD - 1)
                        last_sums(facc[:, halves[1]], True, False)
                u, toks = U_LAST + n, halves[n // KD]
                unit(u, u % 2, [mp[u % 2][:, toks]], [lambda k: u_hi[:, k, toks]], [lambda k: u_lo[:, k, toks]], before)
            pe.wait_ge(s_fs, 2 * KD)
            last_sums(fsq[:, 1, 0:HALF], False, True).then_inc(s_sum, 1)
            spread(7, pt[1], facc[:, halves[1]])

        @block.scalar
        def _(act):
            copy = lambda dst, src, **kw: act.activation(dst, src, ACT.Copy, **kw)

            def split_w(u, par=None):
                if par is None:
                    par = u % 2
                act.wait_ge(s_w[par], 8 * u + (16 - 8 * par))
                if not isinstance(u, int) or u >= 2:
                    act.wait_ge(s_mm, u - 1)
                copy(w_hi[par][:], w_raw[par][:]).then_inc(s_wh, 1)

            def std(n, src):
                act.wait_ge(s_sum, n + 1)
                at = 4 * (n % 2)
                act.activation(rs[:, at:at + 4], src[:, 0:4], ACT.Sqrt, bias=eps[:, 0:1], scale=1.0 / D_MODEL).then_inc(s_std, 1)

            act.dma_start(gain[:], gains).then_inc(s_gain, 16)
            act.wait_ge(s_zero, 1)
            copy(rs[:, 0:1], eps[:, 0:1])
            act.wait_ge(s_gain, 16)
            zn = [0]
            def convert_x(hf):
                def parts(k):
                    n = hf * KD + k
                    act.wait_ge(s_x[k], 16 * (hf + 1))
                    if hf:
                        act.wait_ge(*((s_xu, k + 1) if k < KD - 1 else (s_mm, N_IN)))
                    copy(x_hi[:, k, :], x_in[k], scale=gain[:, 0, k:k + 1]).then_inc(s_xh, 1)

                def square(k):
                    n = hf * KD + k
                    if n >= 2:
                        act.wait_ge(s_xq, n - 1)
                    act.activation(sq[n % 2][:], x_in[k], ACT.Square).then_inc(s_sq, 1)

                for what, k in TAKE_X[hf]:
                    {"parts": parts, "square": square, "slab": split_w, "project": lambda j: project(0, j)}[what](k)

            def project(hf, j):
                u = hf * N_IN + j
                if hf and j in (6, 7):
                    kv = j - 6
                    act.wait_ge(s_hp, kv + 1)
                    src = pt[kv][:, 0:2 * P].rearrange("p (h n) -> p h n", h=2)[:, :, 0:2 * N_CMP]
                    act.activation(hid[kv][:], src, ACT.Gelu_apprx_tanh).then_inc(s_hid, 1)
                if hf and j == 8:
                    act.wait_ge(s_kcp, 1)
                    copy(kc_hi[:, :, 0:N_CMP], ob[0][:, 0:2 * N_CMP].rearrange("p (g n) -> p g n", g=2)).then_inc(s_kch, 1)
                if u + 2 < U_OUT and u != N_IN - 1:
                    split_w(u + 2)
                if j == GATES:
                    act.wait_ge(s_ev, u + 1)
                    act.activation(zv[:, 3, :], zv[:, 3, :], ACT.Sigmoid).then_inc(s_sig, 1)
                if j == GATES + 3:
                    for n in range(3):
                        act.wait_ge(s_vt, 4 * hf + n + 1)
                        copy(v[:, [SWA, SLC, WIN][n], 4 * hf:4 * hf + 4, :, 0, :],
                             tp[n].rearrange("p (t g d) -> p t g d", t=4, g=GROUPS)).then_inc(s_vh, 1)
                is_k = j in (KS_SWA, K_SLC, K_WIN)
                if is_k or j >= N_KV_CHUNKS:
                    toks = slice(hf * HALF, (hf + 1) * HALF)
                    act.wait_ge(s_ev, u + 1)
                    if zn[0]:
                        act.wait_ge(s_zl, zn[0])
                    copy(z_hi[:], z[:]).then_inc(s_zh, 1)
                    for g in range(2):
                        src = z[g * HD:(g + 1) * HD, :]
                        if is_k:
                            typ = {KS_SWA: SWA, K_SLC: SLC, K_WIN: WIN}[j]
                            copy(k_hi[0:HD, typ, g, toks], src)
                            last = copy(k_hi[HD:P, typ, g, toks], src)
                        else:
                            last = copy(qa[0:HD, 2 * (j - N_KV_CHUNKS) + g, toks], src)
                    last.then_inc(s_za, 1)
                    zn[0] += 1


            split_w(0)
            convert_x(0)
            std(0, ob[0])
            for j in range(N_IN - 1):
                project(0, j)
            convert_x(1)
            std(1, ob[0])
            for j in range(N_IN):
                project(1, j)

            def exp_item(n):
                b, h = ITEMS[n]
                kind, i, g = BLOCKS[b]
                base = g * HPG + (8 if kind == "swa" else 0)
                act.wait_ge(s_sc, n + 1)
                for r in (range(HPG) if h is None else [h]):
                    if h is None:
                        p = probc[SLOT[b]][:, r * CMP_PAD:(r + 1) * CMP_PAD]
                    else:
                        p = prob[:, SLOT[b], r, 0:keys(kind, i)[1]]
                    act.activation(p, p, ACT.Exp, bias=nmax[:, b % 4, r:r + 1], scale=-1.0,
                                   accum_out=den[:, b % 4, r:r + 1]).then_inc(s_exp, 1)
                if kind == "swa" and h == HPG - 1:
                    act.wait_ge(s_ns, i * GROUPS + g + 1)
                    act.activation(esink[:, b % 4, :], esink[:, b % 4, :], ACT.Exp).then_inc(s_exp, 1)

            def turned_hi(t):
                b, kt = STEPS[t]
                act.wait_ge(s_tr, t + 1)
                if t >= 3:
                    act.wait_ge(s_pv, t - 2)
                if BLOCKS[b][0] == "cmp":
                    if b >= 4:
                        act.wait_ge(s_pv, STEP_END[b - 4])
                    copy(pct[:, 0:256], pt[t % 2][0:CMP_PAD, 0:256]).then_inc(s_hi, 1)
                else:
                    copy(pt_hi[t % 3][:], pt[t % 2]).then_inc(s_hi, 1)

            def mixed_copy(t):
                kind, i, g = BLOCKS[STEPS[t][0]]
                act.wait_ge(s_pv, t + 1)
                if CLOSE_NO[t]:
                    act.wait_ge(s_oev, CLOSE_NO[t])
                src = ob[kind == "swa"][0:HD, :].rearrange("p (c e q) -> p e c q", c=2, e=2)
                for e in range(2):
                    last = copy(mixed[e * HD:(e + 1) * HD], src[:, e])
                last.then_inc(s_oa, 1)

            def mixed_hi(t):
                kind, i, g = BLOCKS[STEPS[t][0]]
                act.wait_ge(s_om, CLOSE_NO[t] + 1)
                h0 = (8 if kind == "swa" else 0) + g * HPG
                copy(qa[:, h0:h0 + HPG:2, i * P:(i + 1) * P], mixed[:]).then_inc(s_oh, 1)

            def first_slab(par):
                last = LAST["win" if par else "cmp", 1]
                if par < 2:
                    act.wait_ge(s_pv, STEP_END[last])
                    act.wait_ge(s_sc, ITEM_END[last])
                split_w(U_OUT + par)

            for what, n in ORDER["ACT"]:
                {"exp": exp_item, "hi": turned_hi, "out_copy": mixed_copy, "out_hi": mixed_hi, "w_hi": first_slab}[what](n)

            def norm_act(n):
                c, hf = n % KD, n // KD
                h = y[:, c, halves[hf]]
                act.wait_ge(*((s_h[0], n // 2 + 1) if n in (0, 2, 4, 6) else (s_h[1], n // 2 + 1 if n < KD else n - 3)))
                copy(m_hi[:, c, halves[hf]], h, scale=gain[:, 2, c:c + 1]).then_inc(s_mh, 1)
                act.dma_start(h_dram[c, :, halves[hf]], h).then_inc(s_hst, 16)
                if n + 4 < 2 * KD:
                    c4, hf4 = (n + 4) % KD, (n + 4) // KD
                    act.dma_start(nx[:, n % 4, :], xT[c4, :, halves[hf4]]).then_inc(s_nx[n % 4], 16)

            def square_h(n):
                c, hf = n % KD, n // KD
                if n >= KD + 3:
                    act.wait_ge(s_hq, n - KD - 2)
                elif n >= 3:
                    act.wait_ge(s_ha, n - 2)
                act.activation(hsq[:, n % 3, :], y[:, c, halves[hf]], ACT.Square).then_inc(s_hs, 1)

            act.wait_ge(s_lo, len(STEPS))
            for n in range(2 * KD):
                c, hf = n % KD, n // KD
                u = U_OUT + n
                act.wait_ge(s_mm, u + 1)
                if n >= 2:
                    act.wait_ge(s_nq, n - 1)
                if 0 < n and c < KD - 1:
                    split_w(u + 2)
                act.activation(nsq[:, n % 2, :], mp[u % 2][:, 0:HALF], ACT.Square).then_inc(s_y, 1)
                copy(y[:, c, halves[hf]], mp[u % 2][:, 0:HALF]).then_inc(s_ev, 1)
                if c == KD - 1:
                    split_w(u + 2)
                if n == KD - 1:
                    std(2, pt[0])
                for m in NORMS_WITH.get(n - 1 - KD, []):
                    norm_act(m)
                    square_h(m)
            std(3, pt[1])
            for n in range(KD, 2 * KD):
                norm_act(n)
                if n >= KD + 3:
                    square_h(n - 3)
                if n == KD + 4:
                    std(4, pt[0][:, 8:12])
            for n in range(2 * KD - 3, 2 * KD):
                square_h(n)

            def up_act(u, par, f, done):
                split_w(u + 2, par)
                act.wait_ge(s_u, done)
                copy(u_hi[:, bass.ds(f, 1), :].rearrange("p a t -> p (a t)"), uz[:, par, :]).then_inc(s_uh, 1)

            def quarter(q, last):
                u0 = q * (2 * FQ) + U_MLP
                with act.Fori(0, FQ // 2) as j:
                    for par in range(2):
                        f = 2 * j + par
                        up_act(u0 + f, par, f, q * FQ + f + 1)
                if not last:
                    with act.Fori(0, FQ // 2) as j:
                        for par in range(2):
                            split_w(u0 + 2 * j + (FQ + par + 2), par)

            std(5, pt[1][:, 8:12])
            quarter(0, False)
            with act.Fori(1, QUARTERS - 1) as q:
                quarter(q, False)
            quarter(QUARTERS - 1, True)

            act.wait_ge(s_hst, 16 * 2 * KD)
            act.wait_ge(s_ul, QUARTERS * FQ)
            for n in range(2 * KD):
                c, u, toks = n % KD, U_LAST + n, halves[n // KD]
                act.wait_ge(s_mm, u + 1)
                act.dma_start(fh[:, c, toks], h_dram[c, :, toks]).then_inc(s_fh[n // KD], 16)
                if u + 2 < N_UNITS:
                    split_w(u + 2)
                act.wait_ge(s_ev, u + 1)
                if n >= 2:
                    act.wait_ge(s_fa, n - 1)
                act.activation(fsq[:, n % 2, 0:HALF], yacc[:, c, toks], ACT.Square).then_inc(s_fs, 1)
                if n == KD - 1:
                    std(6, ob[0])
            std(7, ob[1])

        @block.vector
        def _(dve):
            TT, STT, TS = dve.tensor_tensor, dve.scalar_tensor_tensor, dve.tensor_scalar
            f32 = lambda ap: ap.bitcast(F32)
            chain = [0]

            def link(ins):
                ins.then_inc(s_dc, 1)
                chain[0] += 1
                dve.wait_ge(s_dc, chain[0])

            def diagonal(n, dst):
                at = 4 * (n % 2)
                dve.wait_ge(s_std, n + 1)
                link(dve.reciprocal(rs[:, at:at + 4], rs[:, at:at + 4]))
                TT(dst.rearrange("p (t q) -> p t q", t=4), ident[:].unsqueeze(1).to_broadcast([P, 4, P]),
                   rs[:, at:at + 4].unsqueeze(2).to_broadcast([P, 4, P]), ALU.mult).then_inc(s_diag, 1)

            def split_w(u, par=None):
                if par is None:
                    par = u % 2
                dve.wait_ge(s_wh, u + 1)
                TT(w_lo[par][:], w_raw[par][:], f32(w_hi[par][:]), ALU.subtract).then_inc(s_wl, 1)

            dve.memset(eps[:], EPS)
            dve.memset(f32(kc_hi[:]), 0.0)
            dve.memset(f32(kc_lo[:]), 0.0).then_inc(s_zero, 1)
            dve.wait_ge(s_gain, 16)

            zn = [0]

            def convert_x(hf):
                def parts(k):
                    n = hf * KD + k
                    dve.wait_ge(s_xh, n + 1)
                    STT(x_lo[:, k, :], x_in[k], gain[:, 0, k:k + 1], f32(x_hi[:, k, :]), ALU.mult,
                        ALU.subtract).then_inc(s_xl, 1)

                def square(k):
                    n = hf * KD + k
                    dve.wait_ge(s_sq, n + 1)
                    if k:
                        dve.wait_ge(s_xq, n)
                        TT(xacc[:], xacc[:], sq[n % 2][:], ALU.add).then_inc(s_xq, 1)
                    else:
                        dve.tensor_copy(xacc[:], sq[n % 2][:]).then_inc(s_xq, 1)

                for what, k in TAKE_X[hf]:
                    {"parts": parts, "square": square, "slab": split_w, "project": lambda j: project(0, j)}[what](k)

            def blocks(kv):
                dve.wait_ge(s_cw, 16 * 12)
                dve.wait_ge(s_ev, N_IN + (VC_ if kv else KC) + 1)
                for c in range(4):
                    late, q = c // 2, c % 2 * 4
                    dst = blk_at[kv][:, c, :].rearrange("p (q g n) -> p q g n", q=4, g=GROUPS)
                    src = zkv[:, kv, q:q + 4, :, late:late + N_CMP]
                    emb = pe_sb[:, kv, 4 * c:4 * c + 4].unsqueeze(2).unsqueeze(3).to_broadcast([P, 4, GROUPS, N_CMP])
                    last = TT(dst, src, emb, ALU.add)
                    if c % 2:
                        last.then_inc(s_blk, 1)

            def project(hf, j):
                u = hf * N_IN + j
                if hf and j == 8:
                    dve.wait_ge(s_kch, 1)
                    TT(kc_lo[:, :, 0:N_CMP], ob[0][:, 0:2 * N_CMP].rearrange("p (g n) -> p g n", g=2),
                       f32(kc_hi[:, :, 0:N_CMP]), ALU.subtract)
                    dve.wait_ge(s_kcp, 2)
                    link(dve.memset(vc, 0.0))
                    dve.tensor_copy(vc[0:N_CMP, :, 0:HD], ob[1][0:N_CMP, 0:P].rearrange("p (g n) -> p g n", g=2)).then_inc(s_kcl, 1)
                if u + 2 < U_OUT and u != N_IN - 1:
                    split_w(u + 2)
                if hf and j in (KC + 1, VC_ + 1):
                    blocks(j - KC - 1)
                if j == 0:
                    dve.wait_ge(s_rstd, hf + 1)
                    link(dve.tensor_copy(rstd[:], stat))
                dve.wait_ge(s_mm, u + 1)
                src = mp[u % 2][:, 0:HALF]
                toks = slice(hf * HALF, (hf + 1) * HALF)
                if j in (VT_SWA, VT_SLC, VT_WIN, GATES):
                    n = {VT_SWA: 0, VT_SLC: 1, VT_WIN: 2, GATES: 3}[j]
                    if hf:
                        dve.wait_ge(s_vt, 4)
                    TT(zv[:, n, :], src, rstd[:], ALU.mult).then_inc(s_ev, 1)
                elif j in (KC, VC_):
                    kv = int(j == VC_)
                    for g in range(GROUPS):
                        rows = slice(g * HD, (g + 1) * HD)
                        a = src[rows, :].rearrange("p (n q e) -> p e q n", q=8, e=2)
                        b = rstd[rows, :].rearrange("p (n q e) -> p e q n", q=8, e=2)
                        for e in range(2):
                            last = TT(zkv[e * HD:(e + 1) * HD, kv, :, g, hf * 32:hf * 32 + 32], a[:, e], b[:, e], ALU.mult)
                    last.then_inc(s_ev, 1)
                else:
                    if zn[0]:
                        dve.wait_ge(s_za, zn[0])
                        dve.wait_ge(s_zl, zn[0])
                    if j < N_KV_CHUNKS:
                        TT(z[:], src, rstd[:], ALU.mult).then_inc(s_ev, 1)
                    else:
                        c = j - N_KV_CHUNKS
                        STT(z[:], src, qscale[:, c:c + 1], rstd[:], ALU.mult, ALU.mult).then_inc(s_ev, 1)
                    dve.wait_ge(s_ev, u + 1)
                    dve.wait_ge(s_zh, zn[0] + 1)
                    for g in range(2):
                        rows = slice(g * HD, (g + 1) * HD)
                        if j < N_KV_CHUNKS:
                            typ = {KS_SWA: SWA, K_SLC: SLC, K_WIN: WIN}[j]
                            TT(k_lo[0:HD, typ, g, toks], z[rows, :], f32(z_hi[rows, :]), ALU.subtract)
                            last = TT(k_lo[HD:P, typ, g, toks], z[rows, :], f32(z_hi[rows, :]), ALU.subtract)
                        else:
                            last = TT(qa[HD:P, 2 * (j - N_KV_CHUNKS) + g, toks], z[rows, :], f32(z_hi[rows, :]), ALU.subtract)
                    last.then_inc(s_zl, 1)
                    zn[0] += 1
                if j == GATES + 3:
                    for n in range(3):
                        dve.wait_ge(s_vh, 3 * hf + n + 1)
                        hi, lo = (v[:, [SWA, SLC, WIN][n], 4 * hf:4 * hf + 4, :, e, :] for e in range(2))
                        TT(lo, tp[n].rearrange("p (t g d) -> p t g d", t=4, g=GROUPS), f32(hi), ALU.subtract).then_inc(s_vl, 1)
                    dve.wait_ge(s_vt, 4 * hf + 4)
                    dve.tensor_copy(gate[:, 4 * hf:4 * hf + 4, :],
                                    tp[3].rearrange("p (t c) -> p t c", t=4)[:, :, 0:24]).then_inc(s_vl, 1)

            split_w(0)
            convert_x(0)
            dve.wait_ge(s_const, 16 * 4)
            link(TS(nsink[:], sink[:], -1.0, None, ALU.mult))
            diagonal(0, xacc[:])
            for j in range(N_IN - 1):
                project(0, j)
            convert_x(1)
            diagonal(1, xacc[:])
            for j in range(N_IN):
                project(1, j)

            dve.wait_ge(s_tab, 16 * 5)

            def score_item(n):
                b, h = ITEMS[n]
                kind, i, g = BLOCKS[b]
                dve.wait_ge(s_S, n + 1)
                if SLOT_BEFORE[b] is not None:
                    dve.wait_ge(s_tr, STEP_END[SLOT_BEFORE[b]])
                for r in (range(HPG) if h is None else [h]):
                    if kind == "cmp":
                        src = banks[:, BANK[n] * HALF + r * CMP_PAD:BANK[n] * HALF + (r + 1) * CMP_PAD]
                        dst = probc[SLOT[b]][:, r * CMP_PAD:(r + 1) * CMP_PAD]
                        table, head, floor = t_c[:, 8 * (NT - 1 - i):8 * (NT - 1 - i) + CMP_PAD], g * HPG + r, NO_KEY
                    else:
                        first, width = keys(kind, i)
                        src, dst = banks[:, BANK[n] * HALF:BANK[n] * HALF + width], prob[:, SLOT[b], r, 0:width]
                        head, floor = g * HPG + r, 3e38
                        if kind == "swa":
                            table, head, floor = t_s[:, 256 - width:256], 8 + head, nsink[:, g * HPG + r:g * HPG + r + 1]
                        elif kind == "win":
                            table = t_w[:, 640 - width:640]
                        elif i < 4:
                            table = t_d[:, SEQ - width:SEQ]
                        else:
                            dve.wait_ge(s_wm, SELECTS.index((i, g)) + 1)
                            table = wmask[:, g, 0:width]
                    last = dve.tensor_tensor_reduce(dst, src, table, -SL[head], floor, ALU.add, ALU.min, nmax[:, b % 4, r:r + 1])
                last.then_inc(s_sc, 1)
                if kind == "swa" and h == HPG - 1:
                    dve.wait_ge(s_sc, n + 1)
                    TT(esink[:, b % 4, :], nmax[:, b % 4, :], sink[:, g * HPG:(g + 1) * HPG], ALU.add).then_inc(s_ns, 1)

            def post(x):
                b, k = x
                kind, i, g = BLOCKS[b]
                d, r = den[:, b % 4, :], rgate[:, b % 4, :]
                gates = gate[:, i, g * 12:(g + 1) * 12].rearrange("p (h k) -> p k h", k=3)
                last = k == n_posts(b) - 1
                if k:
                    dve.wait_ge(s_dc, chain[0])
                else:
                    dve.wait_ge(s_exp, EXP_END[b])
                if kind == "cmp":
                    pr = probc[SLOT[b]][:].rearrange("p (h n) -> p h n", h=HPG)
                    wide = lambda ap: ap.unsqueeze(2).to_broadcast([P, HPG, CMP_PAD])
                    if k == 0:
                        step = TS(d, d, 1e-30, None, ALU.max)
                    elif k == 1:
                        step = dve.reciprocal(r, d)
                    elif k == 2:
                        step = TT(pr, pr, wide(r), ALU.mult)
                    elif last:
                        step = TT(pr, pr, wide(gates[:, 0, :]), ALU.mult)
                    elif k == 3:
                        step = dve.tensor_reduce(pall[:], pr.rearrange("p h n -> p n h"), AX.X, ALU.add)
                    elif k == 4:
                        step = dve.tensor_reduce(imp[:], pall[:].rearrange("p (j r) -> p j r", r=4), AX.X, ALU.add)
                    elif k == 5:
                        step = TT(imp[:, 1:N_SEL], imp[:, 1:N_SEL], pall[:, 3:CMP_PAD - 1:4], ALU.add)
                    elif k == 6:
                        step = TT(score[:], imp[:], force[:, i - 4, :], ALU.add)
                    elif k == 7:
                        step = dve.max(top8[:], score[:])
                    elif k == 8:
                        step = dve.match_replace(picked[:], top8[:], score[:], TAKEN)
                    else:
                        n = SELECTS.index((i, g))
                        if n >= 2:
                            dve.wait_ge(s_wm, n - 1)
                        step = TS(selmask[:, g, :], picked[:], 1.5e30, NEG, ALU.is_lt, ALU.mult)
                elif k == 0:
                    step = TT(d, d, esink[:, b % 4, :], ALU.add) if kind == "swa" else dve.reciprocal(r, d)
                elif kind == "swa":
                    step = dve.reciprocal(r, d)
                else:
                    step = TT(r, r, gates[:, 2 if kind == "win" else 1, :], ALU.mult)
                if last:
                    step.then_inc(s_post, 1)
                else:
                    step.then_inc(s_dc, 1)
                    chain[0] += 1

            def turned_lo(t):
                b, kt = STEPS[t]
                dve.wait_ge(s_hi, t + 1)
                if BLOCKS[b][0] == "cmp":
                    dve.tensor_copy(pct[:, 256:HALF], pt[t % 2][0:CMP_PAD, 256:HALF]).then_inc(s_lo, 1)
                else:
                    TT(lo_part(t), pt[t % 2], f32(pt_hi[t % 3][:]), ALU.subtract).then_inc(s_lo, 1)

            def mixed_add(t):
                kind = BLOCKS[STEPS[t][0]][0]
                src = ob[kind == "swa"][HD:P, :].rearrange("p (c e q) -> p e c q", c=2, e=2)
                dve.wait_ge(s_oa, CLOSE_NO[t] + 1)
                for e in range(2):
                    rows = slice(e * HD, (e + 1) * HD)
                    last = TT(mixed[rows], src[:, e], mixed[rows], ALU.add)
                last.then_inc(s_om, 1)

            def first_slab(par):
                dve.wait_ge(s_sc, ITEM_END[LAST["win", 1]])
                dve.wait_ge(s_wm, len(SELECTS))
                split_w(U_OUT + par)

            for what, n in ORDER["DVE"]:
                {"take": score_item, "post": post, "lo": turned_lo, "out_mix": mixed_add, "w_lo": first_slab}[what](n)

            def norm_dve(n):
                c, hf = n % KD, n // KD
                h = y[:, c, halves[hf]]
                STT(h, h, gain[:, 1, c:c + 1], ob[hf], ALU.mult, ALU.mult).then_inc(s_t, 1)
                if hf == 0 and n % 2 == 0:
                    dve.wait_ge(s_nx[n % 4], 16 * (n // 4 + 1))
                    dve.wait_ge(s_t, n + 1)
                    TT(h, h, nx[:, n % 4, :], ALU.add).then_inc(s_h[0], 1)

            def norm_lo(n):
                c, hf = n % KD, n // KD
                dve.wait_ge(s_mh, n + 1)
                STT(m_lo[:, c, halves[hf]], y[:, c, halves[hf]], gain[:, 2, c:c + 1], f32(m_hi[:, c, halves[hf]]), ALU.mult,
                    ALU.subtract).then_inc(s_ml, 1)

            for n in range(2 * KD):
                if 0 < n and n % KD < KD - 1:
                    split_w(U_OUT + n + 2)
                dve.wait_ge(s_y, n + 1)
                dst = nacc[:, n // KD, :]
                if n % KD:
                    dve.wait_ge(s_nq, n)
                    TT(dst, dst, nsq[:, n % 2, :], ALU.add).then_inc(s_nq, 1)
                else:
                    dve.tensor_copy(dst, nsq[:, n % 2, :]).then_inc(s_nq, 1)
                if n % KD == KD - 1:
                    split_w(U_OUT + n + 2)
                if n == KD - 1:
                    diagonal(2, nacc[:, 0, :])
                if n == KD:
                    dve.wait_ge(s_rstd, 3)
                for m in NORMS_WITH.get(n - KD, []):
                    norm_dve(m)
                for m in NORMS_WITH.get(n - 2 - KD, []):
                    norm_lo(m)
            norm_lo(KD - 1)
            diagonal(3, nacc[:, 1, :])
            dve.wait_ge(s_rstd, 4)
            for n in range(KD, 2 * KD):
                norm_dve(n)
                if n >= KD + 2:
                    norm_lo(n - 2)
                if n == KD + 6:
                    diagonal(4, hacc[:, 0:HALF])
            norm_lo(2 * KD - 2)
            norm_lo(2 * KD - 1)
            diagonal(5, hacc[:, HALF:SEQ])

            def up_dve(u, par, f, done):
                dve.wait_ge(s_mm, u + 1)
                TT(uz[:, par, :], mp[par], hacc[:], ALU.mult).then_inc(s_ev, 1)
                dve.wait_ge(s_ev, u + 1)
                STT(uz[:, par, :], uz[:, par, :], 0.0, uz[:, par, :], ALU.max, ALU.mult).then_inc(s_u, 1)
                split_w(u + 2, par)
                dve.wait_ge(s_uh, done)
                flat = lambda ap: ap.rearrange("p a t -> p (a t)")
                TT(flat(u_lo[:, bass.ds(f, 1), :]), uz[:, par, :], flat(f32(u_hi[:, bass.ds(f, 1), :])),
                   ALU.subtract).then_inc(s_ul, 1)

            def down_dve(u, par, c, first):
                dve.wait_ge(s_mm, u + 1)
                dst = yacc[:, bass.ds(c, 1), :].rearrange("p a t -> p (a t)")
                if first:
                    dve.tensor_copy(dst, mp[par]).then_inc(s_ev, 1)
                else:
                    TT(dst, dst, mp[par], ALU.add).then_inc(s_ev, 1)

            def quarter(q, first, last):
                u0 = q * (2 * FQ) + U_MLP
                with dve.Fori(0, FQ // 2) as j:
                    for par in range(2):
                        f = 2 * j + par
                        up_dve(u0 + f, par, f, q * FQ + f + 1)
                if not last:
                    with dve.Fori(0, FQ // 2) as j:
                        for par in range(2):
                            c = 2 * j + par
                            split_w(u0 + c + (FQ + 2), par)
                            down_dve(u0 + c + FQ, par, c, first)

            for t in range(2):
                dve.wait_ge(s_rstd, 5 + t)
                link(dve.tensor_copy(hacc[:, halves[t]], pt[t]))
            dve.wait_ge(s_hst, 16 * 2 * KD)
            dve.wait_ge(s_h[1], 12)
            quarter(0, True, False)
            with dve.Fori(1, QUARTERS - 1) as q:
                quarter(q, False, False)
            quarter(QUARTERS - 1, False, True)

            def norm_out(n):
                c, hf = n % KD, n // KD
                y2 = yacc[:, c, halves[hf]]
                STT(y2, y2, gain[:, 3, c:c + 1], pt[hf], ALU.mult, ALU.mult).then_inc(s_ft, 1)
                if hf and c not in POOL_ADDS:
                    dve.wait_ge(s_ft, n + 1)
                    TT(y2, y2, fh[:, c, halves[hf]], ALU.add).then_inc(s_fo, 1)

            for n in range(2 * KD):
                c, hf, u = n % KD, n // KD, U_LAST + n
                toks = halves[hf]
                dve.wait_ge(s_mm, u + 1)
                TT(yacc[:, c, toks], yacc[:, c, toks], mp[u % 2][:, toks], ALU.add).then_inc(s_ev, 1)
                if u + 2 < N_UNITS:
                    split_w(u + 2)
                if n < 2 * KD - 1:
                    dve.wait_ge(s_fs, n + 1)
                    dst = facc[:, toks]
                    if c:
                        dve.wait_ge(s_fa, n)
                        TT(dst, dst, fsq[:, n % 2, 0:HALF], ALU.add).then_inc(s_fa, 1)
                    else:
                        dve.tensor_copy(dst, fsq[:, n % 2, 0:HALF]).then_inc(s_fa, 1)
                if n == KD - 1:
                    diagonal(6, facc[:, halves[0]])
                if n == KD:
                    dve.wait_ge(s_rstd, 7)
                for m in LAST_WITH.get(n - KD, []):
                    norm_out(m)
            diagonal(7, facc[:, halves[1]])
            dve.wait_ge(s_rstd, 8)
            dve.wait_ge(s_fh[1], 16 * KD)
            for n in range(KD, 2 * KD):
                norm_out(n)

        @block.gpsimd
        def _(pool):
            def scale(b):
                kind, i, g = BLOCKS[b]
                if kind == "cmp":
                    if i >= 4:
                        n = SELECTS.index((i, g))
                        width = (i + 1) * P
                        pool.wait_ge(s_post, b + 1)
                        if i > 4:
                            pool.wait_ge(s_sc, ITEM_END[BLOCKS.index(("sel", i - 1, g))])
                        pool.tensor_tensor(wmask[:, g, 0:width].rearrange("p (j t) -> p j t", t=HD),
                                           t_d[:, SEQ - width:SEQ].rearrange("p (j t) -> p j t", t=HD),
                                           selmask[:, g, 0:width // HD].unsqueeze(2).to_broadcast([P, width // HD, HD]),
                                           ALU.add).then_inc(s_wm, 1)
                else:
                    width = keys(kind, i)[1]
                    pool.wait_ge(s_post, b + 1)
                    for r in range(HPG):
                        pr = prob[:, SLOT[b], r, 0:width]
                        last = pool.tensor_scalar(pr, pr, rgate[:, b % 4, r:r + 1], 0.0, ALU.mult, ALU.add)
                    last.then_inc(s_p, 1)

            def mixed_lo(t):
                kind, i, g = BLOCKS[STEPS[t][0]]
                pool.wait_ge(s_oh, CLOSE_NO[t] + 1)
                h0, toks = (8 if kind == "swa" else 0) + g * HPG, slice(i * P, (i + 1) * P)
                pool.tensor_tensor(qa[:, h0 + 1:h0 + HPG:2, toks], mixed[:], qa[:, h0:h0 + HPG:2, toks].bitcast(F32),
                                   ALU.subtract).then_inc(s_oev, 1)

            for what, n in ORDER["POOL"]:
                {"scale": scale, "out_lo": mixed_lo}[what](n)

            pool.wait_ge(s_oev, len(CLOSES))
            pool.wait_ge(s_pv, len(STEPS))
            pool.memset(ones[:], 1.0).then_inc(s_one, 1)
            pool.wait_ge(s_sum, 3)
            pool.memset(hacc[:], 0.0).then_inc(s_zero, 1)
            pool.wait_ge(s_zero, 2)
            def add_square(n):
                toks = halves[n // KD]
                pool.wait_ge(s_hs, n + 1)
                if n:
                    pool.wait_ge(s_ha, n)
                pool.tensor_tensor(hacc[:, toks], hacc[:, toks], hsq[:, n % 3, :], ALU.add).then_inc(s_ha, 1)

            for n in range(2 * KD):
                if n % 2 or n >= KD:
                    h = y[:, n % KD, halves[n // KD]]
                    pool.wait_ge(s_t, n + 1)
                    pool.wait_ge(s_nx[n % 4], 16 * (n // 4 + 1))
                    pool.tensor_tensor(h, h, nx[:, n % 4, :], ALU.add).then_inc(s_h[1], 1)
                if 1 <= n <= KD:
                    add_square(n - 1)

            for n in list(range(KD)) + [KD + c for c in POOL_ADDS]:
                y2 = yacc[:, n % KD, halves[n // KD]]
                pool.wait_ge(s_ft, n + 1)
                pool.wait_ge(s_fh[n // KD], 16 * KD)
                pool.tensor_tensor(y2, y2, fh[:, n % KD, halves[n // KD]], ALU.add).then_inc(s_fp, 1)


def kernel(**inputs):
    import concourse.bacc as bacc
    from concourse.bass_utils import run_bass_kernel_spmd

    def layer(name):
        return np.asarray(inputs[name])[0]

    def slabs(w):
        return w.reshape(w.shape[0] // P, P, w.shape[1] // P, P).transpose(2, 1, 0, 3)

    w = layer("w_in")
    starts = np.cumsum([0, 512, 128, 128, 128, 128, 128, 128, 24, 512, 128])
    q_n, kc, v_c, ks, vs, kw, vw, gt, q_s, k_s, v_s = starts
    cols = lambda at, n=P: w[:, at:at + n]
    pad = np.zeros((D_MODEL, P - 24), w.dtype)
    w_in = np.concatenate([cols(k_s), cols(v_s), cols(kc), cols(v_c), cols(vs), cols(vw),
                           cols(gt, 24), pad, cols(ks), cols(kw), cols(q_n, 512), cols(q_s, 512)], axis=1)
    up, down = slabs(layer("w_up")), layer("w_down")
    mlp = []
    for q in range(QUARTERS):
        mlp.append(up[q * FQ:(q + 1) * FQ])
        mlp.append(slabs(down[q * FQ * P:(q + 1) * FQ * P]))
    gains = np.stack([layer(n).reshape(KD, P).T for n in ("norm_mix_pre", "norm_mix_post", "norm_mlp_pre", "norm_mlp_post")], axis=1)
    w1 = np.stack([layer(n).reshape(16, P, 256).transpose(1, 0, 2) for n in ("cmp_w1_k", "cmp_w1_v")])
    w2 = np.stack([np.concatenate([layer(n)] * 2, axis=1).reshape(2, P, P).transpose(1, 0, 2) for n in ("cmp_w2_k", "cmp_w2_v")])
    pe = np.stack([layer(n).reshape(16, P).T for n in ("cmp_pe_k", "cmp_pe_v")])
    arrays = {
        "xT": np.asarray(inputs["x"])[0].T.reshape(KD, P, SEQ),
        "w_in": slabs(w_in),
        "w_out": slabs(layer("w_out")),
        "w_mlp": np.concatenate(mlp),
        "gains": gains, "w1": w1, "w2": w2, "pe": pe,
        "sinks": np.broadcast_to(layer("sinks").reshape(1, 8), (P, 8)),
        "consts": constants(),
    }
    arrays = {n: np.ascontiguousarray(a) for n, a in arrays.items()}
    nc = bacc.Bacc("TRN2", target_bir_lowering=False, num_devices=1, dynamic_dma_scratch_size=1024)
    aps = [nc.dram_tensor(n, a.shape, F32, kind="ExternalInput").ap() for n, a in arrays.items()]
    h_dram = nc.dram_tensor("h_scratch", (KD, P, SEQ), F32, kind="Internal").ap()
    out = nc.dram_tensor("out", (KD, P, SEQ), F32, kind="ExternalOutput").ap()
    hybrid_layer(nc, *aps, h_dram, out)
    result = run_bass_kernel_spmd(nc, [arrays], core_ids=[0]).results[0]["out"]
    return np.ascontiguousarray(result.reshape(D_MODEL, SEQ).T)[None]
```
